# Optimizing a Trainium2 kernel written in Bass

```python
import math
import jax, jax.numpy as jnp
from jax import lax
import numpy as np

D_MODEL = 1024
BATCH = 1
SEQ = 512
DEPTH = 2

N_EVEN = (DEPTH + 1) // 2
N_ODD = DEPTH // 2
MIX_WIDTH = D_MODEL
MLSTM_WIDTH = MIX_WIDTH // 2
MLSTM_HEADS = 4
MLSTM_HEAD_DIM = MLSTM_WIDTH // MLSTM_HEADS
MLSTM_CONV = 4
MLSTM_CHUNK = 64
DIFF_WIDTH = MIX_WIDTH - MLSTM_WIDTH
DIFF_HEADS = 4
DIFF_V_DIM = DIFF_WIDTH // DIFF_HEADS
DIFF_HEAD_DIM = DIFF_V_DIM // 2
Q_BLOCK = 128
ROPE_THETA = 10000.0
CONV_WIDTH = 3
N_GROUPS = 4
EXPERTS_PER_GROUP = 8
EXPERT_FF = 256
EPS = 1e-6
AB_SPLITS = [2 * MLSTM_WIDTH, MLSTM_WIDTH, MLSTM_WIDTH, 2 * MLSTM_HEADS, DIFF_WIDTH, DIFF_WIDTH, DIFF_WIDTH]
AB_IN_COLS = sum(AB_SPLITS)

kernel_name = 'hybrid_mlstm_diffattn_shortconv_hmoe'

def rmsnorm(x, g):
    xf = x.astype(jnp.float32)
    y = xf * lax.rsqrt(jnp.mean(xf * xf, axis=-1, keepdims=True) + EPS)
    return (y * g.astype(jnp.float32)).astype(x.dtype)

def rope(x, positions):
    d = x.shape[-1]
    half = d // 2
    inv_freq = 1.0 / (ROPE_THETA ** (jnp.arange(half, dtype=jnp.float32) / half))
    ang = positions.astype(jnp.float32)[..., None] * inv_freq
    cos = jnp.cos(ang)[:, :, None, :]
    sin = jnp.sin(ang)[:, :, None, :]
    xf = x.astype(jnp.float32)
    x1, x2 = xf[..., :half], xf[..., half:]
    return jnp.concatenate([x1 * cos - x2 * sin, x2 * cos + x1 * sin], axis=-1).astype(x.dtype)

def causal_depthwise_conv(x, w):
    k, c = w.shape
    return lax.conv_general_dilated(
        x, w.reshape(k, 1, c).astype(x.dtype), window_strides=(1,), padding=[(k - 1, 0)],
        dimension_numbers=('NWC', 'WIO', 'NWC'), feature_group_count=c)

def mlstm_chunkwise(q, k, v, i_pre, f_pre):
    B, H, S, d = q.shape
    L = MLSTM_CHUNK
    nc = S // L
    to_chunks = lambda t: jnp.moveaxis(t.astype(jnp.float32).reshape(B, H, nc, L, *t.shape[3:]), 2, 0)
    qc, kc, vc = to_chunks(q), to_chunks(k), to_chunks(v)
    logf = to_chunks(jax.nn.log_sigmoid(f_pre.astype(jnp.float32)))
    ig = to_chunks(i_pre)
    tril = jnp.tril(jnp.ones((L, L), dtype=bool))

    def step(carry, xs):
        C, n, m = carry
        qb, kb, vb, lf, ib = xs
        b = jnp.cumsum(lf, axis=-1)
        dmat = jnp.where(tril, b[..., :, None] - b[..., None, :] + ib[..., None, :], -jnp.inf)
        inter = b + m[..., None]
        m_row = jnp.maximum(inter, jnp.max(dmat, axis=-1))
        w = jnp.exp(dmat - m_row[..., None])
        s = jnp.einsum('bhid,bhjd->bhij', qb, kb) * w
        inter_w = jnp.exp(inter - m_row)
        num = jnp.einsum('bhij,bhjd->bhid', s, vb) + inter_w[..., None] * jnp.einsum('bhid,bhde->bhie', qb, C)
        den = jnp.sum(s, axis=-1) + inter_w * jnp.einsum('bhid,bhd->bhi', qb, n)
        h = num / jnp.maximum(jnp.abs(den), jnp.exp(-m_row))[..., None]
        b_last = b[..., -1]
        decay = b_last[..., None] - b + ib
        m_new = jnp.maximum(b_last + m, jnp.max(decay, axis=-1))
        wr = jnp.exp(decay - m_new[..., None])
        carry_w = jnp.exp(b_last + m - m_new)
        C_new = carry_w[..., None, None] * C + jnp.einsum('bhj,bhjd,bhje->bhde', wr, kb, vb)
        n_new = carry_w[..., None] * n + jnp.einsum('bhj,bhjd->bhd', wr, kb)
        return (C_new, n_new, m_new), h

    init = (jnp.zeros((B, H, d, d), jnp.float32), jnp.zeros((B, H, d), jnp.float32), jnp.zeros((B, H), jnp.float32))
    _, hs = lax.scan(step, init, (qc, kc, vc, logf, ig))
    return jnp.moveaxis(hs, 0, 2).reshape(B, H, S, d)

def diff_attention(q, k, v, lam):
    B, H, _, S, d = q.shape
    nb = S // Q_BLOCK
    q_blocks = q.reshape(B, H, 2, nb, Q_BLOCK, d).transpose(3, 0, 1, 2, 4, 5)
    key_pos = jnp.arange(S)
    scale = d ** -0.5

    def one_block(args):
        qi, bi = args
        s = jnp.einsum('bhcqd,bhckd->bhcqk', qi, k).astype(jnp.float32) * scale
        q_pos = bi * Q_BLOCK + jnp.arange(Q_BLOCK)
        s = jnp.where(key_pos[None, :] <= q_pos[:, None], s, -jnp.inf)
        p = jax.nn.softmax(s, axis=-1)
        a = p[:, :, 0] - lam * p[:, :, 1]
        return jnp.einsum('bhqk,bhkd->bhqd', a.astype(v.dtype), v)

    out = lax.map(one_block, (q_blocks, jnp.arange(nb)))
    return out.transpose(1, 0, 3, 2, 4).reshape(B, S, H, v.shape[-1])

def mlstm_diff_mixer(h, positions, w_in, gate_bias, conv_w, mlstm_norm, lam_vecs, diff_norm, w_out, layer_idx):
    B, S, _ = h.shape
    idx = list(np.cumsum(AB_SPLITS)[:-1])
    m_qk, m_v, m_o, m_gates, d_q, d_k, d_v = jnp.split(h @ w_in, idx, axis=-1)
    m_qk = jax.nn.silu(causal_depthwise_conv(m_qk, conv_w))
    m_q, m_k = jnp.split(m_qk, 2, axis=-1)
    gates = (m_gates + gate_bias).astype(jnp.float32)
    i_pre = gates[..., :MLSTM_HEADS].transpose(0, 2, 1)
    f_pre = gates[..., MLSTM_HEADS:].transpose(0, 2, 1)
    heads = lambda t: t.reshape(B, S, MLSTM_HEADS, MLSTM_HEAD_DIM).transpose(0, 2, 1, 3)
    hm = mlstm_chunkwise(heads(m_q) * MLSTM_HEAD_DIM ** -0.5, heads(m_k), heads(m_v), i_pre, f_pre)
    hm = rmsnorm(hm.transpose(0, 2, 1, 3), mlstm_norm).astype(h.dtype)
    hm = hm * jax.nn.sigmoid(m_o.reshape(B, S, MLSTM_HEADS, MLSTM_HEAD_DIM))
    dq = rope(d_q.reshape(B, S, 2 * DIFF_HEADS, DIFF_HEAD_DIM), positions)
    dk = rope(d_k.reshape(B, S, 2 * DIFF_HEADS, DIFF_HEAD_DIM), positions)
    dq = dq.reshape(B, S, DIFF_HEADS, 2, DIFF_HEAD_DIM).transpose(0, 2, 3, 1, 4)
    dk = dk.reshape(B, S, DIFF_HEADS, 2, DIFF_HEAD_DIM).transpose(0, 2, 3, 1, 4)
    dv = d_v.reshape(B, S, DIFF_HEADS, DIFF_V_DIM).transpose(0, 2, 1, 3)
    lam_init = 0.8 - 0.6 * math.exp(-0.3 * layer_idx)
    lv = lam_vecs.astype(jnp.float32)
    lam = jnp.exp(jnp.sum(lv[0] * lv[1])) - jnp.exp(jnp.sum(lv[2] * lv[3])) + lam_init
    hd = diff_attention(dq, dk, dv, lam)
    hd = rmsnorm(hd, diff_norm) * (1.0 - lam_init)
    merged = jnp.concatenate([hm.reshape(B, S, MLSTM_WIDTH), hd.reshape(B, S, DIFF_WIDTH)], axis=-1)
    return merged @ w_out

def short_conv_mixer(h, w_in, conv_w, w_out):
    b_gate, c_gate, xt = jnp.split(h @ w_in, 3, axis=-1)
    return (b_gate * causal_depthwise_conv(c_gate * xt, conv_w)) @ w_out

def hier_moe(x, w_rg, b_rg, w_re, b_re, w_gate, w_up, w_down):
    B, S, D = x.shape
    xt = x.reshape(B * S, D)
    g_prob = jax.nn.softmax((xt @ w_rg + b_rg).astype(jnp.float32), axis=-1)
    g_val, g_idx = lax.top_k(g_prob, 1)
    e_logits = (xt @ w_re + b_re).astype(jnp.float32).reshape(-1, N_GROUPS, EXPERTS_PER_GROUP)
    e_sel = jnp.take_along_axis(e_logits, g_idx[:, :, None], axis=1)[:, 0]
    e_val, e_idx = lax.top_k(e_sel, 2)
    e_w = jax.nn.softmax(e_val, axis=-1)
    within = jnp.sum(jax.nn.one_hot(e_idx, EXPERTS_PER_GROUP, dtype=jnp.float32) * e_w[..., None], axis=1)
    gates = (g_val * jax.nn.one_hot(g_idx[:, 0], N_GROUPS, dtype=jnp.float32))[:, :, None] * within[:, None, :]
    gates = gates.astype(x.dtype)
    y = jnp.zeros_like(xt)
    for g in range(N_GROUPS):
        hg = jax.nn.silu(jnp.einsum('td,edf->tef', xt, w_gate[g])) * jnp.einsum('td,edf->tef', xt, w_up[g])
        y = y + jnp.einsum('tef,efd->td', hg * gates[:, g, :, None], w_down[g])
    return y.reshape(B, S, D)

def setup_inputs(seed: int = 0) -> dict:
    key = jax.random.key(seed)
    ks = jax.random.split(key, 24)
    nrm = lambda k, shape, s: jax.random.normal(k, shape, jnp.float32) * s
    D = D_MODEL
    i_bias = nrm(ks[5], (N_EVEN, MLSTM_HEADS), 0.1)
    f_bias = jnp.linspace(3.0, 6.0, MLSTM_HEADS, dtype=jnp.float32)[None, :] + nrm(ks[6], (N_EVEN, MLSTM_HEADS), 0.01)
    return {
        'x': nrm(ks[0], (BATCH, SEQ, D), 1.0),
        'positions': jnp.broadcast_to(jnp.arange(SEQ, dtype=jnp.int32), (BATCH, SEQ)),
        'norm_mix': 1.0 + nrm(ks[1], (DEPTH, D), 0.01),
        'norm_ffn': 1.0 + nrm(ks[2], (DEPTH, D), 0.01),
        'ab_w_in': nrm(ks[3], (N_EVEN, D, AB_IN_COLS), D ** -0.5),
        'ab_gate_bias': jnp.concatenate([i_bias, f_bias], axis=-1),
        'ab_conv_w': nrm(ks[4], (N_EVEN, MLSTM_CONV, 2 * MLSTM_WIDTH), MLSTM_CONV ** -0.5),
        'ab_mlstm_norm': 1.0 + nrm(ks[7], (N_EVEN, MLSTM_HEAD_DIM), 0.01),
        'ab_lambda': nrm(ks[8], (N_EVEN, 4, DIFF_HEAD_DIM), 0.1),
        'ab_diff_norm': 1.0 + nrm(ks[9], (N_EVEN, DIFF_V_DIM), 0.01),
        'ab_w_out': nrm(ks[10], (N_EVEN, MIX_WIDTH, D), MIX_WIDTH ** -0.5),
        'c_w_in': nrm(ks[11], (N_ODD, D, 3 * D), D ** -0.5),
        'c_conv_w': nrm(ks[12], (N_ODD, CONV_WIDTH, D), CONV_WIDTH ** -0.5),
        'c_w_out': nrm(ks[13], (N_ODD, D, D), D ** -0.5),
        'moe_w_rg': nrm(ks[14], (DEPTH, D, N_GROUPS), D ** -0.5),
        'moe_b_rg': nrm(ks[15], (DEPTH, N_GROUPS), 0.01),
        'moe_w_re': nrm(ks[16], (DEPTH, D, N_GROUPS * EXPERTS_PER_GROUP), D ** -0.5),
        'moe_b_re': nrm(ks[17], (DEPTH, N_GROUPS * EXPERTS_PER_GROUP), 0.01),
        'moe_w_gate': nrm(ks[18], (DEPTH, N_GROUPS, EXPERTS_PER_GROUP, D, EXPERT_FF), D ** -0.5),
        'moe_w_up': nrm(ks[19], (DEPTH, N_GROUPS, EXPERTS_PER_GROUP, D, EXPERT_FF), D ** -0.5),
        'moe_w_down': nrm(ks[20], (DEPTH, N_GROUPS, EXPERTS_PER_GROUP, EXPERT_FF, D), EXPERT_FF ** -0.5),
        'final_norm': 1.0 + nrm(ks[21], (D,), 0.01),
    }

def reference(x, positions, norm_mix, norm_ffn, ab_w_in, ab_gate_bias, ab_conv_w, ab_mlstm_norm,
              ab_lambda, ab_diff_norm, ab_w_out, c_w_in, c_conv_w, c_w_out, moe_w_rg, moe_b_rg,
              moe_w_re, moe_b_re, moe_w_gate, moe_w_up, moe_w_down, final_norm):
    for layer in range(DEPTH):
        h = rmsnorm(x, norm_mix[layer])
        j = layer // 2
        if layer % 2 == 0:
            mix = mlstm_diff_mixer(h, positions, ab_w_in[j], ab_gate_bias[j], ab_conv_w[j], ab_mlstm_norm[j],
                                   ab_lambda[j], ab_diff_norm[j], ab_w_out[j], layer)
        else:
            mix = short_conv_mixer(h, c_w_in[j], c_conv_w[j], c_w_out[j])
        x = x + mix
        x = x + hier_moe(rmsnorm(x, norm_ffn[layer]), moe_w_rg[layer], moe_b_rg[layer], moe_w_re[layer],
                         moe_b_re[layer], moe_w_gate[layer], moe_w_up[layer], moe_w_down[layer])
    return rmsnorm(x, final_norm)


_drawn_inputs = setup_inputs


def setup_inputs(seed=0):
    import zlib

    import numpy as np

    out = dict(_drawn_inputs(seed))
    spreads = {}
    factors = {'ab_mlstm_norm': 12.36,
     'moe_b_rg': 19.573,
     'final_norm': 30.234,
     'norm_ffn': 3.114,
     'ab_diff_norm': 4.767,
     'moe_b_re': 3.902}
    for name, (base, spread) in spreads.items():
        noise = np.random.default_rng([zlib.crc32(name.encode()), seed]).standard_normal(out[name].shape)
        drawn = base * np.exp(spread * noise) if base else spread * noise
        out[name] = __import__('jax').numpy.asarray(drawn.astype(out[name].dtype))
    for name, factor in factors.items():
        out[name] = (out[name] * factor).astype(out[name].dtype)
    return out
```

```python
from contextlib import ExitStack

import concourse.bass as bass
from concourse import mybir

ALU = mybir.AluOpType
ACT = mybir.ActivationFunctionType
AX_X = mybir.AxisListType.X
F32 = mybir.dt.float32
BF16 = mybir.dt.bfloat16
I32 = mybir.dt.int32
U32 = mybir.dt.uint32

P = 128
D = 1024
S = 512
KT = D // P
TT = S // P
H = 4
HD = 128
DD = 64
HALF = DD // 2
EPS = 1e-6
NG = 4
EG = 8
NE = NG * EG
FF = 256
FT = FF // P
CAP = P
SMALL = 64
RING = 4
SLOT = 3 * KT * FF
XB = 4
LAM_INIT = 0.2
NEG = -3.0e38
MASK = -1.0e30
EMPTY = 1 << 14
OV_ROUNDS = S // CAP - 1

C_MQK, C_MV, C_MO, C_GATE, C_DQ, C_DK, C_DV = 0, 1024, 1536, 2048, 2056, 2568, 3080

L0_COLS = [C_DQ, C_DK, C_DV, C_MV, C_MQK, C_MQK + 512, C_MO]
N_MIX0 = len(L0_COLS) + 2
N_MIX1 = 4 + 2
EXPERT_USE = [N_MIX0, N_MIX0 + NE + N_MIX1]
MIX_USE = [0, N_MIX0 + NE]
MIX_DONE = [0, N_MIX0]

PAIRS = [(j, i) for j in range(TT) for i in range(j, TT)]

TWO_PI = (6.28125, 0.00193023681640625, 5.066394805908203e-06, 3.795019905382127e-09)
PI_IN = 3.1415925
MAGIC = 12582912.0


def build(nc, x_in, positions, norm_mix, norm_ffn, w_in0, gate_bias, conv0, mlstm_norm, lam_vecs,
          diff_norm, w_out0, w_in1, conv1, w_out1, w_rg, b_rg, w_re, b_re, w_gate, w_up, w_down,
          final_norm, inv_freq, out):
    with ExitStack() as ctx:
        def sb(name, shape, dt=F32):
            return ctx.enter_context(nc.sbuf_tensor(name, shape, dt))

        def sem(name):
            return ctx.enter_context(nc.semaphore(name))

        ps = ctx.enter_context(nc.psum_tensor("ps", [P, 8, 512], F32))
        x_sb = sb("x_sb", [P, TT, D])
        hT = sb("hT", [P, KT, S])
        ring = sb("ring", [P, RING, SLOT])
        work = sb("work", [P, 16400])
        ident = sb("ident", [P, P])
        ident_bf = sb("ident_bf", [P, P], BF16)
        causal_bf = sb("causal_bf", [P, P], BF16)
        before_bf = sb("before_bf", [P, P], BF16)
        ones_bf = sb("ones_bf", [P, P], BF16)
        zeros4 = sb("zeros4", [H, P])
        iota32 = sb("iota32", [P, NE])
        iota32_i = sb("iota32_i", [P, NE], I32)
        pair_id = sb("pair_id", [P, TT, 2], I32)
        empty_i = sb("empty_i", [P, P], I32)
        g_mix = sb("g_mix", [P, 2, KT])
        g_ffn = sb("g_ffn", [P, 2, KT])
        g_mlstm = sb("g_mlstm", [P, 1])
        g_diff = sb("g_diff", [P, 1])
        g_diff_s = sb("g_diff_s", [P, 1])
        gate_w = sb("gate_w", [P, KT, 2 * H])
        gate_b = sb("gate_b", [P, 2 * H])
        conv0_w = sb("conv0_w", [P, KT, 4])
        conv1_w = sb("conv1_w", [P, KT, 3])
        lam_c = sb("lam_c", [P, 8])
        router_w = sb("router_w", [P, 2, KT, NG + NE])
        router_b = sb("router_b", [P, 2, NG + NE])
        pos_i = sb("pos_i", [P, TT], I32)
        pos_f = sb("pos_f", [P, TT])
        invf = sb("invf", [P, HALF])
        sin_t = sb("sin_t", [P, TT, HALF])
        cos_t = sb("cos_t", [P, TT, HALF])
        ss = sb("ss", [P, 5, TT])
        ms = sb("ms", [P, 5, TT])
        rstd = sb("rstd", [P, 5, TT])
        neg_half = sb("neg_half", [P, TT])
        gates = sb("gates", [P, TT, 2 * H])
        gate_tmp = sb("gate_tmp", [P, 3, TT, H])
        negc = sb("negc", [H, S])
        m_state = sb("m_state", [H, TT + 1])
        ucol = sb("ucol", [P, len(PAIRS) + TT, H])
        em = sb("em", [P, TT, H])
        att_s = sb("att_s", [P, 12])
        hn = sb("hn", [P, 8, TT])
        hn_ms = sb("hn_ms", [P, 8, TT])
        hn_r = sb("hn_r", [P, 8, TT])
        den_t = sb("den_t", [P, 4, TT])
        lg = sb("lg", [P, TT, 8 + NE])
        g8 = sb("g8", [P, TT, 8])
        gi8 = sb("gi8", [P, TT, 8], U32)
        g_hot = sb("g_hot", [P, TT, 4 + EG * NG])
        g_f = sb("g_f", [P, TT, 2])
        esel = sb("esel", [P, TT, EG])
        e8 = sb("e8", [P, TT, 8])
        ei8 = sb("ei8", [P, TT, 8], U32)
        ei_f = sb("ei_f", [P, TT, 2])
        eid = sb("eid", [P, TT, 2])
        hot_bf = sb("hot_bf", [P, TT, NE], BF16)
        rank = sb("rank", [P, TT, 2])
        dest = sb("dest", [P, TT, 2], I32)
        soft = sb("soft", [P, 6, TT])
        pair_w = sb("pair_w", [P, 2, 2, TT])
        cnt_f = sb("cnt_f", [1, NE])
        cnt_i = sb("cnt_i", [1, 2, NE], I32)
        cnt_max = sb("cnt_max", [1, 2], I32)
        slot_pair = sb("slot_pair", [P, 2, NE], I32)
        slot_tok = sb("slot_tok", [P, 2, NE], I32)
        slot_f = sb("slot_f", [P, NE])
        tok_now = sb("tok_now", [P, XB], I32)
        pair_now = sb("pair_now", [P, XB], I32)
        fence = sb("fence", [1, 2])

        def part(start, size, pattern=None, **kw):
            v = work[:, start:start + size]
            return v.rearrange(pattern, **kw) if pattern else v

        ang = part(0, 512, "p (n t e) -> p n t e", n=4, t=TT)
        lam_sb = part(512, 256, "p (n d) -> p n d", n=4)
        lam_t = part(768, 128, "p (n d) -> p n d", n=2)
        dqT = part(0, 2048, "p (h s) -> p h s", h=H)
        dkT = part(2048, 2048, "p (h s) -> p h s", h=H)
        dv = part(4096, 2048, "p (t c) -> p t c", t=TT)
        mv = part(6144, TT * H * (HD + 1), "p (t h e) -> p t h e", t=TT, h=H)
        qkT = part(8208, 4096, "p (c s) -> p c s", c=2 * H)
        rope_a = part(12304, 1024, "p (b c) -> p b c", b=2)
        rope_b = part(13328, 1024, "p (b c) -> p b c", b=2)
        roped = part(14352, 1024, "p (b c) -> p b c", b=2)
        conv_acc = part(15376, 1024, "p (b c) -> p b c", b=2)
        att_e = part(12304, 1024, "p (c k) -> p c k", c=2)
        att_a = part(13328, 512)
        att_aT = part(13840, 512)
        att_o = part(14352, 512)
        att_q = part(14864, 512)
        row_b = work[0:H, 8208:8720]
        row_u = work[0:H, 8720:9232]
        row_c = work[0:H, 9232:9744]
        row_m = work[0:H, 9744:10256]
        row_off = work[0:H, 10256:11280].rearrange("p (n j) -> p n j", n=8)
        ml_w = part(0, 2560, "p (b k) -> p b k", b=2)
        ml_s = part(2560, 2560, "p (b k) -> p b k", b=2)
        ml_h = part(5120, 1024, "p (b k) -> p b k", b=2)
        ml_q = part(14352, 512)
        o_gate = ring[:, 0, 4096:6144].rearrange("p (t c) -> p t c", t=TT)
        mergedM = hT[:, 0:H, :]
        mergedD = ring[:, 3, 4096:6144].rearrange("p (h s) -> p h s", h=H)
        xn = part(12304, 2048, "p (b c) -> p b c", b=2)
        junk = part(15376, 1024)
        hot = part(8208, TT * 2 * NE, "p (t k e) -> p t k e", t=TT, k=2)
        rank_t = part(8464, TT * 2 * NE, "p (t k e) -> p t k e", t=TT, k=2)
        xg = part(0, XB * D, "p (b c) -> p b c", b=XB)
        xgT = part(4096, 2048, "p (b k s) -> p b k s", b=2, k=KT)
        hid = part(6144, 512, "p (b c) -> p b c", b=2)
        sil = part(6656, 512, "p (b c) -> p b c", b=2)
        y_sb = part(7168, 2048, "p (b c) -> p b c", b=2)
        ov_w = part(9216, SLOT)
        ov_pair = part(15376, NE).bitcast(I32)
        ov_tok = part(15408, NE).bitcast(I32)
        ov_f = part(15440, NE)
        yp = part(0, 8192, "p (t k c) -> p t k c", t=TT, k=2)
        fin = part(8192, 4096, "p (t c) -> p t c", t=TT)
        g_final = part(12304, 1024)
        yT = part(0, 4096, "p (c s) -> p c s", c=KT)
        c_sb = part(4096, 1024, "p (b s) -> p b s", b=2)
        cx = part(5120, 1024, "p (b s) -> p b s", b=2)
        c_acc = part(6144, 1024, "p (b s) -> p b s", b=2)

        xn_dram = [nc.dram_tensor(f"xn_rows_{n}", [S, D], F32).ap() for n in range(2)]
        pair_dram = [nc.dram_tensor(f"pair_rows_{n}", [2 * S, D], F32).ap() for n in range(2)]
        list_dram = [nc.dram_tensor(f"slot_list_{n}", [S * NE, 1], I32).ap() for n in range(2)]

        x_loaded = [sem(f"x_loaded_{t}") for t in range(TT)]
        consts_loaded = sem("consts_loaded")
        slot_loaded = [sem(f"slot_loaded_{s}") for s in range(RING)]
        mixer_used = sem("mixer_used")
        masks_ready = sem("masks_ready")
        pool_chain = sem("pool_chain")
        dve_chain = sem("dve_chain")
        act_chain = sem("act_chain")
        consts_ready = sem("consts_ready")
        lists_empty = sem("lists_empty")
        angles_ready = sem("angles_ready")
        rope_table = sem("rope_table")
        lam_sum = sem("lam_sum")
        lam_exp = sem("lam_exp")
        x_ready = sem("x_ready")
        sumsq = sem("sumsq")
        rstd_ready = sem("rstd_ready")
        xn_ready = sem("xn_ready")
        xT_done = sem("xT_done")
        hT_ready = sem("hT_ready")
        xn_stored = [sem(f"xn_stored_{b}") for b in range(2)]
        proj_done = sem("proj_done")
        gates_abs = sem("gates_abs")
        gates_ln = sem("gates_ln")
        gates_ready = sem("gates_ready")
        gateT_done = sem("gateT_done")
        rows_ready = sem("rows_ready")
        rowsT_done = sem("rowsT_done")
        ucol_ready = sem("ucol_ready")
        em_ready = sem("em_ready")
        rope_parts = sem("rope_parts")
        roped_ready = sem("roped_ready")
        ropeT_done = sem("ropeT_done")
        dqkT_ready = sem("dqkT_ready")
        kv_copied = sem("kv_copied")
        conv_ready = sem("conv_ready")
        qk_ready = sem("qk_ready")
        ogate_ready = sem("ogate_ready")
        att_scores = sem("att_scores")
        att_max = sem("att_max")
        att_exp = sem("att_exp")
        att_probs = sem("att_probs")
        att_T = sem("att_T")
        att_aT_ready = sem("att_aT_ready")
        att_pv = sem("att_pv")
        att_o_copied = sem("att_o_copied")
        head_ss = sem("head_ss")
        head_rstd = sem("head_rstd")
        att_normed = sem("att_normed")
        att_fT = sem("att_fT")
        diff_merged = sem("diff_merged")
        ml_scores = sem("ml_scores")
        ml_exp = sem("ml_exp")
        ml_masked = sem("ml_masked")
        ml_sT = sem("ml_sT")
        ml_num = sem("ml_num")
        ml_normed = sem("ml_normed")
        ml_fT = sem("ml_fT")
        mlstm_merged = sem("mlstm_merged")
        wo_done = sem("wo_done")
        logits_done = sem("logits_done")
        hot_ready = sem("hot_ready")
        top_ready = sem("top_ready")
        soft_exp = sem("soft_exp")
        rank_done = sem("rank_done")
        count_done = sem("count_done")
        counts_ready = sem("counts_ready")
        dest_ready = sem("dest_ready")
        list_stored = sem("list_stored")
        list_loaded = sem("list_loaded")
        slots_ready = sem("slots_ready")
        xg_cleared = sem("xg_cleared")
        psum_cleared = sem("psum_cleared")
        xg_loaded = [sem(f"xg_loaded_{b}") for b in range(XB)]
        gT_done = sem("gT_done")
        xgT_ready = sem("xgT_ready")
        gu_done = sem("gu_done")
        silu_done = sem("silu_done")
        hid_ready = sem("hid_ready")
        down_done = sem("down_done")
        y_ready = sem("y_ready")
        y_stored = [sem(f"y_stored_{b}") for b in range(2)]
        tok_copied = sem("tok_copied")
        indirect_turn = sem("indirect_turn")
        pair_copied = sem("pair_copied")
        pairs_stored = sem("pairs_stored")
        yp_loaded = [sem(f"yp_loaded_{t}") for t in range(TT)]
        ov = [{n: sem(f"ov{layer}_{n}") for n in (
            "list", "idx", "w", "rows", "T", "xT", "gu", "silu", "hid", "down", "y", "stored",
            "copied")}
            for layer in range(2)]
        c_done = sem("c_done")
        c_copied = sem("c_copied")
        c_evac = sem("c_evac")
        g_final_loaded = sem("g_final_loaded")
        out_ready = sem("out_ready")
        out_stored = sem("out_stored")

        dmas_of_use = [1] * N_MIX0 + [3] * NE + [3] * 4 + [1] * 2 + [3] * NE

        def loaded_value(use):
            return 16 * sum(dmas_of_use[u] for u in range(use % RING, use + 1, RING))

        def expert_loaded_value(layer, i, b):
            return loaded_value(EXPERT_USE[layer] + b) + 48 * i

        def wait_slot_free(eng, use):
            u = use - RING
            if u < 0:
                return
            if u < N_MIX0:
                eng.wait_ge(mixer_used, u + 1)
            elif u < MIX_USE[1]:
                eng.wait_ge(down_done, u - N_MIX0 + 1)
            elif u < EXPERT_USE[1]:
                eng.wait_ge(mixer_used, MIX_DONE[1] + u - MIX_USE[1] + 1)
            else:
                eng.wait_ge(down_done, NE + u - EXPERT_USE[1] + 1)

        def expert_loop(eng, body):
            body(0, True, False)
            with eng.Fori(1, NE // RING - 1) as i:
                body(i, False, False)
            body(NE // RING - 1, False, True)

        consumed = {}
        for j in range(29):
            consumed[j] = ((gates_abs, 1) if j < 1 else (rope_parts, j) if j < 9 else
                           (kv_copied, j - 8) if j < 17 else (conv_ready, j - 16) if j < 25 else
                           (ogate_ready, j - 24))
        ATT0 = 13
        N_CONST = 2 + 6 * 2 + 7

        block = ctx.enter_context(nc.Block())

        @block.sync
        def _(sp):
            for t in range(TT):
                sp.dma_start(x_sb[:, t, :], x_in[t * P:(t + 1) * P, :]).then_inc(x_loaded[t], 16)

            def load(use, dst, src):
                sp.dma_start(dst, src).then_inc(slot_loaded[use % RING], 16)

            def load_expert(layer, i, b):
                e = i * RING + b
                use = EXPERT_USE[layer] + b
                s = use % RING
                sl = bass.ds(e, 1)
                load(use, ring[:, s, 0:2048], w_gate[layer][sl].rearrange("o (p k) f -> p (o k f)", k=KT))
                load(use, ring[:, s, 2048:4096], w_up[layer][sl].rearrange("o (p k) f -> p (o k f)", k=KT))
                load(use, ring[:, s, 4096:6144].rearrange("p (k n) -> p k n", k=FT),
                     w_down[layer][sl].rearrange("o (k p) n -> p (o k) n", p=P))

            def load_w_out(use, w, c0):
                wait_slot_free(sp, use)
                load(use, ring[:, use % RING, 0:4096].rearrange("p (c n) -> p c n", c=4),
                     w[c0 * P:(c0 + 4) * P, :].rearrange("(c p) n -> p c n", p=P))

            def load_experts(layer):
                base = NE * layer

                def body(i, first, last):
                    for b in range(RING):
                        if first:
                            wait_slot_free(sp, EXPERT_USE[layer] + b)
                        else:
                            sp.wait_ge(down_done, base + i * RING + b - RING + 1)
                        load_expert(layer, i, b)
                expert_loop(sp, body)

            for use, c0 in enumerate(L0_COLS):
                wait_slot_free(sp, use)
                load(use, ring[:, use % RING, 0:4096].rearrange("p (k c) -> p k c", k=KT),
                     w_in0[:, c0:c0 + 512].rearrange("(p k) c -> p k c", k=KT))
            load_w_out(7, w_out0, 0)
            load_w_out(8, w_out0, 4)
            load_experts(0)
            for q in range(4):
                use = MIX_USE[1] + q
                wait_slot_free(sp, use)
                slot = ring[:, use % RING, :].rearrange("p (k c) -> p k c", k=KT)
                for j in range(3):
                    load(use, slot[:, :, j * 256:(j + 1) * 256],
                         w_in1[:, j * D + q * 256:j * D + (q + 1) * 256].rearrange("(p k) c -> p k c", k=KT))
            load_w_out(MIX_USE[1] + 4, w_out1, 0)
            load_w_out(MIX_USE[1] + 5, w_out1, 4)
            load_experts(1)
            for t in range(TT):
                sp.wait_ge(out_ready, t + 1)
                sp.dma_start(out[t * P:(t + 1) * P, :], fin[:, t, :]).then_inc(out_stored, 16)
            sp.wait_ge(out_stored, 16 * TT)

        @block.tensor
        def _(pe):
            def transpose_norm(n, t):
                k0 = 4 * n + t
                pe.wait_ge(xn_ready, k0 + 1)
                if k0:
                    pe.wait_ge(hT_ready, k0)
                src = xn[:, t % 2, :].rearrange("s (p k) -> s k p", k=KT)
                for k in range(KT):
                    mm = pe.transpose(ps[:, k // 4, (k % 4) * P:(k % 4 + 1) * P], src[:, k, :], ident[:, :])
                mm.then_inc(xT_done, 1)

            def w_out_tile(layer, t, chunks):
                use = MIX_USE[layer] + (7 if layer == 0 else 4)
                if t == 0:
                    pe.wait_ge(slot_loaded[use % RING], loaded_value(use))
                    pe.wait_ge(slot_loaded[(use + 1) % RING], loaded_value(use + 1))
                if t >= 2:
                    pe.wait_ge(x_ready, 8 * layer + t - 1)
                for n in range(2):
                    bank = 4 + 2 * (t % 2) + n
                    for m, c in enumerate(chunks):
                        w = ring[:, (use + c // 4) % RING, 0:4096].rearrange("p (c n) -> p c n", c=4)
                        lhs = ((mergedM if c < 4 else mergedD)[:, c % 4, t * P:(t + 1) * P] if layer == 0
                               else yT[:, c, t * P:(t + 1) * P])
                        mm = pe.matmul(ps[:, bank, :], lhs, w[:, c % 4, n * 512:(n + 1) * 512],
                                       start=(m == 0), stop=(m == KT - 1))
                mm.then_inc(wo_done, 1)
                if t == TT - 1:
                    pe.wait_ge(wo_done, 4 * layer + TT)
                    pe.sem_inc(mixer_used, 2)

            def router_tile(layer, t):
                pe.wait_ge(hT_ready, 4 * (2 * layer + 1) + t + 1)
                for k in range(KT):
                    mm = pe.matmul(ps[:, 2, t * 36:t * 36 + 36], hT[:, k, t * P:(t + 1) * P],
                                   router_w[:, layer, k, :], start=(k == 0), stop=(k == KT - 1))
                mm.then_inc(logits_done, 1)

            def rank_tile(layer, t):
                pe.wait_ge(hot_ready, 4 * layer + t + 1)
                if t:
                    pe.wait_ge(dest_ready, 4 * layer + t)
                for j in range(t + 1):
                    mm = pe.matmul(ps[:, 3, t * NE:(t + 1) * NE], (before_bf if j == t else ones_bf)[:, :],
                                   hot_bf[:, j, :], start=(j == 0), stop=(j == t))
                mm.then_inc(rank_done, 1)

            def count_experts():
                for j in range(TT):
                    mm = pe.matmul(ps[0:1, 2, 256:256 + NE], ones_bf[:, 0:1], hot_bf[:, j, :],
                                   start=(j == 0), stop=(j == TT - 1))
                mm.then_inc(count_done, 1)

            def w_out_norm_route(layer, chunks):
                n = 2 * layer + 1
                for t in range(TT):
                    w_out_tile(layer, t, chunks)
                    if t >= 2:
                        rank_tile(layer, t - 2)
                    if t >= 1:
                        transpose_norm(n, t - 1)
                        router_tile(layer, t - 1)
                rank_tile(layer, TT - 2)
                transpose_norm(n, TT - 1)
                router_tile(layer, TT - 1)
                rank_tile(layer, TT - 1)
                count_experts()

            def transpose_rows(src, out_sem):
                v = src.rearrange("s (p k) -> s k p", k=KT)
                for k in range(KT):
                    mm = pe.transpose(ps[:, k // 4, (k % 4) * P:(k % 4 + 1) * P], v[:, k, :], ident[:, :])
                mm.then_inc(out_sem, 1)

            def gate_up(w, xt, bank, slots, out_sem):
                for j in range(2 * FT):
                    m = w[:, (j // FT) * 2048:(j // FT + 1) * 2048].rearrange("p (k f) -> p k f", k=KT)
                    f0 = (j % FT) * P
                    for k in range(KT):
                        mm = pe.matmul(ps[:, bank, j * P:j * P + slots], m[:, k, f0:f0 + P],
                                       xt[:, k, 0:slots], start=(k == 0), stop=(k == KT - 1))
                mm.then_inc(out_sem, 1)

            def down(w, hd, bank, out_sem):
                m = w[:, 4096:6144].rearrange("p (k n) -> p k n", k=FT)
                for n in range(2):
                    for f in range(FT):
                        mm = pe.matmul(ps[:, bank + n, :], hd[:, f * P:(f + 1) * P],
                                       m[:, f, n * 512:(n + 1) * 512], start=(f == 0), stop=(f == FT - 1))
                mm.then_inc(out_sem, 1)

            def experts(layer):
                base = NE * layer
                rows_before = 16 * (NE // XB) * layer

                def turn(i, b):
                    g = base + i * RING + b
                    pe.wait_ge(xg_loaded[b], rows_before + 16 * i + 16)
                    if not (isinstance(g, int) and g == 0):
                        pe.wait_ge(xgT_ready, g)
                    transpose_rows(xg[:, b, :], gT_done)

                def gate_up_step(i, b, first):
                    g = base + i * RING + b
                    use = EXPERT_USE[layer] + b
                    count = pe.value_load(cnt_i[0:1, layer, bass.ds(i * RING + b, 1)], min_val=0, max_val=S)
                    pe.wait_ge(slot_loaded[use % RING], expert_loaded_value(layer, i, b))
                    pe.wait_ge(xgT_ready, g + 1)
                    if not (first and b < 2 and layer == 0):
                        pe.wait_ge(hid_ready, g - 1)
                    w = ring[:, use % RING, :]
                    with pe.If(count > SMALL):
                        gate_up(w, xgT[:, b % 2], 2 + b % 2, CAP, gu_done)
                    with pe.Else():
                        gate_up(w, xgT[:, b % 2], 2 + b % 2, SMALL, gu_done)

                def down_step(i, b, first):
                    g = base + i * RING + b
                    use = EXPERT_USE[layer] + b
                    pe.wait_ge(hid_ready, g + 1)
                    if not (first and b < 2 and layer == 0):
                        pe.wait_ge(y_ready, g - 1)
                    down(ring[:, use % RING, :], hid[:, b % 2, :], 4 + 2 * (b % 2), down_done)

                pe.wait_ge(counts_ready, layer + 1)
                pe.wait_ge(psum_cleared, layer + 1)
                turn(0, 0)

                def body(i, first, last):
                    for b in range(RING):
                        gate_up_step(i, b, first)
                        if b < RING - 1:
                            turn(i, b + 1)
                        elif not last:
                            turn(i + 1, 0)
                        if b > 0:
                            down_step(i, b - 1, first)
                        elif not first:
                            down_step(i - 1, RING - 1, False)
                expert_loop(pe, body)
                down_step(NE // RING - 1, RING - 1, False)

            def overflow(layer):
                o = ov[layer]
                most = pe.value_load(cnt_max[0:1, layer:layer + 1], min_val=0, max_val=S)
                for r in range(OV_ROUNDS):
                    with pe.If(most > CAP * (r + 1)):
                        with pe.Fori(0, NE) as e:
                            q = e + r * NE + 1
                            pe.wait_ge(o["rows"], 16 * q)
                            transpose_rows(xg[:, 0, :], o["T"])
                            pe.wait_ge(o["xT"], q)
                            pe.wait_ge(o["w"], 48 * q)
                            gate_up(ov_w, xgT[:, 0], 2, CAP, o["gu"])
                            pe.wait_ge(o["hid"], q)
                            down(ov_w, hid[:, 0, :], 4, o["down"])

            pe.wait_ge(masks_ready, 3)
            for t in range(TT):
                transpose_norm(0, t)

            pe.wait_ge(consts_loaded, 16 * N_CONST)
            pe.wait_ge(hT_ready, TT)

            def w_slot(use):
                pe.wait_ge(slot_loaded[use % RING], loaded_value(use))
                return ring[:, use % RING, 0:4096].rearrange("p (k c) -> p k c", k=KT)

            def project(j):
                if j >= 2:
                    pe.wait_ge(*consumed[j - 2])
                bank = ps[:, j % 2, :]
                if j == 0:
                    for t in range(TT):
                        for k in range(KT):
                            mm = pe.matmul(bank[:, t * 8:t * 8 + 8], hT[:, k, t * P:(t + 1) * P], gate_w[:, k, :],
                                           start=(k == 0), stop=(k == KT - 1))
                    mm.then_inc(proj_done, 1)
                    return
                use, t = (j - 1) // 4, (j - 1) % 4
                w = w_slot(use)
                for k in range(KT):
                    if use in (4, 5):
                        lhs, rhs = w[:, k, t * P:(t + 1) * P], hT[:, k, :]
                    else:
                        lhs, rhs = hT[:, k, t * P:(t + 1) * P], w[:, k, :]
                    mm = pe.matmul(bank, lhs, rhs, start=(k == 0), stop=(k == KT - 1))
                mm.then_inc(proj_done, 1)
                if t == 3:
                    pe.wait_ge(proj_done, j + 1)
                    pe.sem_inc(mixer_used, 1)

            def rope_T(r):
                pe.wait_ge(roped_ready, r + 1)
                if r >= 2:
                    pe.wait_ge(dqkT_ready, r - 1)
                for h in range(H):
                    mm = pe.transpose(ps[:, 2 + r % 2, h * P:(h + 1) * P], roped[:, r % 2, h * P:(h + 1) * P],
                                      ident[:, :])
                mm.then_inc(ropeT_done, 1)

            def gate_rows_T():
                pe.wait_ge(gates_ready, 1)
                for t in range(TT):
                    for j in range(2):
                        mm = pe.transpose(ps[0:H, 6 + j, t * P:(t + 1) * P], gates[:, t, j * H:(j + 1) * H],
                                          ident[:, :])
                mm.then_inc(gateT_done, 1)

            def gate_cols_T():
                pe.wait_ge(rows_ready, 1)
                for n, (j, i) in enumerate(PAIRS):
                    src = row_u[:, j * P:(j + 1) * P] if i == j else row_off[:, OFF[(j, i)], :]
                    mm = pe.transpose(ps[:, 5, n * H:(n + 1) * H], src, ident[0:H, 0:H])
                for i in range(TT):
                    n = len(PAIRS) + i
                    mm = pe.transpose(ps[:, 5, n * H:(n + 1) * H], row_m[:, i * P:(i + 1) * P], ident[0:H, 0:H])
                mm.then_inc(rowsT_done, 1)

            def att_score(a):
                h, i = a // TT, a % TT
                n = (i + 1) * P
                if a == 0:
                    pe.wait_ge(dqkT_ready, 8)
                    pe.wait_ge(ucol_ready, 1)
                else:
                    pe.wait_ge(att_exp, a)
                for c in range(2):
                    q = slice(c * DD, (c + 1) * DD)
                    if i:
                        pe.matmul(ps[:, 4 + c, 0:i * P], dqT[q, h, i * P:n], dkT[q, h, 0:i * P],
                                  start=True, stop=True)
                    pe.matmul(ps[:, 4 + c, i * P:n], dqT[q, h, i * P:n], dkT[q, h, i * P:n],
                              start=True, stop=False)
                    mm = pe.matmul(ps[:, 4 + c, i * P:n], ident_bf[:, :], causal_bf[:, :], start=False, stop=True)
                mm.then_inc(att_scores, 1)

            def att_turn(a):
                i = a % TT
                pe.wait_ge(att_probs, a + 1)
                if a >= 1:
                    pe.wait_ge(att_aT_ready, a)
                for j in range(i + 1):
                    mm = pe.transpose(ps[:, 6, j * P:(j + 1) * P], att_a[:, j * P:(j + 1) * P], ident[:, :])
                mm.then_inc(att_T, 1)

            def att_values(a):
                h, i = a // TT, a % TT
                pe.wait_ge(att_aT_ready, a + 1)
                if i == 0:
                    if h:
                        pe.wait_ge(att_o_copied, h)
                    else:
                        pe.wait_ge(kv_copied, 4)
                for j in range(i + 1):
                    mm = pe.matmul(ps[:, 7, i * P:(i + 1) * P], att_aT[:, j * P:(j + 1) * P],
                                   dv[:, j, h * HD:(h + 1) * HD], start=(j == 0), stop=(j == i))
                mm.then_inc(att_pv, 1)

            def att_finish_T(h):
                pe.wait_ge(att_normed, h + 1)
                if h:
                    pe.wait_ge(diff_merged, h)
                for i in range(TT):
                    mm = pe.transpose(ps[:, 2, i * P:(i + 1) * P], att_o[:, i * P:(i + 1) * P], ident[:, :])
                mm.then_inc(att_fT, 1)

            for j in range(ATT0 + 19):
                if j < 29:
                    project(j)
                if j == 1:
                    gate_rows_T()
                if j == 6:
                    gate_cols_T()
                if 4 <= j < 12:
                    rope_T(j - 4)
                a = j - ATT0
                if 0 <= a - 2 < 16:
                    att_values(a - 2)
                if 0 <= a - 1 < 16:
                    att_turn(a - 1)
                if 0 <= a < 16:
                    att_score(a)
                if a >= 6 and (a - 6) % 4 == 0:
                    att_finish_T((a - 6) // 4)

            def ml_score(h):
                if h == 0:
                    pe.wait_ge(ogate_ready, TT)
                    pe.wait_ge(diff_merged, H)
                    pe.wait_ge(qk_ready, 2 * H)
                else:
                    pe.wait_ge(ml_sT, h)
                    if h >= 2:
                        pe.wait_ge(ml_exp, h - 1)
                pe.matmul(ps[:, h % 2, :], ident[0:H, h:h + 1].to_broadcast([H, P]), negc[:, :], start=True, stop=True)
                for j in range(TT):
                    bank, c0 = ML_BANK[j]
                    mm = pe.matmul(ps[:, bank, c0:c0 + S - j * P], qkT[:, H + h, j * P:(j + 1) * P],
                                   qkT[:, h, j * P:S], start=True, stop=True)
                mm.then_inc(ml_scores, 1)

            def ml_values(h):
                pe.wait_ge(ml_sT, h + 1)
                if h == 0:
                    pe.wait_ge(kv_copied, 8)
                else:
                    pe.wait_ge(ml_normed, h)
                for i in range(TT):
                    c0 = (i % 2) * (HD + 1)
                    for j in range(i + 1):
                        s0 = ML_COL[j] + (i - j) * P
                        mm = pe.matmul(ps[:, 5 + i // 2, c0:c0 + HD + 1], ml_s[:, h % 2, s0:s0 + P],
                                       mv[:, j, h, :], start=(j == 0), stop=(j == i))
                mm.then_inc(ml_num, 1)

            def ml_finish_T(h):
                pe.wait_ge(ml_normed, h + 1)
                if h:
                    pe.wait_ge(mlstm_merged, h)
                for i in range(TT):
                    mm = pe.transpose(ps[:, 7, i * P:(i + 1) * P], ml_h[:, h % 2, i * P:(i + 1) * P], ident[:, :])
                mm.then_inc(ml_fT, 1)

            ml_score(0)
            for h in range(H):
                if h + 1 < H:
                    ml_score(h + 1)
                ml_values(h)
                if h:
                    ml_finish_T(h - 1)
            ml_finish_T(H - 1)

            pe.wait_ge(mlstm_merged, H)
            w_out_norm_route(0, [4, 5, 6, 7, 0, 1, 2, 3])
            experts(0)
            overflow(0)

            for t in range(TT):
                transpose_norm(2, t)
            pe.wait_ge(hT_ready, 3 * TT)
            for ct in range(KT):
                use = MIX_USE[1] + ct // 2
                pe.wait_ge(slot_loaded[use % RING], loaded_value(use))
                if ct >= 2:
                    pe.wait_ge(c_evac, ct - 1)
                w = ring[:, use % RING, :].rearrange("p (k c) -> p k c", k=KT)
                for n, j in enumerate((1, 2, 0)):
                    c0 = j * 256 + (ct % 2) * P
                    bank = 2 + 3 * (ct % 2) + n
                    for k in range(KT):
                        mm = pe.matmul(ps[:, bank, :], w[:, k, c0:c0 + P], hT[:, k, :],
                                       start=(k == 0), stop=(k == KT - 1))
                    mm.then_inc(c_done, 1)
                if ct % 2:
                    pe.wait_ge(c_done, 3 * (ct + 1))
                    pe.sem_inc(mixer_used, 1)
            pe.wait_ge(c_evac, KT)
            w_out_norm_route(1, list(range(KT)))
            experts(1)
            overflow(1)

        @block.scalar
        def _(act):
            n_chain = [0]

            def link(ins):
                n_chain[0] += 1
                ins.then_inc(act_chain, 1)
                act.wait_ge(act_chain, n_chain[0])

            def const(dst, src):
                act.dma_start(dst, src).then_inc(consts_loaded, 16)

            const(gate_w[:, :, :], w_in0[:, C_GATE:C_GATE + 2 * H].rearrange("(p k) c -> p k c", k=KT))
            const(gate_b[:, :], gate_bias.partition_broadcast(P))
            for n in range(2):
                const(g_mix[:, n, :], norm_mix[n].rearrange("(p k) -> p k", k=KT))
                const(g_ffn[:, n, :], norm_ffn[n].rearrange("(p k) -> p k", k=KT))
                const(router_w[:, n, :, 0:NG], w_rg[n].rearrange("(p k) c -> p k c", k=KT))
                const(router_w[:, n, :, NG:], w_re[n].rearrange("(p k) c -> p k c", k=KT))
                const(router_b[:, n, 0:NG], b_rg[n].partition_broadcast(P))
                const(router_b[:, n, NG:], b_re[n].partition_broadcast(P))
            const(g_mlstm[:, :], mlstm_norm.rearrange("(p o) -> p o", o=1))
            const(g_diff[:, :], diff_norm.rearrange("(p o) -> p o", o=1))
            const(conv0_w[:, :, :], conv0)
            const(conv1_w[:, :, :], conv1)
            const(lam_sb[:, :, :], lam_vecs.partition_broadcast(P))
            act.dma_start(pos_i[:, :], positions.rearrange("(t p) -> p t", p=P),
                          allow_slow_non_contiguous=True).then_inc(consts_loaded, 16)
            const(invf[:, :], inv_freq.partition_broadcast(P))

            def square(n, t):
                k0 = 4 * n + t
                if n == 0:
                    act.wait_ge(x_loaded[t], 16)
                else:
                    act.wait_ge(x_ready, 4 * (n - 1) + t + 1)
                if k0:
                    act.wait_ge(sumsq, k0)
                act.activation(junk, x_sb[:, t, :], ACT.Square, accum_out=ss[:, n, t:t + 1]).then_inc(sumsq, 1)

            def store_rows(layer, t):
                act.wait_ge(xn_ready, 4 * (2 * layer + 1) + t + 1)
                act.dma_start(xn_dram[layer][t * P:(t + 1) * P, :], xn[:, t % 2, :]).then_inc(xn_stored[t % 2], 16)

            def norm_route(layer):
                for t in range(TT):
                    square(2 * layer + 1, t)
                    store_rows(layer, t)
                act.wait_ge(top_ready, layer + 1)
                for t in range(TT):
                    act.activation(g_hot[:, t, 0:NG], lg[:, t, 0:NG], ACT.Exp, bias=soft[:, 0, t:t + 1],
                                   accum_out=soft[:, 1, t:t + 1])
                act.activation(soft[:, 3, :], soft[:, 2, :], ACT.Exp).then_inc(soft_exp, 1)

            def silu_step(bank, sil_v, gate_sem, gate_value, out_sem):
                act.wait_ge(gate_sem, gate_value)
                act.activation(sil_v, ps[:, bank, 0:2 * P], ACT.Silu).then_inc(out_sem, 1)

            def y_copy(bank, y_v, out_sem):
                act.activation(y_v.rearrange("p (n c) -> p n c", n=2), ps[:, bank:bank + 2, :],
                               ACT.Copy).then_inc(out_sem, 1)

            def experts(layer):
                base = NE * layer
                stored_before = 16 * (NE // 2) * layer

                def silu_of(i, b, first):
                    g = base + i * RING + b
                    if not (first and b < 2 and layer == 0):
                        act.wait_ge(hid_ready, g - 1)
                    silu_step(2 + b % 2, sil[:, b % 2, :], gu_done, g + 1, silu_done)

                def y_of(i, b, first):
                    g = base + i * RING + b
                    act.wait_ge(down_done, g + 1)
                    if not (first and b < 2 and layer == 0):
                        act.wait_ge(y_stored[b % 2], stored_before + 32 * i + 16 * ((b - 2) // 2 + 1))
                    y_copy(4 + 2 * (b % 2), y_sb[:, b % 2, :], y_ready)

                def body(i, first, last):
                    for b in range(RING):
                        silu_of(i, b, first)
                        if b > 0:
                            y_of(i, b - 1, first)
                        elif not first:
                            y_of(i - 1, RING - 1, False)
                expert_loop(act, body)
                y_of(NE // RING - 1, RING - 1, False)

            def overflow(layer):
                o = ov[layer]
                act.wait_ge(counts_ready, layer + 1)
                most = act.value_load(cnt_max[0:1, layer:layer + 1], min_val=0, max_val=S)
                for r in range(OV_ROUNDS):
                    with act.If(most > CAP * (r + 1)):
                        with act.Fori(0, NE) as e:
                            q = e + r * NE + 1
                            sl = bass.ds(e, 1)
                            act.dma_start(ov_w[:, 0:2048], w_gate[layer][sl].rearrange(
                                "o (p k) f -> p (o k f)", k=KT)).then_inc(o["w"], 16)
                            act.dma_start(ov_w[:, 2048:4096], w_up[layer][sl].rearrange(
                                "o (p k) f -> p (o k f)", k=KT)).then_inc(o["w"], 16)
                            act.dma_start(ov_w[:, 4096:6144].rearrange("p (k n) -> p k n", k=FT), w_down[layer][
                                sl].rearrange("o (k p) n -> p (o k) n", p=P)).then_inc(o["w"], 16)
                            silu_step(2, sil[:, 0, :], o["gu"], q, o["silu"])
                            act.wait_ge(o["down"], q)
                            y_copy(4, y_sb[:, 0, :], o["y"])

            def load_pairs(layer):
                act.wait_ge(pairs_stored, layer + 1)
                src = pair_dram[layer].rearrange("(k t p) d -> t p k d", k=2, p=P)
                for t in range(TT):
                    act.dma_start(yp[:, t, :, :], src[t]).then_inc(yp_loaded[t], 16)

            for t in range(TT):
                square(0, t)
            act.wait_ge(lam_sum, 1)
            act.activation(lam_c[:, 2:4], lam_c[:, 0:2], ACT.Exp).then_inc(lam_exp, 1)
            act.wait_ge(angles_ready, 1)
            act.activation(sin_t[:, :, :], ang[:, 2, :, :], ACT.Sin)
            act.activation(cos_t[:, :, :], ang[:, 3, :, :], ACT.Sin).then_inc(rope_table, 1)
            act.wait_ge(gates_abs, 1)
            link(act.activation(gate_tmp[:, 1], gate_tmp[:, 0], ACT.Exp, scale=-1.0))
            act.activation(gate_tmp[:, 2], gate_tmp[:, 1], ACT.Ln, bias=1.0).then_inc(gates_ln, 1)

            def rope_copy(r):
                act.wait_ge(ropeT_done, r + 1)
                dst = (dqT if r < 4 else dkT)[:, :, (r % 4) * P:(r % 4 + 1) * P]
                act.activation(dst, ps[:, 2 + r % 2, :].rearrange("p (h s) -> p h s", h=H),
                               ACT.Copy).then_inc(dqkT_ready, 1)

            def job(j):
                if 9 <= j < 17:
                    act.wait_ge(proj_done, j + 1)
                    t = (j - 1) % 4
                    if j < 13:
                        act.activation(dv[:, t, :], ps[:, j % 2, :], ACT.Copy).then_inc(kv_copied, 1)
                    else:
                        act.activation(mv[:, t, :, 0:HD], ps[:, j % 2, :].rearrange("p (h e) -> p h e", h=H),
                                       ACT.Copy).then_inc(kv_copied, 1)
                elif 17 <= j < 25:
                    act.wait_ge(conv_ready, j - 16)
                    act.activation(qkT[:, j - 17, :], conv_acc[:, j % 2, :], ACT.Silu).then_inc(qk_ready, 1)
                elif 25 <= j < 29:
                    act.wait_ge(proj_done, j + 1)
                    act.activation(o_gate[:, j - 25, :], ps[:, j % 2, :], ACT.Sigmoid).then_inc(ogate_ready, 1)

            def att_copy_T(a):
                n = (a % TT + 1) * P
                act.wait_ge(att_T, a + 1)
                if a >= 1:
                    act.wait_ge(att_pv, a)
                act.activation(att_aT[:, 0:n], ps[:, 6, 0:n], ACT.Copy).then_inc(att_aT_ready, 1)

            def att_exps(a):
                n = (a % TT + 1) * P
                act.wait_ge(att_max, a + 1)
                if a >= 1:
                    act.wait_ge(att_probs, a)
                for c in range(2):
                    ins = act.activation(att_e[:, c, 0:n], ps[:, 4 + c, 0:n], ACT.Exp, bias=att_s[:, 2 + c:3 + c],
                                         scale=DD ** -0.5, accum_out=att_s[:, 4 + c:5 + c])
                ins.then_inc(att_exp, 1)

            for j in range(ATT0 + 19):
                job(j)
                if 4 <= j < 12:
                    rope_copy(j - 4)
                if j == 8:
                    act.wait_ge(ucol_ready, 1)
                    act.activation(em[:, :, :], ucol[:, len(PAIRS):, :], ACT.Exp).then_inc(em_ready, 1)
                a = j - ATT0
                if a - 2 >= 0 and (a - 2) % 4 == 3 and a - 2 < 16:
                    h = (a - 2) // 4
                    act.wait_ge(att_pv, 4 * h + 4)
                    if h:
                        act.wait_ge(att_fT, h)
                    act.activation(att_o[:, :], ps[:, 7, :], ACT.Copy).then_inc(att_o_copied, 1)
                if 0 <= a - 1 < 16:
                    att_copy_T(a - 1)
                if 0 <= a < 16:
                    att_exps(a)
                if a >= 6 and (a - 6) % 4 == 0:
                    h = (a - 6) // 4
                    act.wait_ge(att_fT, h + 1)
                    act.activation(mergedD[:, h, :], ps[:, 2, :], ACT.Copy, scale=g_diff_s[:, 0:1]).then_inc(
                        diff_merged, 1)

            def ml_weights(h):
                act.wait_ge(ml_scores, h + 1)
                if h == 0:
                    act.wait_ge(att_pv, 16)
                    act.wait_ge(ucol_ready, 1)
                if h >= 2:
                    act.wait_ge(ml_sT, h - 1)
                for n, (j, i) in enumerate(PAIRS):
                    c0 = ML_COL[j] + (i - j) * P
                    ins = act.activation(ml_w[:, h % 2, c0:c0 + P], ps[:, h % 2, i * P:(i + 1) * P], ACT.Exp,
                                         bias=ucol[:, n, h:h + 1])
                ins.then_inc(ml_exp, 1)

            def ml_merge(h):
                act.wait_ge(ml_fT, h + 1)
                if h == 0:
                    act.wait_ge(mixer_used, len(L0_COLS))
                act.activation(mergedM[:, h, :], ps[:, 7, :], ACT.Copy, scale=g_mlstm[:, 0:1]).then_inc(
                    mlstm_merged, 1)

            ml_weights(0)
            for h in range(H):
                if h + 1 < H:
                    ml_weights(h + 1)
                if h:
                    ml_merge(h - 1)
            ml_merge(H - 1)
            norm_route(0)
            experts(0)
            overflow(0)
            load_pairs(0)

            for t in range(TT):
                square(2, t)
            for ct in range(KT):
                act.wait_ge(c_done, 3 * ct + 1)
                if ct >= 2:
                    act.wait_ge(c_evac, ct - 1)
                act.activation(c_sb[:, ct % 2, :], ps[:, 2 + 3 * (ct % 2), :], ACT.Copy).then_inc(c_copied, 1)
            norm_route(1)
            experts(1)
            overflow(1)
            load_pairs(1)
            act.dma_start(g_final, final_norm.partition_broadcast(P)).then_inc(g_final_loaded, 16)
            for t in range(TT):
                square(4, t)

        @block.vector
        def _(dve):
            n_chain = [0]

            def link(ins):
                n_chain[0] += 1
                ins.then_inc(dve_chain, 1)
                dve.wait_ge(dve_chain, n_chain[0])

            def normalise(n, t):
                k0 = 4 * n + t
                dve.wait_ge(rstd_ready, k0 + 1)
                if k0 >= 2:
                    dve.wait_ge(xT_done, k0 - 1)
                if n in (1, 3) and t >= 2:
                    dve.wait_ge(xn_stored[t % 2], 16 * (n // 2 * 2 + 1))
                dve.tensor_scalar(xn[:, t % 2, :], x_sb[:, t, :], rstd[:, n, t:t + 1], None,
                                  ALU.mult).then_inc(xn_ready, 1)

            def gain_T(n, t):
                k0 = 4 * n + t
                dve.wait_ge(xT_done, k0 + 1)
                g = (g_mix if n % 2 == 0 else g_ffn)[:, n // 2, :].unsqueeze(2).to_broadcast([P, KT, P])
                dve.tensor_tensor(hT[:, :, t * P:(t + 1) * P],
                                  ps[:, 0:2, :].rearrange("p b (k s) -> p (b k) s", s=P), g,
                                  ALU.mult).then_inc(hT_ready, 1)

            def residual(layer, t):
                dve.wait_ge(wo_done, 4 * layer + t + 1)
                b = 4 + 2 * (t % 2)
                dve.tensor_tensor(x_sb[:, t, :].rearrange("p (n c) -> p n c", n=2), ps[:, b:b + 2, :],
                                  x_sb[:, t, :].rearrange("p (n c) -> p n c", n=2), ALU.add).then_inc(x_ready, 1)

            def route(layer, t):
                dve.wait_ge(logits_done, 4 * layer + t + 1)
                dve.tensor_tensor(lg[:, t, 0:NG], ps[:, 2, t * 36:t * 36 + NG], router_b[:, layer, 0:NG], ALU.add)
                link(dve.tensor_tensor(lg[:, t, 8:8 + NE], ps[:, 2, t * 36 + NG:t * 36 + 36],
                                       router_b[:, layer, NG:], ALU.add))
                link(dve.max(g8[:, t, :], lg[:, t, 0:8]))
                link(dve.max_index(gi8[:, t, :], g8[:, t, :], lg[:, t, 0:8]))
                link(dve.tensor_copy(g_f[:, t, 0:1], gi8[:, t, 0:1]))
                dve.tensor_scalar(g_f[:, t, 1:2], g_f[:, t, 0:1], float(EG), None, ALU.mult)
                link(dve.tensor_scalar(g_hot[:, t, 0:NG], iota32[:, 0:NG], g_f[:, t, 0:1], None, ALU.is_equal))
                masked = g_hot[:, t, NG:].rearrange("p (e g) -> p e g", g=NG)
                link(dve.tensor_tensor(masked, lg[:, t, 8:].rearrange("p (g e) -> p e g", g=NG),
                                       g_hot[:, t, 0:NG].unsqueeze(1).to_broadcast([P, EG, NG]), ALU.mult))
                link(dve.tensor_reduce(esel[:, t, :], masked, AX_X, ALU.add))
                link(dve.max(e8[:, t, :], esel[:, t, :]))
                link(dve.max_index(ei8[:, t, :], e8[:, t, :], esel[:, t, :]))
                link(dve.tensor_copy(ei_f[:, t, :], ei8[:, t, 0:2]))
                link(dve.tensor_scalar(eid[:, t, :], ei_f[:, t, :], g_f[:, t, 1:2], None, ALU.add))
                dve.tensor_scalar(hot[:, t, 0, :], iota32[:, :], eid[:, t, 0:1], None, ALU.is_equal)
                link(dve.tensor_scalar(hot[:, t, 1, :], iota32[:, :], eid[:, t, 1:2], None, ALU.is_equal))
                dve.tensor_tensor(hot_bf[:, t, :], hot[:, t, 0, :], hot[:, t, 1, :], ALU.add).then_inc(hot_ready, 1)

            def place(layer, t):
                dve.wait_ge(rank_done, 4 * layer + t + 1)
                link(dve.tensor_tensor(rank_t[:, t], hot[:, t],
                                       ps[:, 3, t * NE:(t + 1) * NE].unsqueeze(1).to_broadcast([P, 2, NE]), ALU.mult))
                link(dve.tensor_reduce(rank[:, t, :], rank_t[:, t], AX_X, ALU.add))
                dve.scalar_tensor_tensor(out=dest[:, t, :], in0=rank[:, t, :], scalar=float(NE), in1=eid[:, t, :],
                                         op0=ALU.mult, op1=ALU.add).then_inc(dest_ready, 1)

            def w_out_norm_route(layer):
                n = 2 * layer + 1
                for t in range(TT):
                    residual(layer, t)
                    normalise(n, t)
                    if t >= 1:
                        gain_T(n, t - 1)
                        route(layer, t - 1)
                    if t >= 2:
                        place(layer, t - 2)
                gain_T(n, TT - 1)
                place(layer, TT - 2)
                route(layer, TT - 1)
                place(layer, TT - 1)
                dve.wait_ge(count_done, layer + 1)
                link(dve.tensor_copy(cnt_f[:, :], ps[0:1, 2, 256:256 + NE]))
                dve.tensor_copy(cnt_i[:, layer, :], cnt_f[:, :])
                link(dve.tensor_reduce(cnt_max[:, layer:layer + 1], cnt_f[:, :], AX_X, ALU.max))
                dve.memset(ps[:, 2, :], 0.0)
                link(dve.memset(ps[:, 3, :], 0.0))
                dve.engine_nop().then_inc(counts_ready, 1)
                dve.engine_nop().then_inc(psum_cleared, 1)
                dve.tensor_scalar(soft[:, 0, :], g8[:, :, 0], -1.0, None, ALU.mult)
                dve.tensor_tensor(soft[:, 2, :], e8[:, :, 1], e8[:, :, 0], ALU.subtract).then_inc(top_ready, 1)
                dve.wait_ge(list_loaded, 16 * (layer + 1))
                slot_tokens(slot_f[:, :], slot_pair[:, layer, :], slot_tok[:, layer, :])
                dve.engine_nop().then_inc(slots_ready, 1)
                dve.wait_ge(soft_exp, layer + 1)
                link(dve.tensor_scalar(soft[:, 4, :], soft[:, 3, :], 1.0, None, ALU.add))
                link(dve.tensor_tensor(soft[:, 5, :], soft[:, 4, :], soft[:, 1, :], ALU.mult))
                link(dve.reciprocal(pair_w[:, layer, 0, :], soft[:, 5, :]))
                link(dve.tensor_tensor(pair_w[:, layer, 1, :], pair_w[:, layer, 0, :], soft[:, 3, :], ALU.mult))

            def slot_tokens(tmp, pairs, toks):
                link(dve.tensor_scalar(tmp, pairs, float(S), -float(S), ALU.is_ge, ALU.mult))
                link(dve.tensor_tensor(toks, tmp, pairs, ALU.add))

            def gathered_gain(layer, dst, out_sem):
                g = g_ffn[:, layer, :].unsqueeze(2).to_broadcast([P, KT, P])
                dve.tensor_tensor(dst, ps[:, 0:2, :].rearrange("p b (k s) -> p (b k) s", s=P), g,
                                  ALU.mult).then_inc(out_sem, 1)

            def hidden(bank, sil_v, hid_v, out_sem):
                dve.tensor_tensor(hid_v, sil_v, ps[:, bank, 2 * P:4 * P], ALU.mult).then_inc(out_sem, 1)

            def experts(layer):
                base = NE * layer

                def gain_of(i, b, early):
                    g = base + i * RING + b
                    dve.wait_ge(gT_done, g + 1)
                    if not (early and layer == 0):
                        dve.wait_ge(gu_done, g - 1)
                    gathered_gain(layer, xgT[:, b % 2], xgT_ready)

                def hidden_of(i, b, first):
                    g = base + i * RING + b
                    dve.wait_ge(silu_done, g + 1)
                    if not (first and b < 2 and layer == 0):
                        dve.wait_ge(down_done, g - 1)
                    hidden(2 + b % 2, sil[:, b % 2, :], hid[:, b % 2, :], hid_ready)

                gain_of(0, 0, True)

                def body(i, first, last):
                    for b in range(RING):
                        if b < RING - 1:
                            gain_of(i, b + 1, first and b == 0)
                        elif not last:
                            gain_of(i + 1, 0, False)
                        hidden_of(i, b, first)
                expert_loop(dve, body)

            def overflow(layer):
                o = ov[layer]
                most = dve.value_load(cnt_max[0:1, layer:layer + 1], min_val=0, max_val=S)
                for r in range(OV_ROUNDS):
                    with dve.If(most > CAP * (r + 1)):
                        dve.wait_ge(o["list"], 16 * (r + 1))
                        dve.tensor_scalar(ov_f[:, :], ov_pair[:, :], float(S), -float(S), ALU.is_ge,
                                          ALU.mult).then_inc(o["idx"], 1)
                        dve.wait_ge(o["idx"], 2 * r + 1)
                        dve.tensor_tensor(ov_tok[:, :], ov_f[:, :], ov_pair[:, :], ALU.add).then_inc(o["idx"], 1)
                        with dve.Fori(0, NE) as e:
                            q = e + r * NE + 1
                            dve.wait_ge(o["T"], q)
                            gathered_gain(layer, xgT[:, 0], o["xT"])
                            dve.wait_ge(o["silu"], q)
                            hidden(2, sil[:, 0, :], hid[:, 0, :], o["hid"])

            def combine(layer, t):
                dve.wait_ge(yp_loaded[t], 16 * (layer + 1))
                for k in range(2):
                    ins = dve.scalar_tensor_tensor(out=x_sb[:, t, :], in0=yp[:, t, k, :],
                                                   scalar=pair_w[:, layer, k, t:t + 1], in1=x_sb[:, t, :],
                                                   op0=ALU.mult, op1=ALU.add)
                    if k == 0:
                        link(ins)
                ins.then_inc(x_ready, 1)

            dve.memset(neg_half[:, :], -0.5)
            dve.memset(zeros4[:, :], 0.0)
            dve.memset(lg[:, :, 4:8], NEG)
            dve.memset(m_state[:, 0:1], 0.0)
            dve.memset(mv[:, :, :, HD:HD + 1], 1.0)
            dve.wait_ge(masks_ready, 3)
            link(dve.tensor_copy(iota32[:, :], iota32_i[:, :]))
            link(dve.tensor_copy(ident_bf[:, :], ident[:, :]))
            dve.engine_nop().then_inc(consts_ready, 1)

            for t in range(TT):
                normalise(0, t)
                if t == 0:
                    dve.wait_ge(consts_loaded, 16 * N_CONST)
                else:
                    gain_T(0, t - 1)
            gain_T(0, TT - 1)

            link(dve.tensor_tensor(lam_t[:, :, :], lam_sb[:, 0::2, :], lam_sb[:, 1::2, :], ALU.mult))
            dve.tensor_reduce(lam_c[:, 0:2], lam_t[:, :, :], AX_X, ALU.add).then_inc(lam_sum, 1)
            dve.tensor_scalar(g_diff_s[:, :], g_diff[:, :], 1.0 - LAM_INIT, None, ALU.mult)

            link(dve.tensor_copy(pos_f[:, :], pos_i[:, :]))
            for t in range(TT):
                ins = dve.tensor_scalar(ang[:, 0, t, :], invf[:, :], pos_f[:, t:t + 1], None, ALU.mult)
            link(ins)
            link(dve.tensor_scalar(ang[:, 1], ang[:, 0], 0.15915494309189535, MAGIC, ALU.mult, ALU.add))
            link(dve.tensor_scalar(ang[:, 1], ang[:, 1], MAGIC, None, ALU.subtract))
            for c in TWO_PI:
                link(dve.scalar_tensor_tensor(out=ang[:, 0], in0=ang[:, 1], scalar=-c, in1=ang[:, 0],
                                              op0=ALU.mult, op1=ALU.add))
            link(dve.tensor_scalar(ang[:, 2], ang[:, 0], PI_IN, -PI_IN, ALU.min, ALU.max))
            link(dve.tensor_scalar(ang[:, 0], ang[:, 0], 1.5707963267948966, None, ALU.add))
            link(dve.tensor_scalar(ang[:, 1], ang[:, 0], PI_IN, -6.283185307179586, ALU.is_gt, ALU.mult))
            link(dve.tensor_tensor(ang[:, 3], ang[:, 0], ang[:, 1], ALU.add))
            dve.tensor_scalar(ang[:, 3], ang[:, 3], PI_IN, -PI_IN, ALU.min, ALU.max).then_inc(angles_ready, 1)
            dve.wait_ge(lam_exp, 1)
            link(dve.scalar_tensor_tensor(out=lam_c[:, 4:5], in0=lam_c[:, 3:4], scalar=-LAM_INIT, in1=lam_c[:, 2:3],
                                          op0=ALU.add, op1=ALU.subtract))

            def gates_a():
                dve.wait_ge(proj_done, 1)
                link(dve.tensor_tensor(gates[:, :, :], ps[:, 0, 0:TT * 8].rearrange("p (t c) -> p t c", t=TT),
                                       gate_b[:, :].unsqueeze(1).to_broadcast([P, TT, 2 * H]), ALU.add))
                link(dve.tensor_scalar(gate_tmp[:, 1], gates[:, :, H:], -1.0, None, ALU.mult))
                dve.tensor_tensor(gate_tmp[:, 0], gates[:, :, H:], gate_tmp[:, 1], ALU.max).then_inc(gates_abs, 1)

            def gates_b():
                dve.wait_ge(gates_ln, 1)
                dve.scalar_tensor_tensor(out=gates[:, :, H:], in0=gates[:, :, H:], scalar=0.0, in1=gate_tmp[:, 2],
                                         op0=ALU.min, op1=ALU.subtract).then_inc(gates_ready, 1)

            def gate_rows():
                dve.wait_ge(gateT_done, 1)
                for i in range(TT):
                    q = slice(i * P, (i + 1) * P)
                    ins = dve.tensor_tensor_scan(row_b[:, q], ps[0:H, 7, q], zeros4[:, :], 0.0, ALU.add, ALU.add)
                link(ins)
                link(dve.tensor_tensor(row_u[:, :], ps[0:H, 6, :], row_b[:, :], ALU.subtract))
                for i in range(TT):
                    q = slice(i * P, (i + 1) * P)
                    end = (i + 1) * P - 1
                    link(dve.tensor_tensor_scan(row_c[:, q], row_u[:, q], row_u[:, q], m_state[:, i:i + 1],
                                                ALU.max, ALU.max))
                    link(dve.tensor_tensor(m_state[:, i + 1:i + 2], row_c[:, end:end + 1], row_b[:, end:end + 1],
                                           ALU.add))
                dve.tensor_scalar(negc[:, :], row_c[:, :], -1.0, None, ALU.mult)
                link(dve.scalar_tensor_tensor(out=row_m[:, :], in0=row_b[:, :], scalar=-1.0, in1=row_c[:, :],
                                              op0=ALU.mult, op1=ALU.subtract))
                for (j, i), n in OFF.items():
                    prev = row_u[:, j * P:(j + 1) * P] if i == j + 1 else row_off[:, OFF[(j, i - 1)], :]
                    link(dve.tensor_scalar(row_off[:, n, :], prev, row_b[:, i * P - 1:i * P], None, ALU.add))
                dve.engine_nop().then_inc(rows_ready, 1)

            def rope(r):
                j = r + 1
                t = r % 4
                if r == 0:
                    dve.wait_ge(rope_table, 1)
                dve.wait_ge(proj_done, j + 1)
                if r >= 2:
                    dve.wait_ge(roped_ready, r - 1)
                src = ps[:, j % 2, :].rearrange("p (g e) -> p g e", e=HALF)
                for tab, dst in ((cos_t, rope_a), (sin_t, rope_b)):
                    ins = dve.tensor_tensor(dst[:, r % 2, :].rearrange("p (g e) -> p g e", e=HALF), src,
                                            tab[:, t, :].unsqueeze(1).to_broadcast([P, 2 * 2 * H, HALF]), ALU.mult)
                ins.then_inc(rope_parts, 1)

            def conv(j):
                ch = j - 17
                dve.wait_ge(proj_done, j + 1)
                if ch >= 2:
                    dve.wait_ge(qk_ready, ch - 1)
                acc = conv_acc[:, j % 2, :]
                src = ps[:, j % 2, :]
                link(dve.tensor_scalar(acc, src, conv0_w[:, ch, 3:4], None, ALU.mult))
                for s in range(1, 4):
                    ins = dve.scalar_tensor_tensor(out=acc[:, s:S], in0=src[:, 0:S - s],
                                                   scalar=conv0_w[:, ch, 3 - s:4 - s], in1=acc[:, s:S],
                                                   op0=ALU.mult, op1=ALU.add)
                    if s < 3:
                        link(ins)
                ins.then_inc(conv_ready, 1)

            def att_maxima(a):
                n = (a % TT + 1) * P
                dve.wait_ge(att_scores, a + 1)
                link(dve.tensor_reduce(att_s[:, 0:2], ps[:, 4:6, 0:n], AX_X, ALU.max))
                dve.tensor_scalar(att_s[:, 2:4], att_s[:, 0:2], -(DD ** -0.5), None, ALU.mult).then_inc(att_max, 1)

            def att_combine(a):
                n = (a % TT + 1) * P
                dve.wait_ge(att_exp, a + 1)
                if a >= 1:
                    dve.wait_ge(att_T, a)
                link(dve.reciprocal(att_s[:, 6:8], att_s[:, 4:6]))
                link(dve.tensor_tensor(att_s[:, 8:9], att_s[:, 7:8], lam_c[:, 4:5], ALU.mult))
                link(dve.tensor_scalar(att_e[:, 1, 0:n], att_e[:, 1, 0:n], att_s[:, 8:9], None, ALU.mult))
                dve.scalar_tensor_tensor(out=att_a[:, 0:n], in0=att_e[:, 0, 0:n], scalar=att_s[:, 6:7],
                                         in1=att_e[:, 1, 0:n], op0=ALU.mult, op1=ALU.add).then_inc(att_probs, 1)

            def att_norm(h):
                dve.wait_ge(att_o_copied, h + 1)
                link(dve.tensor_tensor(att_q[:, :], att_o[:, :], att_o[:, :], ALU.mult))
                dve.tensor_reduce(hn[:, h, :], att_q[:, :].rearrange("p (i e) -> p i e", e=HD), AX_X,
                                  ALU.add).then_inc(head_ss, 1)
                dve.wait_ge(head_rstd, h + 1)
                v = att_o[:, :].rearrange("p (i e) -> p i e", e=HD)
                dve.tensor_tensor(v, v, hn_r[:, h, :].unsqueeze(2).to_broadcast([P, TT, HD]),
                                  ALU.mult).then_inc(att_normed, 1)

            for j in range(ATT0 + 19):
                if j == 0:
                    gates_a()
                elif j < 9:
                    rope(j - 1)
                elif 17 <= j < 25:
                    conv(j)
                if j == 0:
                    gates_b()
                if j == 2:
                    gate_rows()
                if j == 7:
                    dve.wait_ge(rowsT_done, 1)
                    dve.tensor_copy(ucol[:, :, :], ps[:, 5, 0:(len(PAIRS) + TT) * H].rearrange(
                        "p (n h) -> p n h", h=H)).then_inc(ucol_ready, 1)
                a = j - ATT0
                if 0 <= a < 16:
                    att_maxima(a)
                    att_combine(a)
                if a >= 5 and (a - 5) % 4 == 0 and (a - 5) // 4 < H:
                    att_norm((a - 5) // 4)

            def ml_weighted(h):
                dve.wait_ge(ml_masked, 4 * h + 4)
                if h >= 2:
                    dve.wait_ge(ml_num, h - 1)
                for j in range(TT):
                    bank, c0 = ML_BANK[j]
                    w = S - j * P
                    ins = dve.scalar_tensor_tensor(out=ml_s[:, h % 2, ML_COL[j]:ML_COL[j] + w],
                                                   in0=ps[:, bank, c0:c0 + w], scalar=HD ** -0.5,
                                                   in1=ml_w[:, h % 2, ML_COL[j]:ML_COL[j] + w],
                                                   op0=ALU.mult, op1=ALU.mult)
                ins.then_inc(ml_sT, 1)

            def ml_normalise(h):
                dve.wait_ge(ml_num, h + 1)
                if h == 0:
                    dve.wait_ge(em_ready, 1)
                if h >= 2:
                    dve.wait_ge(ml_fT, h - 1)
                nd = ps[:, 5:7, 0:2 * (HD + 1)].rearrange("p b (i e) -> p b i e", e=HD + 1)
                two = "p (b i) -> p b i"
                link(dve.tensor_copy(den_t[:, 0, :].rearrange(two, b=2), nd[:, :, :, HD]))
                link(dve.tensor_scalar(den_t[:, 1, :], den_t[:, 0, :], -1.0, None, ALU.mult))
                link(dve.tensor_tensor(den_t[:, 2, :], den_t[:, 0, :], den_t[:, 1, :], ALU.max))
                link(dve.tensor_tensor(den_t[:, 1, :], den_t[:, 2, :], em[:, :, h], ALU.max))
                link(dve.reciprocal(den_t[:, 3, :], den_t[:, 1, :]))
                hm = ml_h[:, h % 2, :]
                for b in range(2):
                    ins = dve.tensor_tensor(hm[:, b * 256:(b + 1) * 256].rearrange("p (i e) -> p i e", e=HD),
                                            nd[:, b, :, 0:HD],
                                            den_t[:, 3, 2 * b:2 * b + 2].unsqueeze(2).to_broadcast([P, 2, HD]),
                                            ALU.mult)
                link(ins)
                link(dve.tensor_tensor(ml_q[:, :], hm, hm, ALU.mult))
                dve.tensor_reduce(hn[:, H + h, :], ml_q[:, :].rearrange("p (i e) -> p i e", e=HD), AX_X,
                                  ALU.add).then_inc(head_ss, 1)
                dve.wait_ge(head_rstd, H + h + 1)
                for i in range(TT):
                    q = slice(i * P, (i + 1) * P)
                    ins = dve.scalar_tensor_tensor(out=hm[:, q], in0=hm[:, q], scalar=hn_r[:, H + h, i:i + 1],
                                                   in1=o_gate[:, i, h * HD:(h + 1) * HD],
                                                   op0=ALU.mult, op1=ALU.mult)
                ins.then_inc(ml_normed, 1)

            ml_weighted(0)
            for h in range(H):
                if h + 1 < H:
                    ml_weighted(h + 1)
                if h == 0:
                    dve.wait_ge(ogate_ready, TT)
                ml_normalise(h)

            w_out_norm_route(0)
            experts(0)
            overflow(0)

            for t in range(TT):
                combine(0, t)
                normalise(2, t)
                if t:
                    gain_T(2, t - 1)
            gain_T(2, TT - 1)
            for ct in range(KT):
                b = 2 + 3 * (ct % 2)
                dve.wait_ge(c_copied, ct + 1)
                dve.wait_ge(c_done, 3 * ct + 2)
                v, acc = cx[:, ct % 2, :], c_acc[:, ct % 2, :]
                link(dve.tensor_tensor(v, c_sb[:, ct % 2, :], ps[:, b + 1, :], ALU.mult))
                link(dve.tensor_scalar(acc, v, conv1_w[:, ct, 2:3], None, ALU.mult))
                for s in range(1, 3):
                    link(dve.scalar_tensor_tensor(out=acc[:, s:S], in0=v[:, 0:S - s],
                                                  scalar=conv1_w[:, ct, 2 - s:3 - s], in1=acc[:, s:S],
                                                  op0=ALU.mult, op1=ALU.add))
                dve.wait_ge(c_done, 3 * ct + 3)
                dve.tensor_tensor(yT[:, ct, :], acc, ps[:, b + 2, :], ALU.mult).then_inc(c_evac, 1)
            w_out_norm_route(1)
            experts(1)
            overflow(1)

            dve.wait_ge(g_final_loaded, 16)
            for t in range(TT):
                combine(1, t)
                dve.wait_ge(rstd_ready, 16 + t + 1)
                dve.scalar_tensor_tensor(out=fin[:, t, :], in0=x_sb[:, t, :], scalar=rstd[:, 4, t:t + 1],
                                         in1=g_final, op0=ALU.mult, op1=ALU.mult).then_inc(out_ready, 1)

        @block.gpsimd
        def _(pool):
            n_chain = [0]

            def link(ins):
                n_chain[0] += 1
                ins.then_inc(pool_chain, 1)
                pool.wait_ge(pool_chain, n_chain[0])

            def root(n, t):
                pool.wait_ge(sumsq, 4 * n + t + 1)
                link(pool.tensor_scalar(ms[:, n, t:t + 1], ss[:, n, t:t + 1], 1.0 / D, EPS, ALU.mult, ALU.add))
                pool.tensor_tensor(rstd[:, n, t:t + 1], ms[:, n, t:t + 1], neg_half[:, 0:1],
                                   ALU.pow).then_inc(rstd_ready, 1)

            def head_root(m):
                pool.wait_ge(head_ss, m + 1)
                link(pool.tensor_scalar(hn_ms[:, m, :], hn[:, m, :], 1.0 / HD, EPS, ALU.mult, ALU.add))
                pool.tensor_tensor(hn_r[:, m, :], hn_ms[:, m, :], neg_half[:, :], ALU.pow).then_inc(head_rstd, 1)

            pool.memset(ident[:, :], 0.0)
            pool.memset(causal_bf[:, :], 0.0)
            pool.memset(before_bf[:, :], 0.0)
            pool.memset(ones_bf[:, :], 1.0)
            pool.memset(empty_i[:, :], EMPTY)
            pool_zero = pool.engine_nop()
            link(pool_zero)
            pool.affine_select(out=ident[:, :], in_=ident[:, :], compare_op=ALU.not_equal, fill=1.0, base=0,
                               pattern=[[-1, P]], channel_multiplier=1)
            pool.affine_select(out=causal_bf[:, :], in_=causal_bf[:, :], compare_op=ALU.is_ge, fill=MASK, base=0,
                               pattern=[[-1, P]], channel_multiplier=1)
            pool.affine_select(out=before_bf[:, :], in_=before_bf[:, :], compare_op=ALU.is_ge, fill=1.0, base=0,
                               pattern=[[-1, P]], channel_multiplier=1)
            pool.iota(iota32_i[:, :], [[1, NE]], base=0, channel_multiplier=0)
            link(pool.iota(pair_id[:, :, :], [[P, TT], [S, 2]], base=0, channel_multiplier=1))
            pool.engine_nop().then_inc(masks_ready, 3)
            for n in range(2):
                pool.dma_start(list_dram[n].rearrange("(p c) o -> p (c o)", c=P), empty_i[:, :]).then_inc(
                    lists_empty, 16)

            pool.wait_ge(consts_ready, 1)
            for t in range(TT):
                root(0, t)
            for r in range(8):
                pool.wait_ge(rope_parts, r + 1)
                if r >= 2:
                    pool.wait_ge(ropeT_done, r - 1)
                a, b, o = (v[:, r % 2, :].rearrange("p (g x e) -> p g x e", x=2, e=HALF)
                           for v in (rope_a, rope_b, roped))
                pool.tensor_tensor(o[:, :, 0, :], a[:, :, 0, :], b[:, :, 1, :], ALU.subtract)
                pool.tensor_tensor(o[:, :, 1, :], a[:, :, 1, :], b[:, :, 0, :], ALU.add).then_inc(roped_ready, 1)
            for h in range(H):
                head_root(h)

            def ml_mask(h):
                pool.wait_ge(ml_exp, h + 1)
                for j in range(TT):
                    v = ml_w[:, h % 2, ML_COL[j]:ML_COL[j] + P]
                    pool.affine_select(out=v, in_=v, compare_op=ALU.is_ge, fill=0.0, base=0, pattern=[[1, P]],
                                       channel_multiplier=-1).then_inc(ml_masked, 1)

            ml_mask(0)
            for h in range(H):
                if h + 1 < H:
                    ml_mask(h + 1)
                head_root(H + h)

            def slot_lists(layer):
                n = 2 * layer + 1
                for t in range(TT):
                    root(n, t)
                    if t >= 2:
                        scatter_ids(layer, t - 2)
                scatter_ids(layer, TT - 2)
                scatter_ids(layer, TT - 1)
                pool.wait_ge(list_stored, 16 * 2 * TT * (layer + 1))
                pool.dma_start(slot_pair[:, layer, :], list_dram[layer][0:CAP * NE, :].rearrange(
                    "(s e) o -> s (e o)", e=NE)).then_inc(list_loaded, 16)

            def scatter_ids(layer, t):
                pool.wait_ge(dest_ready, 4 * layer + t + 1)
                if layer == 0 and t == 0:
                    pool.wait_ge(lists_empty, 32)
                for k in range(2):
                    pool.indirect_dma_start(
                        out=list_dram[layer][:, :], out_offset=bass.IndirectOffsetOnAxis(ap=dest[:, t, k:k + 1], axis=0),
                        in_=pair_id[:, t, k:k + 1], in_offset=None, bounds_check=S * NE - 1,
                        oob_is_err=False).then_inc(list_stored, 16)

            def gather(layer, tokens, dst, out_sem):
                pool.sem_inc(indirect_turn, 1)
                pool.indirect_dma_start(
                    out=dst, out_offset=None, in_=xn_dram[layer][:, :],
                    in_offset=bass.IndirectOffsetOnAxis(ap=tokens, axis=0),
                    bounds_check=last_token, oob_is_err=False).then_inc(out_sem, 16)

            def scatter(layer, pairs, src, out_sem):
                pool.sem_inc(indirect_turn, 1)
                pool.indirect_dma_start(
                    out=pair_dram[layer][:, :], out_offset=bass.IndirectOffsetOnAxis(ap=pairs, axis=0),
                    in_=src, in_offset=None, bounds_check=last_pair, oob_is_err=False).then_inc(out_sem, 16)

            def experts(layer):
                base = NE * layer
                pool.wait_ge(x_ready, 8 * layer + TT)
                link(pool.memset(xg[:, :, :], 0.0))
                pool.wait_ge(slots_ready, layer + 1)
                for b in range(2):
                    pool.wait_ge(xn_stored[b], 32 * (layer + 1))

                def gather_step(e, b):
                    pool.tensor_copy(tok_now[:, b:b + 1], slot_tok[:, layer, bass.ds(e, 1)]).then_inc(tok_copied, 1)
                    pool.wait_ge(tok_copied, base + e + 1)
                    gather(layer, tok_now[:, b:b + 1], xg[:, b, :], xg_loaded[b])

                for b in range(XB):
                    gather_step(b, b)

                def body(i, first, last):
                    for b in range(RING):
                        e = i * RING + b
                        pool.tensor_copy(pair_now[:, b:b + 1], slot_pair[:, layer, bass.ds(e, 1)]).then_inc(
                            pair_copied, 1)
                        pool.wait_ge(y_ready, base + e + 1)
                        pool.wait_ge(pair_copied, base + e + 1)
                        scatter(layer, pair_now[:, b:b + 1], y_sb[:, b % 2, :], y_stored[b % 2])
                        if not last:
                            pool.wait_ge(gT_done, base + e + 1)
                            gather_step(e + XB, b)
                expert_loop(pool, body)
                for b in range(2):
                    pool.wait_ge(y_stored[b], 16 * (NE // 2) * (layer + 1))

            def overflow(layer):
                o = ov[layer]
                pool.wait_ge(counts_ready, layer + 1)
                most = pool.value_load(cnt_max[0:1, layer:layer + 1], min_val=0, max_val=S)
                for r in range(OV_ROUNDS):
                    with pool.If(most > CAP * (r + 1)):
                        s0 = CAP * (r + 1) * NE
                        pool.dma_start(ov_pair[:, :], list_dram[layer][s0:s0 + CAP * NE, :].rearrange(
                            "(s e) o -> s (e o)", e=NE)).then_inc(o["list"], 16)
                        pool.wait_ge(o["idx"], 2 * r + 2)
                        with pool.Fori(0, NE) as e:
                            q = e + r * NE + 1
                            pool.tensor_copy(tok_now[:, 0:1], ov_tok[:, bass.ds(e, 1)])
                            pool.tensor_copy(pair_now[:, 0:1], ov_pair[:, bass.ds(e, 1)]).then_inc(o["copied"], 1)
                            pool.wait_ge(o["copied"], q)
                            gather(layer, tok_now[:, 0:1], xg[:, 0, :], o["rows"])
                            pool.wait_ge(o["y"], q)
                            scatter(layer, pair_now[:, 0:1], y_sb[:, 0, :], o["stored"])
                            pool.wait_ge(o["stored"], 16 * q)
                pool.memset(fence[:, layer:layer + 1], 0.0).then_inc(pairs_stored, 1)

            last_token = pool.to_reg(S - 1)
            last_pair = pool.to_reg(2 * S - 1)
            slot_lists(0)
            experts(0)
            overflow(0)
            for t in range(TT):
                root(2, t)
            slot_lists(1)
            experts(1)
            overflow(1)
            for t in range(TT):
                root(4, t)


OFF = {p: n for n, p in enumerate([(j, i) for j in range(TT) for i in range(j + 1, TT)])}
ML_BANK = [(2, 0), (3, 0), (4, 0), (3, 384)]
ML_COL = [0, 512, 896, 1152]


_INS = ['x', 'positions', 'norm_mix', 'norm_ffn', 'ab_w_in', 'ab_gate_bias', 'ab_conv_w', 'ab_mlstm_norm',
        'ab_lambda', 'ab_diff_norm', 'ab_w_out', 'c_w_in', 'c_conv_w', 'c_w_out', 'moe_w_rg', 'moe_b_rg',
        'moe_w_re', 'moe_b_re', 'moe_w_gate', 'moe_w_up', 'moe_w_down', 'final_norm']


def kernel(**inputs):
    import numpy as _np
    import concourse.bacc as _bacc
    from concourse.bass_utils import run_bass_kernel_spmd as _run

    nc = _bacc.Bacc("TRN2", target_bir_lowering=False, num_devices=1)
    arrays, aps = {}, {}

    def give(name, a):
        a = _np.ascontiguousarray(a)
        arrays[f"in_{name}"] = a
        aps[name] = nc.dram_tensor(f"in_{name}", a.shape, mybir.dt.from_np(a.dtype), kind="ExternalInput").ap()

    for name in _INS:
        a = _np.asarray(inputs[name])
        if name in ('x', 'positions') or name.startswith('ab_') or name.startswith('c_'):
            a = a[0]
        if name in ('ab_conv_w', 'c_conv_w'):
            a = a.reshape(a.shape[0], -1, P).transpose(2, 1, 0)
        if name.startswith('moe_w_') and a.ndim == 5:
            a = a.reshape(a.shape[0], NE, *a.shape[3:])
        give(name, a)
    half = _np.arange(HALF, dtype=_np.float32) / _np.float32(HALF)
    give('inv_freq', (_np.float32(1.0) / _np.power(_np.float32(10000.0), half)).astype(_np.float32))
    out = nc.dram_tensor("out_dram", (S, D), F32, kind="ExternalOutput").ap()
    build(nc, *[aps[n] for n in _INS], aps['inv_freq'], out)
    r = _run(nc, [arrays], core_ids=[0])
    return r.results[0]["out_dram"].reshape(1, S, D)
```

```python
from contextlib import ExitStack

import concourse.bass as bass
from concourse import mybir

ALU = mybir.AluOpType
ACT = mybir.ActivationFunctionType
AX_X = mybir.AxisListType.X
F32 = mybir.dt.float32
F32R = mybir.dt.float32r
BF16 = mybir.dt.bfloat16
I32 = mybir.dt.int32
U32 = mybir.dt.uint32

P = 128
D = 1024
S = 512
KT = D // P
TT = S // P
H = 4
HD = 128
DD = 64
HALF = DD // 2
EPS = 1e-6
NG = 4
EG = 8
NE = NG * EG
FF = 256
FT = FF // P
CAP = P
SMALL = 64
TINY = 32
RING = 4
SLOT = 3 * KT * FF
XB = 4
LAM_INIT = 0.2
NEG = -3.0e38
MASK = -1.0e30
EMPTY = 1 << 14
OV_ROUNDS = S // CAP - 1

C_MQK, C_MV, C_MO, C_GATE, C_DQ, C_DK, C_DV = 0, 1024, 1536, 2048, 2056, 2568, 3080

L0_COLS = [C_DQ, C_DK, C_DV, C_MV, C_MQK, C_MQK + 512, C_MO]
N_HALF = 2 * len(L0_COLS)
HC = 256
N_MIX0 = N_HALF + 2
N_MIX1 = KT + 2
EXPERT_USE = [N_MIX0, N_MIX0 + NE + N_MIX1]
MIX_USE = [0, N_MIX0 + NE]
MIX_DONE = [0, N_MIX0]

PAIRS = [(j, i) for j in range(TT) for i in range(j, TT)]

TWO_PI = (6.28125, 0.00193023681640625, 5.066394805908203e-06, 3.795019905382127e-09)
PI_IN = 3.1415925
MAGIC = 12582912.0


def build(nc, x_in, positions, norm_mix, norm_ffn, w_in0, gate_bias, conv0, mlstm_norm, lam_vecs,
          diff_norm, w_out0, w_in1, conv1, w_out1, w_rg, b_rg, w_re, b_re, w_gate, w_up, w_down,
          final_norm, inv_freq, out):
    with ExitStack() as ctx:
        def sb(name, shape, dt=F32):
            return ctx.enter_context(nc.sbuf_tensor(name, shape, dt))

        def shared(name, shape):
            with nc.sbuf_tensor(name + "_r", shape, F32R) as r:
                pass
            return r, sb(name, shape)

        def sem(name):
            return ctx.enter_context(nc.semaphore(name))

        ps = ctx.enter_context(nc.psum_tensor("ps", [P, 8, 512], F32))
        x_r, x_sb = shared("x_sb", [P, TT, D])
        hT_h, hT = shared("hT", [P, KT, S])
        ring_r, ring = shared("ring", [P, RING, SLOT])
        work_r, work = shared("work", [P, 16400])
        ident = sb("ident", [P, P])
        ident_bf = sb("ident_bf", [P, P], BF16)
        causal_bf = sb("causal_bf", [P, P], BF16)
        before_bf = sb("before_bf", [P, P], BF16)
        ones_bf = sb("ones_bf", [P, P], BF16)
        zeros4 = sb("zeros4", [H, P])
        iota32 = sb("iota32", [P, NE])
        iota32_i = sb("iota32_i", [P, NE], I32)
        pair_id = sb("pair_id", [P, TT, 2], I32)
        empty_i = sb("empty_i", [P, P], I32)
        g_mix = sb("g_mix", [P, 2, KT])
        g_ffn = sb("g_ffn", [P, 2, KT])
        g_mlstm = sb("g_mlstm", [P, 1])
        g_diff = sb("g_diff", [P, 1])
        g_diff_s = sb("g_diff_s", [P, 1])
        gate_w = sb("gate_w", [P, KT, 2 * H])
        gate_b = sb("gate_b", [P, 2 * H])
        conv0_w = sb("conv0_w", [P, KT, 4])
        conv1_w = sb("conv1_w", [P, KT, 3])
        lam_c = sb("lam_c", [P, 8])
        router_w = sb("router_w", [P, 2, KT, NG + NE])
        router_b = sb("router_b", [P, 2, NG + NE])
        pos_i = sb("pos_i", [P, TT], I32)
        pos_f = sb("pos_f", [P, TT])
        invf = sb("invf", [P, HALF])
        sin_t = sb("sin_t", [P, TT, HALF])
        cos_t = sb("cos_t", [P, TT, HALF])
        ss = sb("ss", [P, 5, TT])
        ms = sb("ms", [P, 5, TT])
        rstd = sb("rstd", [P, 5, TT])
        neg_half = sb("neg_half", [P, TT])
        gates = sb("gates", [P, TT, 2 * H])
        gate_tmp = sb("gate_tmp", [P, 3, TT, H])
        negc = sb("negc", [H, S])
        m_state = sb("m_state", [H, TT + 1])
        ucol = sb("ucol", [P, len(PAIRS) + TT, H])
        em = sb("em", [P, TT, H])
        att_s = sb("att_s", [P, 12])
        hn = sb("hn", [P, 8, TT])
        hn_ms = sb("hn_ms", [P, 8, TT])
        hn_r = sb("hn_r", [P, 8, TT])
        den_t = sb("den_t", [P, 4, TT])
        lg = sb("lg", [P, TT, 8 + NE])
        g8 = sb("g8", [P, TT, 8])
        gi8 = sb("gi8", [P, TT, 8], U32)
        g_hot = sb("g_hot", [P, TT, 4 + EG * NG])
        g_f = sb("g_f", [P, TT, 2])
        esel = sb("esel", [P, TT, EG])
        e8 = sb("e8", [P, TT, 8])
        ei8 = sb("ei8", [P, TT, 8], U32)
        ei_f = sb("ei_f", [P, TT, 2])
        eid = sb("eid", [P, TT, 2])
        hot_bf = sb("hot_bf", [P, TT, NE], BF16)
        rank = sb("rank", [P, TT, 2])
        dest = sb("dest", [P, TT, 2], I32)
        soft = sb("soft", [P, 6, TT])
        pair_w = sb("pair_w", [P, 2, 2, TT])
        cnt_f = sb("cnt_f", [1, NE])
        cnt_i = sb("cnt_i", [1, 2, NE], I32)
        cnt_max = sb("cnt_max", [1, 2], I32)
        slot_pair = sb("slot_pair", [P, 2, NE], I32)
        slot_tok = sb("slot_tok", [P, 2, NE], I32)
        slot_f = sb("slot_f", [P, NE])
        slot_half = sb("slot_half", [P, 2, NE], I32)
        half_of = sb("half_of", [P, 1])
        tok_now = sb("tok_now", [P, XB], I32)
        pair_now = sb("pair_now", [P, XB], I32)
        half_now = sb("half_now", [P, XB], I32)
        fence = sb("fence", [1, 2])

        def part(start, size, pattern=None, **kw):
            v = work[:, start:start + size]
            return v.rearrange(pattern, **kw) if pattern else v

        ang = part(0, 512, "p (n t e) -> p n t e", n=4, t=TT)
        lam_sb = part(512, 256, "p (n d) -> p n d", n=4)
        lam_t = part(768, 128, "p (n d) -> p n d", n=2)
        dqT = part(0, 2048, "p (h s) -> p h s", h=H)
        dkT = part(2048, 2048, "p (h s) -> p h s", h=H)
        dv = part(4096, 2048, "p (t c) -> p t c", t=TT)
        mv = part(6144, TT * H * (HD + 1), "p (t h e) -> p t h e", t=TT, h=H)
        qkT = part(8208, 4096, "p (c s) -> p c s", c=2 * H)
        rope_a = part(12304, 1024, "p (b c) -> p b c", b=2)
        rope_b = part(13328, 1024, "p (b c) -> p b c", b=2)
        roped = part(14352, 1024, "p (b c) -> p b c", b=2)
        conv_acc = part(15376, 1024, "p (b c) -> p b c", b=2)
        att_e = part(12304, 1024, "p (c k) -> p c k", c=2)
        att_a = part(13328, 512)
        att_aT = part(13840, 512)
        att_o = part(14352, 512)
        att_q = part(14864, 512)
        row_b = work[0:H, 8208:8720]
        row_u = work[0:H, 8720:9232]
        row_c = work[0:H, 9232:9744]
        row_m = work[0:H, 9744:10256]
        row_off = work[0:H, 10256:11280].rearrange("p (n j) -> p n j", n=8)
        ml_w = part(0, 2560, "p (b k) -> p b k", b=2)
        ml_s = part(2560, 2560, "p (b k) -> p b k", b=2)
        ml_h = part(5120, 1024, "p (b k) -> p b k", b=2)
        ml_q = part(14352, 512)
        gate_h = work_r[:, 1024:1024 + KT * 2 * H].rearrange("p (k c) -> p k c", k=KT)
        gate_l = work_r[:, 2048:2048 + KT * 2 * H].rearrange("p (k c) -> p k c", k=KT)
        o_gate = ring[:, 2, 4096:6144].rearrange("p (t c) -> p t c", t=TT)
        mergedM = hT[:, 0:H, :]
        mergedD = ring[:, 3, 4096:6144].rearrange("p (h s) -> p h s", h=H)
        xn = part(12304, 2048, "p (b c) -> p b c", b=2)
        junk = part(15376, 1024)
        hot = part(8208, TT * 2 * NE, "p (t k e) -> p t k e", t=TT, k=2)
        rank_t = part(8464, TT * 2 * NE, "p (t k e) -> p t k e", t=TT, k=2)
        xg = part(0, XB * D, "p (b c) -> p b c", b=XB)
        xgT = part(4096, 2048, "p (b k s) -> p b k s", b=2, k=KT)
        hid = part(6144, 512, "p (b c) -> p b c", b=2)
        sil = part(6656, 512, "p (b c) -> p b c", b=2)
        y_sb = part(7168, 2048, "p (b c) -> p b c", b=2)
        ov_w = part(9216, SLOT)
        ov_pair = part(15376, NE).bitcast(I32)
        ov_tok = part(15408, NE).bitcast(I32)
        ov_f = part(15440, NE)
        hidT = part(15472, 512, "p (b c) -> p b c", b=2)
        yp = part(0, 8192, "p (t k c) -> p t k c", t=TT, k=2)
        fin = part(8192, 4096, "p (t c) -> p t c", t=TT)
        g_final = part(12304, 1024)
        rest1 = work_r[:, 8208:8208 + 4096].rearrange("p (k s) -> p k s", k=KT)

        def hT_rest(n, t):
            if n == 0:
                return x_r[:, t, :].rearrange("p (k s) -> p k s", k=KT)
            return rest1[:, :, t * P:(t + 1) * P]

        yT = part(0, 4096, "p (c s) -> p c s", c=KT)
        c_sb = part(4096, 1024, "p (b s) -> p b s", b=2)
        cx = part(5120, 1024, "p (b s) -> p b s", b=2)
        c_acc = part(6144, 1024, "p (b s) -> p b s", b=2)

        xn_dram = [nc.dram_tensor(f"xn_rows_{n}", [S, D], F32).ap() for n in range(2)]
        pair_dram = [nc.dram_tensor(f"pair_rows_{n}", [2 * S, D], F32).ap() for n in range(2)]
        list_dram = [nc.dram_tensor(f"slot_list_{n}", [S * NE, 1], I32).ap() for n in range(2)]

        x_loaded = [sem(f"x_loaded_{t}") for t in range(TT)]
        first_loaded = sem("first_loaded")
        consts_loaded = sem("consts_loaded")
        slot_loaded = [sem(f"slot_loaded_{s}") for s in range(RING)]
        mixer_used = sem("mixer_used")
        masks_ready = sem("masks_ready")
        pool_chain = sem("pool_chain")
        dve_chain = sem("dve_chain")
        act_chain = sem("act_chain")
        consts_ready = sem("consts_ready")
        lists_empty = sem("lists_empty")
        angles_ready = sem("angles_ready")
        rope_table = sem("rope_table")
        lam_sum = sem("lam_sum")
        lam_exp = sem("lam_exp")
        x_ready = sem("x_ready")
        sumsq = sem("sumsq")
        rstd_ready = sem("rstd_ready")
        xn_ready = sem("xn_ready")
        xT_done = sem("xT_done")
        high_ready = sem("high_ready")
        rest_ready = sem("rest_ready")
        gate_high = sem("gate_high")
        gate_split = sem("gate_split")
        w_high = sem("w_high")
        w_split = sem("w_split")
        hT_ready = sem("hT_ready")
        xn_stored = [sem(f"xn_stored_{b}") for b in range(2)]
        proj_done = sem("proj_done")
        gates_abs = sem("gates_abs")
        gates_ln = sem("gates_ln")
        gates_ready = sem("gates_ready")
        gateT_done = sem("gateT_done")
        rows_ready = sem("rows_ready")
        rowsT_done = sem("rowsT_done")
        ucol_ready = sem("ucol_ready")
        em_ready = sem("em_ready")
        rope_parts = sem("rope_parts")
        roped_ready = sem("roped_ready")
        ropeT_done = sem("ropeT_done")
        dqkT_ready = sem("dqkT_ready")
        kv_copied = sem("kv_copied")
        conv_ready = sem("conv_ready")
        qk_ready = sem("qk_ready")
        ogate_ready = sem("ogate_ready")
        att_scores = sem("att_scores")
        att_max = sem("att_max")
        att_exp = sem("att_exp")
        att_probs = sem("att_probs")
        att_T = sem("att_T")
        att_aT_ready = sem("att_aT_ready")
        att_pv = sem("att_pv")
        att_o_copied = sem("att_o_copied")
        head_ss = sem("head_ss")
        head_rstd = sem("head_rstd")
        att_normed = sem("att_normed")
        att_fT = sem("att_fT")
        diff_merged = sem("diff_merged")
        ml_scores = sem("ml_scores")
        ml_exp = sem("ml_exp")
        ml_masked = sem("ml_masked")
        ml_sT = sem("ml_sT")
        ml_num = sem("ml_num")
        ml_normed = sem("ml_normed")
        ml_fT = sem("ml_fT")
        mlstm_merged = sem("mlstm_merged")
        wo_done = sem("wo_done")
        logits_done = sem("logits_done")
        hot_ready = sem("hot_ready")
        top_ready = sem("top_ready")
        soft_exp = sem("soft_exp")
        rank_done = sem("rank_done")
        count_done = sem("count_done")
        counts_ready = sem("counts_ready")
        dest_ready = sem("dest_ready")
        list_stored = sem("list_stored")
        list_loaded = sem("list_loaded")
        halves_loaded = sem("halves_loaded")
        halves_ready = sem("halves_ready")
        slots_ready = sem("slots_ready")
        xg_loaded = [sem(f"xg_loaded_{b}") for b in range(XB)]
        gT_done = sem("gT_done")
        xgT_ready = sem("xgT_ready")
        gu_done = sem("gu_done")
        silu_done = sem("silu_done")
        hid_ready = sem("hid_ready")
        hidT_done = sem("hidT_done")
        hidT_ready = sem("hidT_ready")
        down_done = sem("down_done")
        y_ready = sem("y_ready")
        y_stored = [sem(f"y_stored_{b}") for b in range(2)]
        tok_copied = sem("tok_copied")
        indirect_turn = sem("indirect_turn")
        pair_copied = sem("pair_copied")
        pairs_stored = sem("pairs_stored")
        yp_loaded = [sem(f"yp_loaded_{t}") for t in range(TT)]
        ov = [{n: sem(f"ov{layer}_{n}") for n in (
            "list", "idx", "w", "rows", "T", "xT", "gu", "silu", "hid", "hT", "hTc", "down", "y", "stored",
            "copied")}
            for layer in range(2)]
        c_done = sem("c_done")
        c_copied = sem("c_copied")
        c_evac = sem("c_evac")
        g_final_loaded = sem("g_final_loaded")
        out_ready = sem("out_ready")
        out_stored = sem("out_stored")

        dmas_of_use = [1] * N_MIX0 + [3] * NE + [3] * KT + [1] * 2 + [3] * NE

        def loaded_value(use):
            return 16 * sum(dmas_of_use[u] for u in range(use % RING, use + 1, RING))

        def expert_loaded_value(layer, i, b):
            return loaded_value(EXPERT_USE[layer] + b) + 48 * i

        def wait_slot_free(eng, use):
            u = use - RING
            if u < 0:
                return
            if u < N_MIX0:
                eng.wait_ge(mixer_used, u + 1)
            elif u < MIX_USE[1]:
                eng.wait_ge(down_done, u - N_MIX0 + 1)
            elif u < EXPERT_USE[1]:
                eng.wait_ge(mixer_used, MIX_DONE[1] + u - MIX_USE[1] + 1)
            else:
                eng.wait_ge(down_done, NE + u - EXPERT_USE[1] + 1)

        def expert_loop(eng, body):
            body(0, True, False)
            with eng.Fori(1, NE // RING - 1) as i:
                body(i, False, False)
            body(NE // RING - 1, False, True)

        def weights_of(layer, u):
            n = 2048 if layer == 0 else 3072
            s = (MIX_USE[layer] + u) % RING
            return ring[:, s, 0:n], ring_r[:, s, 0:n], ring_r[:, s, n:2 * n]

        consumed = {}
        for j in range(29):
            consumed[j] = ((gates_abs, 1) if j < 1 else (rope_parts, j) if j < 9 else
                           (kv_copied, j - 8) if j < 17 else (conv_ready, j - 16) if j < 25 else
                           (ogate_ready, j - 24))
        ATT0 = 13
        N_CONST = 1 + 5 * 2 + 7

        block = ctx.enter_context(nc.Block())

        @block.sync
        def _(sp):
            for t in range(TT):
                sp.dma_start(x_sb[:, t, :], x_in[t * P:(t + 1) * P, :]).then_inc(x_loaded[t], 16)

            def load(use, dst, src):
                sp.dma_start(dst, src).then_inc(slot_loaded[use % RING], 16)

            def load_expert(layer, i, b):
                e = i * RING + b
                use = EXPERT_USE[layer] + b
                s = use % RING
                sl = bass.ds(e, 1)
                load(use, ring[:, s, 0:2048], w_gate[layer][sl].rearrange("o (p k) f -> p (o k f)", k=KT))
                load(use, ring[:, s, 2048:4096], w_up[layer][sl].rearrange("o (p k) f -> p (o k f)", k=KT))
                load(use, ring[:, s, 4096:6144].rearrange("p (k n) -> p k n", k=FT),
                     w_down[layer][sl].rearrange("o (k p) n -> p (o k) n", p=P))

            def load_w_out(use, w, c0):
                wait_slot_free(sp, use)
                load(use, ring[:, use % RING, 0:4096].rearrange("p (c n) -> p c n", c=4),
                     w[c0 * P:(c0 + 4) * P, :].rearrange("(c p) n -> p c n", p=P))

            def load_experts(layer):
                base = NE * layer

                def body(i, first, last):
                    for b in range(RING):
                        if first:
                            wait_slot_free(sp, EXPERT_USE[layer] + b)
                        else:
                            sp.wait_ge(down_done, base + i * RING + b - RING + 1)
                        load_expert(layer, i, b)
                expert_loop(sp, body)

            def load_pairs(layer):
                sp.wait_ge(pairs_stored, layer + 1)
                src = pair_dram[layer].rearrange("(k t p) d -> t p k d", k=2, p=P)
                for t in range(TT):
                    sp.dma_start(yp[:, t, :, :], src[t]).then_inc(yp_loaded[t], 16)

            for use in range(N_HALF):
                if use == 2:
                    sp.wait_ge(consts_loaded, 16 * N_CONST)
                wait_slot_free(sp, use)
                c0 = L0_COLS[use // 2] + use % 2 * HC
                load(use, ring[:, use % RING, 0:2048].rearrange("p (k c) -> p k c", k=KT),
                     w_in0[:, c0:c0 + HC].rearrange("(p k) c -> p k c", k=KT))
            load_w_out(N_HALF, w_out0, 0)
            load_w_out(N_HALF + 1, w_out0, 4)
            sp.wait_ge(mixer_used, N_HALF)
            for t in range(TT):
                sp.dma_start(x_sb[:, t, :], x_in[t * P:(t + 1) * P, :]).then_inc(x_loaded[t], 16)
            load_experts(0)
            for ct in range(KT):
                use = MIX_USE[1] + ct
                wait_slot_free(sp, use)
                slot = ring[:, use % RING, 0:3072].rearrange("p (j k c) -> p j k c", j=3, k=KT)
                for j in range(3):
                    load(use, slot[:, j],
                         w_in1[:, j * D + ct * P:j * D + (ct + 1) * P].rearrange("(p k) c -> p k c", k=KT))
                if ct == 1:
                    load_pairs(0)
            load_w_out(MIX_USE[1] + KT, w_out1, 0)
            load_w_out(MIX_USE[1] + KT + 1, w_out1, 4)
            load_experts(1)
            load_pairs(1)
            for t in range(TT):
                sp.wait_ge(out_ready, t + 1)
                sp.dma_start(out[t * P:(t + 1) * P, :], fin[:, t, :]).then_inc(out_stored, 16)
            sp.wait_ge(out_stored, 16 * TT)

        @block.tensor
        def _(pe):
            def transpose_norm(n, t):
                k0 = 4 * n + t
                pe.wait_ge(xn_ready, k0 + 1)
                if k0:
                    pe.wait_ge(hT_ready, k0)
                src = xn[:, t % 2, :].rearrange("s (p k) -> s k p", k=KT)
                for k in range(KT):
                    mm = pe.transpose(ps[:, k // 4, (k % 4) * P:(k % 4 + 1) * P], src[:, k, :], ident[:, :])
                mm.then_inc(xT_done, 1)

            def w_out_tile(layer, t, chunks):
                use = MIX_USE[layer] + (N_HALF if layer == 0 else KT)
                if t == 0:
                    pe.wait_ge(slot_loaded[use % RING], loaded_value(use))
                    pe.wait_ge(slot_loaded[(use + 1) % RING], loaded_value(use + 1))
                if t >= 2:
                    pe.wait_ge(x_ready, 8 * layer + t - 1)
                for n in range(2):
                    bank = 4 + 2 * (t % 2) + n
                    for m, c in enumerate(chunks):
                        w = ring[:, (use + c // 4) % RING, 0:4096].rearrange("p (c n) -> p c n", c=4)
                        lhs = ((mergedM if c < 4 else mergedD)[:, c % 4, t * P:(t + 1) * P] if layer == 0
                               else yT[:, c, t * P:(t + 1) * P])
                        mm = pe.matmul(ps[:, bank, :], lhs, w[:, c % 4, n * 512:(n + 1) * 512],
                                       start=(m == 0), stop=(m == KT - 1))
                mm.then_inc(wo_done, 1)
                if t == TT - 1:
                    pe.wait_ge(wo_done, 4 * layer + TT)
                    pe.sem_inc(mixer_used, 2)

            def router_tile(layer, t):
                pe.wait_ge(hT_ready, 4 * (2 * layer + 1) + t + 1)
                for k in range(KT):
                    mm = pe.matmul(ps[:, 2, t * 36:t * 36 + 36], hT[:, k, t * P:(t + 1) * P],
                                   router_w[:, layer, k, :], start=(k == 0), stop=(k == KT - 1))
                mm.then_inc(logits_done, 1)

            def rank_tile(layer, t):
                pe.wait_ge(hot_ready, 4 * layer + t + 1)
                if t:
                    pe.wait_ge(dest_ready, 4 * layer + t)
                for j in range(t + 1):
                    mm = pe.matmul(ps[:, 3, t * NE:(t + 1) * NE], (before_bf if j == t else ones_bf)[:, :],
                                   hot_bf[:, j, :], start=(j == 0), stop=(j == t))
                mm.then_inc(rank_done, 1)

            def count_experts():
                for j in range(TT):
                    mm = pe.matmul(ps[0:1, 2, 256:256 + NE], ones_bf[:, 0:1], hot_bf[:, j, :],
                                   start=(j == 0), stop=(j == TT - 1))
                mm.then_inc(count_done, 1)

            def w_out_norm_route(layer, chunks):
                n = 2 * layer + 1
                for t in range(TT):
                    w_out_tile(layer, t, chunks)
                    if t >= 2:
                        rank_tile(layer, t - 2)
                    if t >= 1:
                        transpose_norm(n, t - 1)
                        router_tile(layer, t - 1)
                rank_tile(layer, TT - 2)
                transpose_norm(n, TT - 1)
                router_tile(layer, TT - 1)
                rank_tile(layer, TT - 1)
                count_experts()

            def transpose_rows(src, out_sem):
                v = src.rearrange("s (p k) -> s k p", k=KT)
                for k in range(KT):
                    mm = pe.transpose(ps[:, k // 4, (k % 4) * P:(k % 4 + 1) * P], v[:, k, :], ident[:, :])
                mm.then_inc(out_sem, 1)

            def gate_up(w, xt, bank, small, out_sem):
                m = w[:, 0:4096].rearrange("p (g k f) -> p g k f", g=2, k=KT)
                order = ([(f, k) for k in range(KT) for f in range(FT)] if small else
                         [(f, k) for f in range(FT) for k in range(KT)])
                for f, k in order:
                    rhs = m[:, :, k, f * P:(f + 1) * P]
                    o = (ps[f * SMALL:(f + 1) * SMALL, bank, 0:2 * P] if small
                         else ps[:, bank, f * 2 * P:(f + 1) * 2 * P])
                    mm = pe.matmul(o.rearrange("s (g f) -> s g f", g=2), xt[:, k, 0:SMALL if small else CAP],
                                   rhs, start=(k == 0), stop=(k == KT - 1))
                mm.then_inc(out_sem, 1)

            def turn_hidden(hd, bank, small, out_sem):
                for f in range(1 if small else FT):
                    mm = pe.transpose(ps[:, bank, f * P:(f + 1) * P], hd[:, f * P:(f + 1) * P], ident[:, :])
                mm.then_inc(out_sem, 1)

            def down(w, ht, bank, small, out_sem):
                m = w[:, 4096:6144].rearrange("p (k n) -> p k n", k=FT)
                slots = SMALL if small else CAP
                for f in range(FT):
                    for n in range(2):
                        o = ps[n * SMALL:(n + 1) * SMALL, bank, :] if small else ps[:, bank + n, :]
                        mm = pe.matmul(o, ht[:, f * slots:(f + 1) * slots], m[:, f, n * 512:(n + 1) * 512],
                                       start=(f == 0), stop=(f == FT - 1))
                mm.then_inc(out_sem, 1)

            def experts(layer):
                base = NE * layer
                rows_before = 16 * (NE // XB) * layer

                def turn(i, b):
                    g = base + i * RING + b
                    pe.wait_ge(xg_loaded[b], rows_before + 16 * i + 16)
                    if not (isinstance(g, int) and g == 0):
                        pe.wait_ge(xgT_ready, g)
                    transpose_rows(xg[:, b, :], gT_done)

                def tokens_of(i, b):
                    return pe.value_load(cnt_i[0:1, layer, bass.ds(i * RING + b, 1)], min_val=0, max_val=S)

                def sized(count, step):
                    with pe.If(count > SMALL):
                        step(False)
                    with pe.Else():
                        step(True)

                def gate_up_step(i, b, first):
                    g = base + i * RING + b
                    use = EXPERT_USE[layer] + b
                    count = tokens_of(i, b)
                    pe.wait_ge(slot_loaded[use % RING], expert_loaded_value(layer, i, b))
                    pe.wait_ge(xgT_ready, g + 1)
                    if not (first and b < 2 and layer == 0):
                        pe.wait_ge(hidT_ready, g - 1)
                    sized(count, lambda small: gate_up(ring[:, use % RING, :], xgT[:, b % 2], 2 + b % 2, small, gu_done))

                def down_and_turn(i, b, before, first):
                    g = base + i * RING + b
                    if before:
                        down_step(*before, first)
                    count = tokens_of(i, b)
                    pe.wait_ge(hid_ready, g + 1)
                    sized(count, lambda small: turn_hidden(hid[:, b % 2, :], 2 + b % 2, small, hidT_done))

                def down_step(i, b, first):
                    g = base + i * RING + b
                    use = EXPERT_USE[layer] + b
                    count = tokens_of(i, b)
                    pe.wait_ge(hidT_ready, g + 1)
                    if not (first and b < 2 and layer == 0):
                        pe.wait_ge(y_ready, g - 1)
                    sized(count, lambda small: down(ring[:, use % RING, :], hidT[:, b % 2, :], 4 + 2 * (b % 2), small,
                                                   down_done))

                pe.wait_ge(counts_ready, layer + 1)
                turn(0, 0)

                def body(i, first, last):
                    for b in range(RING):
                        gate_up_step(i, b, first)
                        if b < RING - 1:
                            turn(i, b + 1)
                        elif not last:
                            turn(i + 1, 0)
                        if b > 0:
                            down_and_turn(i, b, (i, b - 1), first)
                        else:
                            down_and_turn(i, b, None if first else (i - 1, RING - 1), False)
                expert_loop(pe, body)
                down_step(NE // RING - 1, RING - 1, False)

            def overflow(layer):
                o = ov[layer]
                most = pe.value_load(cnt_max[0:1, layer:layer + 1], min_val=0, max_val=S)
                for r in range(OV_ROUNDS):
                    with pe.If(most > CAP * (r + 1)):
                        with pe.Fori(0, NE) as e:
                            q = e + r * NE + 1
                            pe.wait_ge(o["rows"], 16 * q)
                            transpose_rows(xg[:, 0, :], o["T"])
                            pe.wait_ge(o["xT"], q)
                            pe.wait_ge(o["w"], 48 * q)
                            gate_up(ov_w, xgT[:, 0], 2, False, o["gu"])
                            pe.wait_ge(o["hid"], q)
                            turn_hidden(hid[:, 0, :], 2, False, o["hT"])
                            pe.wait_ge(o["hTc"], q)
                            down(ov_w, hidT[:, 0, :], 4, False, o["down"])

            pe.wait_ge(masks_ready, 3)
            for t in range(TT):
                transpose_norm(0, t)

            pe.wait_ge(gate_split, 1)
            pe.wait_ge(rest_ready, TT)

            def products(out, high, rest, k):
                (lh, rh), (ll, rl) = high, rest
                for n, (a, b) in enumerate(((lh, rh), (lh, rl), (ll, rh))):
                    mm = pe.matmul(out, a, b, start=(k == 0 and n == 0), stop=(k == KT - 1 and n == 2))
                return mm

            def project(j):
                if j >= 2:
                    pe.wait_ge(*consumed[j - 2])
                bank = ps[:, j % 2, :]
                if j == 0:
                    for t in range(TT):
                        for k in range(KT):
                            mm = products(bank[:, t * 8:t * 8 + 8], (hT_h[:, k, t * P:(t + 1) * P], gate_h[:, k, :]),
                                          (hT_rest(0, t)[:, k, :], gate_l[:, k, :]), k)
                    mm.then_inc(proj_done, 1)
                    return
                group, t = (j - 1) // 4, (j - 1) % 4
                pe.wait_ge(w_split, 2 * group + 2)

                def w(half):
                    _, low, high = weights_of(0, 2 * group + half)
                    return (high.rearrange("p (k c) -> p k c", k=KT), low.rearrange("p (k c) -> p k c", k=KT))

                if group in (4, 5):
                    high, low = w(t // 2)
                    c = slice((t % 2) * P, (t % 2 + 1) * P)
                    rests = x_r[:, :, :].rearrange("p t (k s) -> p k t s", k=KT)
                    for k in range(KT):
                        mm = products(bank, (high[:, k, c], hT_h[:, k, :]), (low[:, k, c], rests[:, k]), k)
                else:
                    for half in range(2):
                        high, low = w(half)
                        for k in range(KT):
                            mm = products(bank[:, half * HC:(half + 1) * HC],
                                          (hT_h[:, k, t * P:(t + 1) * P], high[:, k, :]),
                                          (hT_rest(0, t)[:, k, :], low[:, k, :]), k)
                mm.then_inc(proj_done, 1)
                if t == 3:
                    pe.wait_ge(proj_done, j + 1)
                    pe.sem_inc(mixer_used, 2)

            def rope_T(r):
                pe.wait_ge(roped_ready, r + 1)
                if r >= 2:
                    pe.wait_ge(dqkT_ready, r - 1)
                for h in range(H):
                    mm = pe.transpose(ps[:, 2 + r % 2, h * P:(h + 1) * P], roped[:, r % 2, h * P:(h + 1) * P],
                                      ident[:, :])
                mm.then_inc(ropeT_done, 1)

            def gate_rows_T():
                pe.wait_ge(gates_ready, 1)
                for t in range(TT):
                    for j in range(2):
                        mm = pe.transpose(ps[0:H, 6 + j, t * P:(t + 1) * P], gates[:, t, j * H:(j + 1) * H],
                                          ident[:, :])
                mm.then_inc(gateT_done, 1)

            def gate_cols_T():
                pe.wait_ge(rows_ready, 1)
                for n, (j, i) in enumerate(PAIRS):
                    src = row_u[:, j * P:(j + 1) * P] if i == j else row_off[:, OFF[(j, i)], :]
                    mm = pe.transpose(ps[:, 5, n * H:(n + 1) * H], src, ident[0:H, 0:H])
                for i in range(TT):
                    n = len(PAIRS) + i
                    mm = pe.transpose(ps[:, 5, n * H:(n + 1) * H], row_m[:, i * P:(i + 1) * P], ident[0:H, 0:H])
                mm.then_inc(rowsT_done, 1)

            def att_score(a):
                h, i = a // TT, a % TT
                n = (i + 1) * P
                if a == 0:
                    pe.wait_ge(dqkT_ready, 8)
                    pe.wait_ge(ucol_ready, 1)
                else:
                    pe.wait_ge(att_exp, a)
                for c in range(2):
                    q = slice(c * DD, (c + 1) * DD)
                    if i:
                        pe.matmul(ps[:, 4 + c, 0:i * P], dqT[q, h, i * P:n], dkT[q, h, 0:i * P],
                                  start=True, stop=True)
                    pe.matmul(ps[:, 4 + c, i * P:n], dqT[q, h, i * P:n], dkT[q, h, i * P:n],
                              start=True, stop=False)
                    mm = pe.matmul(ps[:, 4 + c, i * P:n], ident_bf[:, :], causal_bf[:, :], start=False, stop=True)
                mm.then_inc(att_scores, 1)

            def att_turn(a):
                i = a % TT
                pe.wait_ge(att_probs, a + 1)
                if a >= 1:
                    pe.wait_ge(att_aT_ready, a)
                for j in range(i + 1):
                    mm = pe.transpose(ps[:, 6, j * P:(j + 1) * P], att_a[:, j * P:(j + 1) * P], ident[:, :])
                mm.then_inc(att_T, 1)

            def att_values(a):
                h, i = a // TT, a % TT
                pe.wait_ge(att_aT_ready, a + 1)
                if i == 0:
                    if h:
                        pe.wait_ge(att_o_copied, h)
                    else:
                        pe.wait_ge(kv_copied, 4)
                for j in range(i + 1):
                    mm = pe.matmul(ps[:, 7, i * P:(i + 1) * P], att_aT[:, j * P:(j + 1) * P],
                                   dv[:, j, h * HD:(h + 1) * HD], start=(j == 0), stop=(j == i))
                mm.then_inc(att_pv, 1)

            def att_finish_T(h):
                pe.wait_ge(att_normed, h + 1)
                if h:
                    pe.wait_ge(diff_merged, h)
                for i in range(TT):
                    mm = pe.transpose(ps[:, 2, i * P:(i + 1) * P], att_o[:, i * P:(i + 1) * P], ident[:, :])
                mm.then_inc(att_fT, 1)

            for j in range(ATT0 + 19):
                if j < 29:
                    project(j)
                if j == 1:
                    gate_rows_T()
                if j == 6:
                    gate_cols_T()
                if 4 <= j < 12:
                    rope_T(j - 4)
                a = j - ATT0
                if 0 <= a - 2 < 16:
                    att_values(a - 2)
                if 0 <= a - 1 < 16:
                    att_turn(a - 1)
                if 0 <= a < 16:
                    att_score(a)
                if a >= 6 and (a - 6) % 4 == 0:
                    att_finish_T((a - 6) // 4)

            def ml_score(h):
                if h == 0:
                    pe.wait_ge(ogate_ready, TT)
                    pe.wait_ge(diff_merged, H)
                    pe.wait_ge(qk_ready, 2 * H)
                else:
                    pe.wait_ge(ml_sT, h)
                    if h >= 2:
                        pe.wait_ge(ml_exp, h - 1)
                pe.matmul(ps[:, h % 2, :], ident[0:H, h:h + 1].to_broadcast([H, P]), negc[:, :], start=True, stop=True)
                for j in range(TT):
                    bank, c0 = ML_BANK[j]
                    mm = pe.matmul(ps[:, bank, c0:c0 + S - j * P], qkT[:, H + h, j * P:(j + 1) * P],
                                   qkT[:, h, j * P:S], start=True, stop=True)
                mm.then_inc(ml_scores, 1)

            def ml_values(h):
                pe.wait_ge(ml_sT, h + 1)
                if h == 0:
                    pe.wait_ge(kv_copied, 8)
                else:
                    pe.wait_ge(ml_normed, h)
                for i in range(TT):
                    c0 = (i % 2) * (HD + 1)
                    for j in range(i + 1):
                        s0 = ML_COL[j] + (i - j) * P
                        mm = pe.matmul(ps[:, 5 + i // 2, c0:c0 + HD + 1], ml_s[:, h % 2, s0:s0 + P],
                                       mv[:, j, h, :], start=(j == 0), stop=(j == i))
                mm.then_inc(ml_num, 1)

            def ml_finish_T(h):
                pe.wait_ge(ml_normed, h + 1)
                if h:
                    pe.wait_ge(mlstm_merged, h)
                for i in range(TT):
                    mm = pe.transpose(ps[:, 7, i * P:(i + 1) * P], ml_h[:, h % 2, i * P:(i + 1) * P], ident[:, :])
                mm.then_inc(ml_fT, 1)

            ml_score(0)
            for h in range(H):
                if h + 1 < H:
                    ml_score(h + 1)
                ml_values(h)
                if h:
                    ml_finish_T(h - 1)
            ml_finish_T(H - 1)

            pe.wait_ge(mlstm_merged, H)
            w_out_norm_route(0, [4, 5, 6, 7, 0, 1, 2, 3])
            experts(0)
            overflow(0)

            for t in range(TT):
                transpose_norm(2, t)
            pe.wait_ge(rest_ready, 2 * TT)
            for ct in range(KT):
                pe.wait_ge(w_split, N_HALF + ct + 1)
                if ct >= 2:
                    pe.wait_ge(c_evac, ct - 1)
                _, low, high = (v.rearrange("p (j k c) -> p j k c", j=3, k=KT) for v in weights_of(1, ct))
                for n, j in enumerate((1, 2, 0)):
                    for k in range(KT):
                        mm = products(ps[:, 2 + 3 * (ct % 2) + n, :], (high[:, j, k, :], hT_h[:, k, :]),
                                      (low[:, j, k, :], rest1[:, k, :]), k)
                    mm.then_inc(c_done, 1)
                pe.wait_ge(c_done, 3 * (ct + 1))
                pe.sem_inc(mixer_used, 1)
            pe.wait_ge(c_evac, KT)
            w_out_norm_route(1, list(range(KT)))
            experts(1)
            overflow(1)

        @block.scalar
        def _(act):
            n_chain = [0]

            def link(ins):
                n_chain[0] += 1
                ins.then_inc(act_chain, 1)
                act.wait_ge(act_chain, n_chain[0])

            def const(dst, src):
                act.dma_start(dst, src).then_inc(consts_loaded, 16)

            for n in range(2):
                act.dma_start(g_mix[:, n, :], norm_mix[n].rearrange("(p k) -> p k", k=KT)).then_inc(first_loaded, 16)
            act.dma_start(gate_w[:, :, :], w_in0[:, C_GATE:C_GATE + 2 * H].rearrange(
                "(p k) c -> p k c", k=KT)).then_inc(first_loaded, 16)

            def square(n, t):
                k0 = 4 * n + t
                if n == 0:
                    act.wait_ge(x_loaded[t], 16)
                else:
                    act.wait_ge(x_ready, 4 * (n - 1) + t + 1)
                if k0:
                    act.wait_ge(sumsq, k0)
                act.activation(junk, x_sb[:, t, :], ACT.Square, accum_out=ss[:, n, t:t + 1]).then_inc(sumsq, 1)

            def store_rows(layer, t):
                act.wait_ge(xn_ready, 4 * (2 * layer + 1) + t + 1)
                act.dma_start(xn_dram[layer][t * P:(t + 1) * P, :], xn[:, t % 2, :]).then_inc(xn_stored[t % 2], 16)

            def norm_route(layer):
                for t in range(TT):
                    square(2 * layer + 1, t)
                    store_rows(layer, t)
                act.wait_ge(top_ready, layer + 1)
                for t in range(TT):
                    act.activation(g_hot[:, t, 0:NG], lg[:, t, 0:NG], ACT.Exp, bias=soft[:, 0, t:t + 1],
                                   accum_out=soft[:, 1, t:t + 1])
                act.activation(soft[:, 3, :], soft[:, 2, :], ACT.Exp).then_inc(soft_exp, 1)

            def silu_step(bank, sil_v, gate_sem, gate_value, out_sem):
                act.wait_ge(gate_sem, gate_value)
                act.activation(sil_v.rearrange("p (f c) -> p f c", f=FT),
                               ps[:, bank, :].rearrange("p (f g c) -> p f g c", f=FT, g=2)[:, :, 0, :],
                               ACT.Silu).then_inc(out_sem, 1)

            def y_copy(bank, y_v, out_sem):
                act.activation(y_v.rearrange("p (n c) -> p n c", n=2), ps[:, bank:bank + 2, :],
                               ACT.Copy).then_inc(out_sem, 1)

            def experts(layer):
                base = NE * layer
                stored_before = 16 * (NE // 2) * layer

                def silu_of(i, b, first):
                    g = base + i * RING + b
                    if not (first and b < 2 and layer == 0):
                        act.wait_ge(hid_ready, g - 1)
                    silu_step(2 + b % 2, sil[:, b % 2, :], gu_done, g + 1, silu_done)

                def y_of(i, b, first):
                    g = base + i * RING + b
                    act.wait_ge(down_done, g + 1)
                    if not (first and b < 2 and layer == 0):
                        act.wait_ge(y_stored[b % 2], stored_before + 32 * i + 16 * ((b - 2) // 2 + 1))
                    y_copy(4 + 2 * (b % 2), y_sb[:, b % 2, :], y_ready)

                def body(i, first, last):
                    for b in range(RING):
                        silu_of(i, b, first)
                        if b > 0:
                            y_of(i, b - 1, first)
                        elif not first:
                            y_of(i - 1, RING - 1, False)
                expert_loop(act, body)
                y_of(NE // RING - 1, RING - 1, False)

            def overflow(layer):
                o = ov[layer]
                act.wait_ge(counts_ready, layer + 1)
                most = act.value_load(cnt_max[0:1, layer:layer + 1], min_val=0, max_val=S)
                for r in range(OV_ROUNDS):
                    with act.If(most > CAP * (r + 1)):
                        with act.Fori(0, NE) as e:
                            q = e + r * NE + 1
                            sl = bass.ds(e, 1)
                            act.dma_start(ov_w[:, 0:2048], w_gate[layer][sl].rearrange(
                                "o (p k) f -> p (o k f)", k=KT)).then_inc(o["w"], 16)
                            act.dma_start(ov_w[:, 2048:4096], w_up[layer][sl].rearrange(
                                "o (p k) f -> p (o k f)", k=KT)).then_inc(o["w"], 16)
                            act.dma_start(ov_w[:, 4096:6144].rearrange("p (k n) -> p k n", k=FT), w_down[layer][
                                sl].rearrange("o (k p) n -> p (o k) n", p=P)).then_inc(o["w"], 16)
                            silu_step(2, sil[:, 0, :], o["gu"], q, o["silu"])
                            act.wait_ge(o["down"], q)
                            y_copy(4, y_sb[:, 0, :], o["y"])

            def high_part(n, t):
                act.wait_ge(hT_ready, 4 * n + t + 1)
                act.activation(hT_h[:, :, t * P:(t + 1) * P], xn[:, t % 2, :].rearrange("p (k s) -> p k s", k=KT),
                               ACT.Copy).then_inc(high_ready, 1)

            def high_weights(layer, u):
                use = MIX_USE[layer] + u
                act.wait_ge(slot_loaded[use % RING], loaded_value(use))
                w, _, high = weights_of(layer, u)
                act.activation(high, w, ACT.Copy).then_inc(w_high, 1)

            for t in range(TT):
                square(0, t)
            act.wait_ge(first_loaded, 16 * 3)
            act.activation(gate_h, gate_w[:, :, :], ACT.Copy).then_inc(gate_high, 1)
            const(gate_b[:, :], gate_bias.partition_broadcast(P))
            for n in range(2):
                const(g_ffn[:, n, :], norm_ffn[n].rearrange("(p k) -> p k", k=KT))
                const(router_w[:, n, :, 0:NG], w_rg[n].rearrange("(p k) c -> p k c", k=KT))
                const(router_w[:, n, :, NG:], w_re[n].rearrange("(p k) c -> p k c", k=KT))
                const(router_b[:, n, 0:NG], b_rg[n].partition_broadcast(P))
                const(router_b[:, n, NG:], b_re[n].partition_broadcast(P))
            const(g_mlstm[:, :], mlstm_norm.rearrange("(p o) -> p o", o=1))
            const(g_diff[:, :], diff_norm.rearrange("(p o) -> p o", o=1))
            const(conv0_w[:, :, :], conv0)
            const(conv1_w[:, :, :], conv1)
            const(lam_sb[:, :, :], lam_vecs.partition_broadcast(P))
            act.dma_start(pos_i[:, :], positions.rearrange("(t p) -> p t", p=P),
                          allow_slow_non_contiguous=True).then_inc(consts_loaded, 16)
            const(invf[:, :], inv_freq.partition_broadcast(P))
            for t in range(TT):
                high_part(0, t)
                if t >= 2:
                    high_weights(0, t - 2)
            act.wait_ge(lam_sum, 1)
            act.activation(lam_c[:, 2:4], lam_c[:, 0:2], ACT.Exp).then_inc(lam_exp, 1)
            act.wait_ge(angles_ready, 1)
            act.activation(sin_t[:, :, :], ang[:, 2, :, :], ACT.Sin)
            act.activation(cos_t[:, :, :], ang[:, 3, :, :], ACT.Sin).then_inc(rope_table, 1)
            act.wait_ge(gates_abs, 1)
            link(act.activation(gate_tmp[:, 1], gate_tmp[:, 0], ACT.Exp, scale=-1.0))
            act.activation(gate_tmp[:, 2], gate_tmp[:, 1], ACT.Ln, bias=1.0).then_inc(gates_ln, 1)

            def rope_copy(r):
                act.wait_ge(ropeT_done, r + 1)
                dst = (dqT if r < 4 else dkT)[:, :, (r % 4) * P:(r % 4 + 1) * P]
                act.activation(dst, ps[:, 2 + r % 2, :].rearrange("p (h s) -> p h s", h=H),
                               ACT.Copy).then_inc(dqkT_ready, 1)

            def job(j):
                if 9 <= j < 17:
                    act.wait_ge(proj_done, j + 1)
                    t = (j - 1) % 4
                    if j < 13:
                        act.activation(dv[:, t, :], ps[:, j % 2, :], ACT.Copy).then_inc(kv_copied, 1)
                    else:
                        act.activation(mv[:, t, :, 0:HD], ps[:, j % 2, :].rearrange("p (h e) -> p h e", h=H),
                                       ACT.Copy).then_inc(kv_copied, 1)
                elif 17 <= j < 25:
                    act.wait_ge(conv_ready, j - 16)
                    act.activation(qkT[:, j - 17, :], conv_acc[:, j % 2, :], ACT.Silu).then_inc(qk_ready, 1)
                elif 25 <= j < 29:
                    act.wait_ge(proj_done, j + 1)
                    act.activation(o_gate[:, j - 25, :], ps[:, j % 2, :], ACT.Sigmoid).then_inc(ogate_ready, 1)

            def att_copy_T(a):
                n = (a % TT + 1) * P
                act.wait_ge(att_T, a + 1)
                if a >= 1:
                    act.wait_ge(att_pv, a)
                act.activation(att_aT[:, 0:n], ps[:, 6, 0:n], ACT.Copy).then_inc(att_aT_ready, 1)

            def att_exps(a):
                n = (a % TT + 1) * P
                act.wait_ge(att_max, a + 1)
                if a >= 1:
                    act.wait_ge(att_probs, a)
                for c in range(2):
                    ins = act.activation(att_e[:, c, 0:n], ps[:, 4 + c, 0:n], ACT.Exp, bias=att_s[:, 2 + c:3 + c],
                                         scale=DD ** -0.5, accum_out=att_s[:, 4 + c:5 + c])
                ins.then_inc(att_exp, 1)

            for j in range(ATT0 + 19):
                if j % 4 in (3, 0) and 0 < j < 25:
                    high_weights(0, 2 * ((j - 1) // 4) + 2 + (j % 4 == 0))
                job(j)
                if 4 <= j < 12:
                    rope_copy(j - 4)
                if j == 8:
                    act.wait_ge(ucol_ready, 1)
                    act.activation(em[:, :, :], ucol[:, len(PAIRS):, :], ACT.Exp).then_inc(em_ready, 1)
                a = j - ATT0
                if a - 2 >= 0 and (a - 2) % 4 == 3 and a - 2 < 16:
                    h = (a - 2) // 4
                    act.wait_ge(att_pv, 4 * h + 4)
                    if h:
                        act.wait_ge(att_fT, h)
                    act.activation(att_o[:, :], ps[:, 7, :], ACT.Copy).then_inc(att_o_copied, 1)
                if 0 <= a - 1 < 16:
                    att_copy_T(a - 1)
                if 0 <= a < 16:
                    att_exps(a)
                if a >= 6 and (a - 6) % 4 == 0:
                    h = (a - 6) // 4
                    act.wait_ge(att_fT, h + 1)
                    act.activation(mergedD[:, h, :], ps[:, 2, :], ACT.Copy, scale=g_diff_s[:, 0:1]).then_inc(
                        diff_merged, 1)

            def ml_weights(h):
                act.wait_ge(ml_scores, h + 1)
                if h == 0:
                    act.wait_ge(att_pv, 16)
                    act.wait_ge(ucol_ready, 1)
                if h >= 2:
                    act.wait_ge(ml_sT, h - 1)
                for n, (j, i) in enumerate(PAIRS):
                    c0 = ML_COL[j] + (i - j) * P
                    ins = act.activation(ml_w[:, h % 2, c0:c0 + P], ps[:, h % 2, i * P:(i + 1) * P], ACT.Exp,
                                         bias=ucol[:, n, h:h + 1])
                ins.then_inc(ml_exp, 1)

            def ml_merge(h):
                act.wait_ge(ml_fT, h + 1)
                if h == 0:
                    act.wait_ge(mixer_used, N_HALF)
                act.activation(mergedM[:, h, :], ps[:, 7, :], ACT.Copy, scale=g_mlstm[:, 0:1]).then_inc(
                    mlstm_merged, 1)

            ml_weights(0)
            for h in range(H):
                if h + 1 < H:
                    ml_weights(h + 1)
                if h:
                    ml_merge(h - 1)
            ml_merge(H - 1)
            norm_route(0)
            experts(0)
            overflow(0)

            for u in range(2):
                high_weights(1, u)
            for t in range(TT):
                square(2, t)
                if t:
                    high_part(2, t - 1)
            high_part(2, TT - 1)
            for ct in range(KT):
                act.wait_ge(c_done, 3 * ct + 1)
                if ct >= 2:
                    act.wait_ge(c_evac, ct - 1)
                act.activation(c_sb[:, ct % 2, :], ps[:, 2 + 3 * (ct % 2), :], ACT.Copy).then_inc(c_copied, 1)
                if ct + 2 < KT:
                    high_weights(1, ct + 2)
            norm_route(1)
            experts(1)
            overflow(1)
            act.dma_start(g_final, final_norm.partition_broadcast(P)).then_inc(g_final_loaded, 16)
            for t in range(TT):
                square(4, t)

        @block.vector
        def _(dve):
            n_chain = [0]

            def link(ins):
                n_chain[0] += 1
                ins.then_inc(dve_chain, 1)
                dve.wait_ge(dve_chain, n_chain[0])

            def normalise(n, t):
                k0 = 4 * n + t
                dve.wait_ge(rstd_ready, k0 + 1)
                if k0 >= 2:
                    dve.wait_ge(xT_done, k0 - 1)
                if n in (0, 2) and t >= 2:
                    dve.wait_ge(rest_ready, 4 * (n // 2) + t - 1)
                if n in (1, 3) and t >= 2:
                    dve.wait_ge(xn_stored[t % 2], 16 * (n // 2 * 2 + 1))
                dve.tensor_scalar(xn[:, t % 2, :], x_sb[:, t, :], rstd[:, n, t:t + 1], None,
                                  ALU.mult).then_inc(xn_ready, 1)

            def gain_T(n, t):
                k0 = 4 * n + t
                dve.wait_ge(xT_done, k0 + 1)
                g = g_ffn[:, n // 2, :].unsqueeze(2).to_broadcast([P, KT, P])
                dve.tensor_tensor(hT[:, :, t * P:(t + 1) * P],
                                  ps[:, 0:2, :].rearrange("p b (k s) -> p (b k) s", s=P), g,
                                  ALU.mult).then_inc(hT_ready, 1)

            def turned(n, t):
                dve.wait_ge(xT_done, 4 * n + t + 1)
                g = g_mix[:, n // 2, :].unsqueeze(2).to_broadcast([P, KT, P])
                dve.tensor_tensor(xn[:, t % 2, :].rearrange("p (k s) -> p k s", k=KT),
                                  ps[:, 0:2, :].rearrange("p b (k s) -> p (b k) s", s=P), g,
                                  ALU.mult).then_inc(hT_ready, 1)

            def rest_part(n, t):
                dve.wait_ge(high_ready, 4 * (n // 2) + t + 1)
                dve.tensor_tensor(hT_rest(n, t), xn[:, t % 2, :].rearrange("p (k s) -> p k s", k=KT),
                                  hT_h[:, :, t * P:(t + 1) * P], ALU.subtract).then_inc(rest_ready, 1)

            def rest_weights(layer, u):
                dve.wait_ge(w_high, (0 if layer == 0 else N_HALF) + u + 1)
                w, low, high = weights_of(layer, u)
                dve.tensor_tensor(low, w, high, ALU.subtract).then_inc(w_split, 1)

            def norm_split(n, before):
                for t in range(TT):
                    before(t)
                    if t >= 2:
                        rest_part(n, t - 2)
                    normalise(n, t)
                    if t:
                        turned(n, t - 1)
                turned(n, TT - 1)
                rest_part(n, TT - 2)
                rest_part(n, TT - 1)

            def residual(layer, t):
                dve.wait_ge(wo_done, 4 * layer + t + 1)
                if layer == 0:
                    dve.wait_ge(x_loaded[t], 32)
                b = 4 + 2 * (t % 2)
                dve.tensor_tensor(x_sb[:, t, :].rearrange("p (n c) -> p n c", n=2), ps[:, b:b + 2, :],
                                  x_sb[:, t, :].rearrange("p (n c) -> p n c", n=2), ALU.add).then_inc(x_ready, 1)

            def route(layer, t):
                dve.wait_ge(logits_done, 4 * layer + t + 1)
                dve.tensor_tensor(lg[:, t, 0:NG], ps[:, 2, t * 36:t * 36 + NG], router_b[:, layer, 0:NG], ALU.add)
                link(dve.tensor_tensor(lg[:, t, 8:8 + NE], ps[:, 2, t * 36 + NG:t * 36 + 36],
                                       router_b[:, layer, NG:], ALU.add))
                link(dve.max(g8[:, t, :], lg[:, t, 0:8]))
                link(dve.max_index(gi8[:, t, :], g8[:, t, :], lg[:, t, 0:8]))
                link(dve.tensor_copy(g_f[:, t, 0:1], gi8[:, t, 0:1]))
                dve.tensor_scalar(g_f[:, t, 1:2], g_f[:, t, 0:1], float(EG), None, ALU.mult)
                link(dve.tensor_scalar(g_hot[:, t, 0:NG], iota32[:, 0:NG], g_f[:, t, 0:1], None, ALU.is_equal))
                masked = g_hot[:, t, NG:].rearrange("p (e g) -> p e g", g=NG)
                link(dve.tensor_tensor(masked, lg[:, t, 8:].rearrange("p (g e) -> p e g", g=NG),
                                       g_hot[:, t, 0:NG].unsqueeze(1).to_broadcast([P, EG, NG]), ALU.mult))
                link(dve.tensor_reduce(esel[:, t, :], masked, AX_X, ALU.add))
                link(dve.max(e8[:, t, :], esel[:, t, :]))
                link(dve.max_index(ei8[:, t, :], e8[:, t, :], esel[:, t, :]))
                link(dve.tensor_copy(ei_f[:, t, :], ei8[:, t, 0:2]))
                link(dve.tensor_scalar(eid[:, t, :], ei_f[:, t, :], g_f[:, t, 1:2], None, ALU.add))
                dve.tensor_scalar(hot[:, t, 0, :], iota32[:, :], eid[:, t, 0:1], None, ALU.is_equal)
                link(dve.tensor_scalar(hot[:, t, 1, :], iota32[:, :], eid[:, t, 1:2], None, ALU.is_equal))
                dve.tensor_tensor(hot_bf[:, t, :], hot[:, t, 0, :], hot[:, t, 1, :], ALU.add).then_inc(hot_ready, 1)

            def place(layer, t):
                dve.wait_ge(rank_done, 4 * layer + t + 1)
                link(dve.tensor_tensor(rank_t[:, t], hot[:, t],
                                       ps[:, 3, t * NE:(t + 1) * NE].unsqueeze(1).to_broadcast([P, 2, NE]), ALU.mult))
                link(dve.tensor_reduce(rank[:, t, :], rank_t[:, t], AX_X, ALU.add))
                dve.scalar_tensor_tensor(out=dest[:, t, :], in0=rank[:, t, :], scalar=float(NE), in1=eid[:, t, :],
                                         op0=ALU.mult, op1=ALU.add).then_inc(dest_ready, 1)

            def w_out_norm_route(layer):
                n = 2 * layer + 1
                for t in range(TT):
                    residual(layer, t)
                    normalise(n, t)
                    if t >= 1:
                        gain_T(n, t - 1)
                        route(layer, t - 1)
                    if t >= 2:
                        place(layer, t - 2)
                gain_T(n, TT - 1)
                place(layer, TT - 2)
                route(layer, TT - 1)
                place(layer, TT - 1)
                dve.wait_ge(count_done, layer + 1)
                link(dve.tensor_copy(cnt_f[:, :], ps[0:1, 2, 256:256 + NE]))
                dve.tensor_copy(cnt_i[:, layer, :], cnt_f[:, :])
                link(dve.tensor_reduce(cnt_max[:, layer:layer + 1], cnt_f[:, :], AX_X, ALU.max))
                dve.engine_nop().then_inc(counts_ready, 1)
                dve.tensor_scalar(soft[:, 0, :], g8[:, :, 0], -1.0, None, ALU.mult)
                dve.tensor_tensor(soft[:, 2, :], e8[:, :, 1], e8[:, :, 0], ALU.subtract).then_inc(top_ready, 1)
                dve.wait_ge(list_loaded, 16 * (layer + 1))
                slot_tokens(slot_f[:, :], slot_pair[:, layer, :], slot_tok[:, layer, :])
                dve.engine_nop().then_inc(slots_ready, 1)
                dve.wait_ge(halves_loaded, 32 * (layer + 1))
                dve.tensor_scalar(slot_half[:, layer, :], slot_half[:, layer, :], 2.0, half_of[:, 0:1], ALU.mult,
                                  ALU.add).then_inc(halves_ready, 1)
                dve.wait_ge(soft_exp, layer + 1)
                link(dve.tensor_scalar(soft[:, 4, :], soft[:, 3, :], 1.0, None, ALU.add))
                link(dve.tensor_tensor(soft[:, 5, :], soft[:, 4, :], soft[:, 1, :], ALU.mult))
                link(dve.reciprocal(pair_w[:, layer, 0, :], soft[:, 5, :]))
                link(dve.tensor_tensor(pair_w[:, layer, 1, :], pair_w[:, layer, 0, :], soft[:, 3, :], ALU.mult))

            def slot_tokens(tmp, pairs, toks):
                link(dve.tensor_scalar(tmp, pairs, float(S), -float(S), ALU.is_ge, ALU.mult))
                link(dve.tensor_tensor(toks, tmp, pairs, ALU.add))

            def gathered_gain(layer, dst, out_sem):
                g = g_ffn[:, layer, :].unsqueeze(2).to_broadcast([P, KT, P])
                dve.tensor_tensor(dst, ps[:, 0:2, :].rearrange("p b (k s) -> p (b k) s", s=P), g,
                                  ALU.mult).then_inc(out_sem, 1)

            def hidden(bank, sil_v, hid_v, out_sem):
                dve.tensor_tensor(hid_v.rearrange("p (f c) -> p f c", f=FT), sil_v.rearrange("p (f c) -> p f c", f=FT),
                                  ps[:, bank, :].rearrange("p (f g c) -> p f g c", f=FT, g=2)[:, :, 1, :],
                                  ALU.mult).then_inc(out_sem, 1)

            def hidden_T(bank, ht_v, out_sem):
                dve.tensor_copy(ht_v, ps[:, bank, 0:2 * P]).then_inc(out_sem, 1)

            def experts(layer):
                base = NE * layer

                def gain_of(i, b, early):
                    g = base + i * RING + b
                    dve.wait_ge(gT_done, g + 1)
                    if not (early and layer == 0):
                        dve.wait_ge(gu_done, g - 1)
                    gathered_gain(layer, xgT[:, b % 2], xgT_ready)

                def hidden_of(i, b, first):
                    g = base + i * RING + b
                    dve.wait_ge(silu_done, g + 1)
                    if not (first and b < 2 and layer == 0):
                        dve.wait_ge(hidT_done, g - 1)
                    hidden(2 + b % 2, sil[:, b % 2, :], hid[:, b % 2, :], hid_ready)

                def hidden_T_of(i, b, first):
                    g = base + i * RING + b
                    dve.wait_ge(hidT_done, g + 1)
                    if not (first and b < 2 and layer == 0):
                        dve.wait_ge(down_done, g - 1)
                    hidden_T(2 + b % 2, hidT[:, b % 2, :], hidT_ready)

                gain_of(0, 0, True)

                def body(i, first, last):
                    for b in range(RING):
                        hidden_of(i, b, first)
                        if b < RING - 1:
                            gain_of(i, b + 1, first and b == 0)
                        elif not last:
                            gain_of(i + 1, 0, False)
                        hidden_T_of(i, b, first)
                expert_loop(dve, body)

            def overflow(layer):
                o = ov[layer]
                most = dve.value_load(cnt_max[0:1, layer:layer + 1], min_val=0, max_val=S)
                for r in range(OV_ROUNDS):
                    with dve.If(most > CAP * (r + 1)):
                        dve.wait_ge(o["list"], 16 * (r + 1))
                        dve.tensor_scalar(ov_f[:, :], ov_pair[:, :], float(S), -float(S), ALU.is_ge,
                                          ALU.mult).then_inc(o["idx"], 1)
                        dve.wait_ge(o["idx"], 2 * r + 1)
                        dve.tensor_tensor(ov_tok[:, :], ov_f[:, :], ov_pair[:, :], ALU.add).then_inc(o["idx"], 1)
                        with dve.Fori(0, NE) as e:
                            q = e + r * NE + 1
                            dve.wait_ge(o["T"], q)
                            gathered_gain(layer, xgT[:, 0], o["xT"])
                            dve.wait_ge(o["silu"], q)
                            hidden(2, sil[:, 0, :], hid[:, 0, :], o["hid"])
                            dve.wait_ge(o["hT"], q)
                            hidden_T(2, hidT[:, 0, :], o["hTc"])

            def combine(layer, t):
                dve.wait_ge(yp_loaded[t], 16 * (layer + 1))
                for k in range(2):
                    ins = dve.scalar_tensor_tensor(out=x_sb[:, t, :], in0=yp[:, t, k, :],
                                                   scalar=pair_w[:, layer, k, t:t + 1], in1=x_sb[:, t, :],
                                                   op0=ALU.mult, op1=ALU.add)
                    if k == 0:
                        link(ins)
                ins.then_inc(x_ready, 1)

            dve.memset(neg_half[:, :], -0.5)
            dve.memset(zeros4[:, :], 0.0)
            dve.memset(half_of[0:SMALL, :], 0.0)
            dve.memset(half_of[SMALL:P, :], 1.0)
            dve.memset(lg[:, :, 4:8], NEG)
            dve.memset(m_state[:, 0:1], 0.0)
            dve.memset(mv[:, :, :, HD:HD + 1], 1.0)
            dve.wait_ge(masks_ready, 3)
            link(dve.tensor_copy(iota32[:, :], iota32_i[:, :]))
            link(dve.tensor_copy(ident_bf[:, :], ident[:, :]))
            dve.engine_nop().then_inc(consts_ready, 1)

            def before_tile(t):
                if t == 1:
                    dve.wait_ge(gate_high, 1)
                    dve.tensor_tensor(gate_l, gate_w[:, :, :], gate_h, ALU.subtract).then_inc(gate_split, 1)

            norm_split(0, before_tile)
            for u in range(2):
                rest_weights(0, u)
            dve.wait_ge(consts_loaded, 16 * N_CONST)

            link(dve.tensor_tensor(lam_t[:, :, :], lam_sb[:, 0::2, :], lam_sb[:, 1::2, :], ALU.mult))
            dve.tensor_reduce(lam_c[:, 0:2], lam_t[:, :, :], AX_X, ALU.add).then_inc(lam_sum, 1)
            dve.tensor_scalar(g_diff_s[:, :], g_diff[:, :], 1.0 - LAM_INIT, None, ALU.mult)

            link(dve.tensor_copy(pos_f[:, :], pos_i[:, :]))
            for t in range(TT):
                ins = dve.tensor_scalar(ang[:, 0, t, :], invf[:, :], pos_f[:, t:t + 1], None, ALU.mult)
            link(ins)
            link(dve.tensor_scalar(ang[:, 1], ang[:, 0], 0.15915494309189535, MAGIC, ALU.mult, ALU.add))
            link(dve.tensor_scalar(ang[:, 1], ang[:, 1], MAGIC, None, ALU.subtract))
            for c in TWO_PI:
                link(dve.scalar_tensor_tensor(out=ang[:, 0], in0=ang[:, 1], scalar=-c, in1=ang[:, 0],
                                              op0=ALU.mult, op1=ALU.add))
            link(dve.tensor_scalar(ang[:, 2], ang[:, 0], PI_IN, -PI_IN, ALU.min, ALU.max))
            link(dve.tensor_scalar(ang[:, 0], ang[:, 0], 1.5707963267948966, None, ALU.add))
            link(dve.tensor_scalar(ang[:, 1], ang[:, 0], PI_IN, -6.283185307179586, ALU.is_gt, ALU.mult))
            link(dve.tensor_tensor(ang[:, 3], ang[:, 0], ang[:, 1], ALU.add))
            dve.tensor_scalar(ang[:, 3], ang[:, 3], PI_IN, -PI_IN, ALU.min, ALU.max).then_inc(angles_ready, 1)
            dve.wait_ge(lam_exp, 1)
            link(dve.scalar_tensor_tensor(out=lam_c[:, 4:5], in0=lam_c[:, 3:4], scalar=-LAM_INIT, in1=lam_c[:, 2:3],
                                          op0=ALU.add, op1=ALU.subtract))

            def gates_a():
                dve.wait_ge(proj_done, 1)
                link(dve.tensor_tensor(gates[:, :, :], ps[:, 0, 0:TT * 8].rearrange("p (t c) -> p t c", t=TT),
                                       gate_b[:, :].unsqueeze(1).to_broadcast([P, TT, 2 * H]), ALU.add))
                link(dve.tensor_scalar(gate_tmp[:, 1], gates[:, :, H:], -1.0, None, ALU.mult))
                dve.tensor_tensor(gate_tmp[:, 0], gates[:, :, H:], gate_tmp[:, 1], ALU.max).then_inc(gates_abs, 1)

            def gates_b():
                dve.wait_ge(gates_ln, 1)
                dve.scalar_tensor_tensor(out=gates[:, :, H:], in0=gates[:, :, H:], scalar=0.0, in1=gate_tmp[:, 2],
                                         op0=ALU.min, op1=ALU.subtract).then_inc(gates_ready, 1)

            def gate_rows():
                dve.wait_ge(gateT_done, 1)
                for i in range(TT):
                    q = slice(i * P, (i + 1) * P)
                    ins = dve.tensor_tensor_scan(row_b[:, q], ps[0:H, 7, q], zeros4[:, :], 0.0, ALU.add, ALU.add)
                link(ins)
                link(dve.tensor_tensor(row_u[:, :], ps[0:H, 6, :], row_b[:, :], ALU.subtract))
                for i in range(TT):
                    q = slice(i * P, (i + 1) * P)
                    end = (i + 1) * P - 1
                    link(dve.tensor_tensor_scan(row_c[:, q], row_u[:, q], row_u[:, q], m_state[:, i:i + 1],
                                                ALU.max, ALU.max))
                    link(dve.tensor_tensor(m_state[:, i + 1:i + 2], row_c[:, end:end + 1], row_b[:, end:end + 1],
                                           ALU.add))
                dve.tensor_scalar(negc[:, :], row_c[:, :], -1.0, None, ALU.mult)
                link(dve.scalar_tensor_tensor(out=row_m[:, :], in0=row_b[:, :], scalar=-1.0, in1=row_c[:, :],
                                              op0=ALU.mult, op1=ALU.subtract))
                for (j, i), n in OFF.items():
                    prev = row_u[:, j * P:(j + 1) * P] if i == j + 1 else row_off[:, OFF[(j, i - 1)], :]
                    link(dve.tensor_scalar(row_off[:, n, :], prev, row_b[:, i * P - 1:i * P], None, ALU.add))
                dve.engine_nop().then_inc(rows_ready, 1)

            def rope(r):
                j = r + 1
                t = r % 4
                if r == 0:
                    dve.wait_ge(rope_table, 1)
                dve.wait_ge(proj_done, j + 1)
                if r >= 2:
                    dve.wait_ge(roped_ready, r - 1)
                src = ps[:, j % 2, :].rearrange("p (g e) -> p g e", e=HALF)
                for tab, dst in ((cos_t, rope_a), (sin_t, rope_b)):
                    ins = dve.tensor_tensor(dst[:, r % 2, :].rearrange("p (g e) -> p g e", e=HALF), src,
                                            tab[:, t, :].unsqueeze(1).to_broadcast([P, 2 * 2 * H, HALF]), ALU.mult)
                ins.then_inc(rope_parts, 1)

            def conv(j):
                ch = j - 17
                dve.wait_ge(proj_done, j + 1)
                if ch >= 2:
                    dve.wait_ge(qk_ready, ch - 1)
                acc = conv_acc[:, j % 2, :]
                src = ps[:, j % 2, :]
                link(dve.tensor_scalar(acc, src, conv0_w[:, ch, 3:4], None, ALU.mult))
                for s in range(1, 4):
                    ins = dve.scalar_tensor_tensor(out=acc[:, s:S], in0=src[:, 0:S - s],
                                                   scalar=conv0_w[:, ch, 3 - s:4 - s], in1=acc[:, s:S],
                                                   op0=ALU.mult, op1=ALU.add)
                    if s < 3:
                        link(ins)
                ins.then_inc(conv_ready, 1)

            def att_maxima(a):
                n = (a % TT + 1) * P
                dve.wait_ge(att_scores, a + 1)
                link(dve.tensor_reduce(att_s[:, 0:2], ps[:, 4:6, 0:n], AX_X, ALU.max))
                dve.tensor_scalar(att_s[:, 2:4], att_s[:, 0:2], -(DD ** -0.5), None, ALU.mult).then_inc(att_max, 1)

            def att_combine(a):
                n = (a % TT + 1) * P
                dve.wait_ge(att_exp, a + 1)
                if a >= 1:
                    dve.wait_ge(att_T, a)
                link(dve.reciprocal(att_s[:, 6:8], att_s[:, 4:6]))
                link(dve.tensor_tensor(att_s[:, 8:9], att_s[:, 7:8], lam_c[:, 4:5], ALU.mult))
                link(dve.tensor_scalar(att_e[:, 1, 0:n], att_e[:, 1, 0:n], att_s[:, 8:9], None, ALU.mult))
                dve.scalar_tensor_tensor(out=att_a[:, 0:n], in0=att_e[:, 0, 0:n], scalar=att_s[:, 6:7],
                                         in1=att_e[:, 1, 0:n], op0=ALU.mult, op1=ALU.add).then_inc(att_probs, 1)

            def att_norm(h):
                dve.wait_ge(att_o_copied, h + 1)
                link(dve.tensor_tensor(att_q[:, :], att_o[:, :], att_o[:, :], ALU.mult))
                dve.tensor_reduce(hn[:, h, :], att_q[:, :].rearrange("p (i e) -> p i e", e=HD), AX_X,
                                  ALU.add).then_inc(head_ss, 1)
                dve.wait_ge(head_rstd, h + 1)
                v = att_o[:, :].rearrange("p (i e) -> p i e", e=HD)
                dve.tensor_tensor(v, v, hn_r[:, h, :].unsqueeze(2).to_broadcast([P, TT, HD]),
                                  ALU.mult).then_inc(att_normed, 1)

            for j in range(ATT0 + 19):
                if j % 4 in (3, 0) and 0 < j < 25:
                    rest_weights(0, 2 * ((j - 1) // 4) + 2 + (j % 4 == 0))
                if j == 0:
                    gates_a()
                elif j < 9:
                    rope(j - 1)
                elif 17 <= j < 25:
                    conv(j)
                if j == 0:
                    gates_b()
                if j == 2:
                    gate_rows()
                if j == 7:
                    dve.wait_ge(rowsT_done, 1)
                    dve.tensor_copy(ucol[:, :, :], ps[:, 5, 0:(len(PAIRS) + TT) * H].rearrange(
                        "p (n h) -> p n h", h=H)).then_inc(ucol_ready, 1)
                a = j - ATT0
                if 0 <= a < 16:
                    att_maxima(a)
                    att_combine(a)
                if a >= 5 and (a - 5) % 4 == 0 and (a - 5) // 4 < H:
                    att_norm((a - 5) // 4)

            def ml_weighted(h):
                dve.wait_ge(ml_masked, 4 * h + 4)
                if h >= 2:
                    dve.wait_ge(ml_num, h - 1)
                for j in range(TT):
                    bank, c0 = ML_BANK[j]
                    w = S - j * P
                    ins = dve.scalar_tensor_tensor(out=ml_s[:, h % 2, ML_COL[j]:ML_COL[j] + w],
                                                   in0=ps[:, bank, c0:c0 + w], scalar=HD ** -0.5,
                                                   in1=ml_w[:, h % 2, ML_COL[j]:ML_COL[j] + w],
                                                   op0=ALU.mult, op1=ALU.mult)
                ins.then_inc(ml_sT, 1)

            def ml_normalise(h):
                dve.wait_ge(ml_num, h + 1)
                if h == 0:
                    dve.wait_ge(em_ready, 1)
                if h >= 2:
                    dve.wait_ge(ml_fT, h - 1)
                nd = ps[:, 5:7, 0:2 * (HD + 1)].rearrange("p b (i e) -> p b i e", e=HD + 1)
                two = "p (b i) -> p b i"
                link(dve.tensor_copy(den_t[:, 0, :].rearrange(two, b=2), nd[:, :, :, HD]))
                link(dve.tensor_scalar(den_t[:, 1, :], den_t[:, 0, :], -1.0, None, ALU.mult))
                link(dve.tensor_tensor(den_t[:, 2, :], den_t[:, 0, :], den_t[:, 1, :], ALU.max))
                link(dve.tensor_tensor(den_t[:, 1, :], den_t[:, 2, :], em[:, :, h], ALU.max))
                link(dve.reciprocal(den_t[:, 3, :], den_t[:, 1, :]))
                hm = ml_h[:, h % 2, :]
                for b in range(2):
                    ins = dve.tensor_tensor(hm[:, b * 256:(b + 1) * 256].rearrange("p (i e) -> p i e", e=HD),
                                            nd[:, b, :, 0:HD],
                                            den_t[:, 3, 2 * b:2 * b + 2].unsqueeze(2).to_broadcast([P, 2, HD]),
                                            ALU.mult)
                link(ins)
                link(dve.tensor_tensor(ml_q[:, :], hm, hm, ALU.mult))
                dve.tensor_reduce(hn[:, H + h, :], ml_q[:, :].rearrange("p (i e) -> p i e", e=HD), AX_X,
                                  ALU.add).then_inc(head_ss, 1)
                dve.wait_ge(head_rstd, H + h + 1)
                for i in range(TT):
                    q = slice(i * P, (i + 1) * P)
                    ins = dve.scalar_tensor_tensor(out=hm[:, q], in0=hm[:, q], scalar=hn_r[:, H + h, i:i + 1],
                                                   in1=o_gate[:, i, h * HD:(h + 1) * HD],
                                                   op0=ALU.mult, op1=ALU.mult)
                ins.then_inc(ml_normed, 1)

            ml_weighted(0)
            for h in range(H):
                if h + 1 < H:
                    ml_weighted(h + 1)
                if h == 0:
                    dve.wait_ge(ogate_ready, TT)
                ml_normalise(h)

            w_out_norm_route(0)
            experts(0)
            overflow(0)

            for u in range(2):
                rest_weights(1, u)
            norm_split(2, lambda t: combine(0, t))
            for ct in range(KT):
                b = 2 + 3 * (ct % 2)
                dve.wait_ge(c_copied, ct + 1)
                dve.wait_ge(c_done, 3 * ct + 2)
                v, acc = cx[:, ct % 2, :], c_acc[:, ct % 2, :]
                link(dve.tensor_tensor(v, c_sb[:, ct % 2, :], ps[:, b + 1, :], ALU.mult))
                link(dve.tensor_scalar(acc, v, conv1_w[:, ct, 2:3], None, ALU.mult))
                for s in range(1, 3):
                    link(dve.scalar_tensor_tensor(out=acc[:, s:S], in0=v[:, 0:S - s],
                                                  scalar=conv1_w[:, ct, 2 - s:3 - s], in1=acc[:, s:S],
                                                  op0=ALU.mult, op1=ALU.add))
                dve.wait_ge(c_done, 3 * ct + 3)
                dve.tensor_tensor(yT[:, ct, :], acc, ps[:, b + 2, :], ALU.mult).then_inc(c_evac, 1)
                if ct + 2 < KT:
                    rest_weights(1, ct + 2)
            w_out_norm_route(1)
            experts(1)
            overflow(1)

            dve.wait_ge(g_final_loaded, 16)
            for t in range(TT):
                combine(1, t)
                dve.wait_ge(rstd_ready, 16 + t + 1)
                dve.scalar_tensor_tensor(out=fin[:, t, :], in0=x_sb[:, t, :], scalar=rstd[:, 4, t:t + 1],
                                         in1=g_final, op0=ALU.mult, op1=ALU.mult).then_inc(out_ready, 1)

        @block.gpsimd
        def _(pool):
            n_chain = [0]

            def link(ins):
                n_chain[0] += 1
                ins.then_inc(pool_chain, 1)
                pool.wait_ge(pool_chain, n_chain[0])

            def root(n, t):
                pool.wait_ge(sumsq, 4 * n + t + 1)
                link(pool.tensor_scalar(ms[:, n, t:t + 1], ss[:, n, t:t + 1], 1.0 / D, EPS, ALU.mult, ALU.add))
                pool.tensor_tensor(rstd[:, n, t:t + 1], ms[:, n, t:t + 1], neg_half[:, 0:1],
                                   ALU.pow).then_inc(rstd_ready, 1)

            def head_root(m):
                pool.wait_ge(head_ss, m + 1)
                link(pool.tensor_scalar(hn_ms[:, m, :], hn[:, m, :], 1.0 / HD, EPS, ALU.mult, ALU.add))
                pool.tensor_tensor(hn_r[:, m, :], hn_ms[:, m, :], neg_half[:, :], ALU.pow).then_inc(head_rstd, 1)

            pool.memset(ident[:, :], 0.0)
            pool.memset(causal_bf[:, :], 0.0)
            pool.memset(before_bf[:, :], 0.0)
            pool.memset(ones_bf[:, :], 1.0)
            pool.memset(empty_i[:, :], EMPTY)
            pool_zero = pool.engine_nop()
            link(pool_zero)
            pool.affine_select(out=ident[:, :], in_=ident[:, :], compare_op=ALU.not_equal, fill=1.0, base=0,
                               pattern=[[-1, P]], channel_multiplier=1)
            pool.affine_select(out=causal_bf[:, :], in_=causal_bf[:, :], compare_op=ALU.is_ge, fill=MASK, base=0,
                               pattern=[[-1, P]], channel_multiplier=1)
            pool.affine_select(out=before_bf[:, :], in_=before_bf[:, :], compare_op=ALU.is_ge, fill=1.0, base=0,
                               pattern=[[-1, P]], channel_multiplier=1)
            pool.iota(iota32_i[:, :], [[1, NE]], base=0, channel_multiplier=0)
            link(pool.iota(pair_id[:, :, :], [[P, TT], [S, 2]], base=0, channel_multiplier=1))
            pool.engine_nop().then_inc(masks_ready, 3)
            for n in range(2):
                pool.dma_start(list_dram[n].rearrange("(p c) o -> p (c o)", c=P), empty_i[:, :]).then_inc(
                    lists_empty, 16)

            pool.wait_ge(consts_ready, 1)
            for t in range(TT):
                root(0, t)
            for r in range(8):
                pool.wait_ge(rope_parts, r + 1)
                if r >= 2:
                    pool.wait_ge(ropeT_done, r - 1)
                a, b, o = (v[:, r % 2, :].rearrange("p (g x e) -> p g x e", x=2, e=HALF)
                           for v in (rope_a, rope_b, roped))
                pool.tensor_tensor(o[:, :, 0, :], a[:, :, 0, :], b[:, :, 1, :], ALU.subtract)
                pool.tensor_tensor(o[:, :, 1, :], a[:, :, 1, :], b[:, :, 0, :], ALU.add).then_inc(roped_ready, 1)
            for h in range(H):
                head_root(h)

            def ml_mask(h):
                pool.wait_ge(ml_exp, h + 1)
                for j in range(TT):
                    v = ml_w[:, h % 2, ML_COL[j]:ML_COL[j] + P]
                    pool.affine_select(out=v, in_=v, compare_op=ALU.is_ge, fill=0.0, base=0, pattern=[[1, P]],
                                       channel_multiplier=-1).then_inc(ml_masked, 1)

            ml_mask(0)
            for h in range(H):
                if h + 1 < H:
                    ml_mask(h + 1)
                head_root(H + h)

            def slot_lists(layer):
                n = 2 * layer + 1
                for t in range(TT):
                    root(n, t)
                    if t >= 2:
                        scatter_ids(layer, t - 2)
                scatter_ids(layer, TT - 2)
                scatter_ids(layer, TT - 1)
                pool.wait_ge(list_stored, 16 * 2 * TT * (layer + 1))
                pool.dma_start(slot_pair[:, layer, :], list_dram[layer][0:CAP * NE, :].rearrange(
                    "(s e) o -> s (e o)", e=NE)).then_inc(list_loaded, 16)
                for n in range(2):
                    pool.dma_start(slot_half[n * SMALL:(n + 1) * SMALL, layer, :],
                                   list_dram[layer][0:SMALL * NE, :].rearrange("(s e) o -> s (e o)", e=NE)).then_inc(
                                       halves_loaded, 16)

            def scatter_ids(layer, t):
                pool.wait_ge(dest_ready, 4 * layer + t + 1)
                if layer == 0 and t == 0:
                    pool.wait_ge(lists_empty, 32)
                for k in range(2):
                    pool.indirect_dma_start(
                        out=list_dram[layer][:, :], out_offset=bass.IndirectOffsetOnAxis(ap=dest[:, t, k:k + 1], axis=0),
                        in_=pair_id[:, t, k:k + 1], in_offset=None, bounds_check=S * NE - 1,
                        oob_is_err=False).then_inc(list_stored, 16)

            def gather(layer, tokens, dst, out_sem):
                pool.indirect_dma_start(
                    out=dst, out_offset=None, in_=xn_dram[layer][:, :],
                    in_offset=bass.IndirectOffsetOnAxis(ap=tokens, axis=0),
                    bounds_check=last_token, oob_is_err=False).then_inc(out_sem, 16)

            def scatter(layer, pairs, src, out_sem):
                pool.indirect_dma_start(
                    out=pair_dram[layer][:, :], out_offset=bass.IndirectOffsetOnAxis(ap=pairs, axis=0),
                    in_=src, in_offset=None, bounds_check=last_pair, oob_is_err=False).then_inc(out_sem, 16)

            def scatter_halves(layer, halves, src, out_sem):
                pool.indirect_dma_start(
                    out=pair_dram[layer].rearrange("r (n c) -> (r n) c", n=2),
                    out_offset=bass.IndirectOffsetOnAxis(ap=halves, axis=0),
                    in_=src, in_offset=None, bounds_check=last_half, oob_is_err=False).then_inc(out_sem, 16)

            def tokens_of(layer, e):
                return pool.value_load(cnt_i[0:1, layer, bass.ds(e, 1)], min_val=0, max_val=S)

            def experts(layer):
                base = NE * layer
                pool.wait_ge(x_ready, 8 * layer + TT)
                pool.wait_ge(slots_ready, layer + 1)
                for b in range(2):
                    pool.wait_ge(xn_stored[b], 32 * (layer + 1))

                def gather_step(e, b):
                    pool.tensor_copy(tok_now[:, b:b + 1], slot_tok[:, layer, bass.ds(e, 1)]).then_inc(tok_copied, 1)
                    pool.wait_ge(tok_copied, base + e + 1)
                    pool.sem_inc(indirect_turn, 1)
                    count = tokens_of(layer, e)
                    with pool.If(count > SMALL):
                        gather(layer, tok_now[:, b:b + 1], xg[:, b, :], xg_loaded[b])
                    with pool.Else():
                        with pool.If(count > TINY):
                            gather(layer, tok_now[0:SMALL, b:b + 1], xg[0:SMALL, b, :], xg_loaded[b])
                        with pool.Else():
                            gather(layer, tok_now[0:TINY, b:b + 1], xg[0:TINY, b, :], xg_loaded[b])

                for b in range(XB):
                    gather_step(b, b)
                pool.wait_ge(halves_ready, layer + 1)

                def body(i, first, last):
                    for b in range(RING):
                        e = i * RING + b
                        pool.tensor_copy(half_now[:, b:b + 1], slot_half[:, layer, bass.ds(e, 1)])
                        pool.tensor_copy(pair_now[:, b:b + 1], slot_pair[:, layer, bass.ds(e, 1)]).then_inc(
                            pair_copied, 1)
                        pool.wait_ge(y_ready, base + e + 1)
                        pool.wait_ge(pair_copied, base + e + 1)
                        pool.sem_inc(indirect_turn, 1)
                        with pool.If(tokens_of(layer, e) > SMALL):
                            scatter(layer, pair_now[:, b:b + 1], y_sb[:, b % 2, :], y_stored[b % 2])
                        with pool.Else():
                            scatter_halves(layer, half_now[:, b:b + 1], y_sb[:, b % 2, 0:512], y_stored[b % 2])
                        if not last:
                            pool.wait_ge(gT_done, base + e + 1)
                            gather_step(e + XB, b)
                expert_loop(pool, body)
                for b in range(2):
                    pool.wait_ge(y_stored[b], 16 * (NE // 2) * (layer + 1))

            def overflow(layer):
                o = ov[layer]
                pool.wait_ge(counts_ready, layer + 1)
                most = pool.value_load(cnt_max[0:1, layer:layer + 1], min_val=0, max_val=S)
                for r in range(OV_ROUNDS):
                    with pool.If(most > CAP * (r + 1)):
                        s0 = CAP * (r + 1) * NE
                        pool.dma_start(ov_pair[:, :], list_dram[layer][s0:s0 + CAP * NE, :].rearrange(
                            "(s e) o -> s (e o)", e=NE)).then_inc(o["list"], 16)
                        pool.wait_ge(o["idx"], 2 * r + 2)
                        with pool.Fori(0, NE) as e:
                            q = e + r * NE + 1
                            pool.tensor_copy(tok_now[:, 0:1], ov_tok[:, bass.ds(e, 1)])
                            pool.tensor_copy(pair_now[:, 0:1], ov_pair[:, bass.ds(e, 1)]).then_inc(o["copied"], 1)
                            pool.wait_ge(o["copied"], q)
                            pool.sem_inc(indirect_turn, 1)
                            gather(layer, tok_now[:, 0:1], xg[:, 0, :], o["rows"])
                            pool.wait_ge(o["y"], q)
                            pool.sem_inc(indirect_turn, 1)
                            scatter(layer, pair_now[:, 0:1], y_sb[:, 0, :], o["stored"])
                            pool.wait_ge(o["stored"], 16 * q)
                pool.memset(fence[:, layer:layer + 1], 0.0).then_inc(pairs_stored, 1)

            last_token = pool.to_reg(S - 1)
            last_pair = pool.to_reg(2 * S - 1)
            last_half = pool.to_reg(4 * S - 1)
            slot_lists(0)
            experts(0)
            overflow(0)
            for t in range(TT):
                root(2, t)
            slot_lists(1)
            experts(1)
            overflow(1)
            for t in range(TT):
                root(4, t)


OFF = {p: n for n, p in enumerate([(j, i) for j in range(TT) for i in range(j + 1, TT)])}
ML_BANK = [(2, 0), (3, 0), (4, 0), (3, 384)]
ML_COL = [0, 512, 896, 1152]


_INS = ['x', 'positions', 'norm_mix', 'norm_ffn', 'ab_w_in', 'ab_gate_bias', 'ab_conv_w', 'ab_mlstm_norm',
        'ab_lambda', 'ab_diff_norm', 'ab_w_out', 'c_w_in', 'c_conv_w', 'c_w_out', 'moe_w_rg', 'moe_b_rg',
        'moe_w_re', 'moe_b_re', 'moe_w_gate', 'moe_w_up', 'moe_w_down', 'final_norm']


def kernel(**inputs):
    import numpy as _np
    import concourse.bacc as _bacc
    from concourse.bass_utils import run_bass_kernel_spmd as _run

    nc = _bacc.Bacc("TRN2", target_bir_lowering=False, num_devices=1)
    arrays, aps = {}, {}

    def give(name, a):
        a = _np.ascontiguousarray(a)
        arrays[f"in_{name}"] = a
        aps[name] = nc.dram_tensor(f"in_{name}", a.shape, mybir.dt.from_np(a.dtype), kind="ExternalInput").ap()

    for name in _INS:
        a = _np.asarray(inputs[name])
        if name in ('x', 'positions') or name.startswith('ab_') or name.startswith('c_'):
            a = a[0]
        if name in ('ab_conv_w', 'c_conv_w'):
            a = a.reshape(a.shape[0], -1, P).transpose(2, 1, 0)
        if name.startswith('moe_w_') and a.ndim == 5:
            a = a.reshape(a.shape[0], NE, *a.shape[3:])
        give(name, a)
    half = _np.arange(HALF, dtype=_np.float32) / _np.float32(HALF)
    give('inv_freq', (_np.float32(1.0) / _np.power(_np.float32(10000.0), half)).astype(_np.float32))
    out = nc.dram_tensor("out_dram", (S, D), F32, kind="ExternalOutput").ap()
    build(nc, *[aps[n] for n in _INS], aps['inv_freq'], out)
    r = _run(nc, [arrays], core_ids=[0])
    return r.results[0]["out_dram"].reshape(1, S, D)
```

```python
from contextlib import ExitStack

import concourse.bass as bass
from concourse import mybir

ALU = mybir.AluOpType
ACT = mybir.ActivationFunctionType
AX_X = mybir.AxisListType.X
F32 = mybir.dt.float32
F32R = mybir.dt.float32r
BF16 = mybir.dt.bfloat16
I32 = mybir.dt.int32
U32 = mybir.dt.uint32

P = 128
D = 1024
S = 512
KT = D // P
TT = S // P
H = 4
HD = 128
DD = 64
HALF = DD // 2
EPS = 1e-6
GF = 32
GC = GF + H
NG = 4
EG = 8
NE = NG * EG
FF = 256
FT = FF // P
CAP = P
SMALL = 64
TINY = 32
RING = 4
SLOT = 3 * KT * FF
XB = 4
LAM_INIT = 0.2
NEG = -3.0e38
MASK = -1.0e30
EMPTY = 1 << 14
OV_ROUNDS = S // CAP - 1

C_MQK, C_MV, C_MO, C_GATE, C_DQ, C_DK, C_DV = 0, 1024, 1536, 2048, 2056, 2568, 3080

L0_COLS = [C_DQ, C_DK, C_DV, C_MV, C_MQK, C_MQK + 512, C_MO]
N_HALF = 2 * len(L0_COLS)
HC = 256
N_MIX0 = N_HALF + 2
N_MIX1 = KT + 2
EXPERT_USE = [N_MIX0, N_MIX0 + NE + N_MIX1]
MIX_USE = [0, N_MIX0 + NE]
MIX_DONE = [0, N_MIX0]

PAIRS = [(j, i) for j in range(TT) for i in range(j, TT)]

TWO_PI = (6.28125, 0.00193023681640625, 5.066394805908203e-06, 3.795019905382127e-09)
PI_IN = 3.1415925
MAGIC = 12582912.0


def build(nc, x_in, positions, norm_mix, norm_ffn, w_in0, gate_bias, conv0, mlstm_norm, lam_vecs,
          diff_norm, w_out0, w_in1, conv1, w_out1, w_rg, b_rg, w_re, b_re, w_gate, w_up, w_down,
          final_norm, inv_freq, out):
    with ExitStack() as ctx:
        def sb(name, shape, dt=F32):
            return ctx.enter_context(nc.sbuf_tensor(name, shape, dt))

        def shared(name, shape):
            with nc.sbuf_tensor(name + "_r", shape, F32R) as r:
                pass
            return r, sb(name, shape)

        def sem(name):
            return ctx.enter_context(nc.semaphore(name))

        ps = ctx.enter_context(nc.psum_tensor("ps", [P, 8, 512], F32))
        x_r, x_sb = shared("x_sb", [P, TT, D])
        hT_h, hT = shared("hT", [P, KT, S])
        ring_r, ring = shared("ring", [P, RING, SLOT])
        work_r, work = shared("work", [P, 16400])
        ident = sb("ident", [P, P])
        ident_bf = sb("ident_bf", [P, P], BF16)
        causal_bf = sb("causal_bf", [P, P], BF16)
        before_bf = sb("before_bf", [P, P], BF16)
        ones_bf = sb("ones_bf", [P, P], BF16)
        iota_slot = sb("iota_slot", [P, P], BF16)
        iota_half = sb("iota_half", [P, P], BF16)
        tok_f = sb("tok_f", [P, 1])
        zeros4 = sb("zeros4", [H, P])
        iota32 = sb("iota32", [P, NE])
        iota32_i = sb("iota32_i", [P, NE], I32)
        pair_id = sb("pair_id", [P, TT, 2], I32)
        empty_i = sb("empty_i", [P, P], I32)
        g_mix = sb("g_mix", [P, 2, KT])
        g_ffn = sb("g_ffn", [P, 2, KT])
        g_mlstm = sb("g_mlstm", [P, 1])
        g_diff = sb("g_diff", [P, 1])
        g_diff_s = sb("g_diff_s", [P, 1])
        gate_b = sb("gate_b", [H, 2])
        conv0_w = sb("conv0_w", [P, KT, 4])
        conv1_w = sb("conv1_w", [P, KT, 3])
        lam_c = sb("lam_c", [P, 8])
        router_w = sb("router_w", [P, 2, KT, NG + NE])
        router_b = sb("router_b", [P, 2, NG + NE])
        pos_i = sb("pos_i", [P, TT], I32)
        pos_f = sb("pos_f", [P, TT])
        invf = sb("invf", [P, HALF])
        sin_t = sb("sin_t", [P, TT, HALF])
        cos_t = sb("cos_t", [P, TT, HALF])
        ss = sb("ss", [P, 5, TT])
        ms = sb("ms", [P, 5, TT])
        rstd = sb("rstd", [P, 5, TT])
        neg_half = sb("neg_half", [P, TT])
        negc = sb("negc", [H, S])
        m_state = sb("m_state", [H, TT + 1])
        ucol = sb("ucol", [P, len(PAIRS) + TT, H])
        em = sb("em", [P, TT, H])
        att_s = sb("att_s", [P, 12])
        hn = sb("hn", [P, 8, TT])
        hn_ms = sb("hn_ms", [P, 8, TT])
        hn_r = sb("hn_r", [P, 8, TT])
        den_t = sb("den_t", [P, 4, TT])
        lg = sb("lg", [P, TT, 8 + NE])
        g8 = sb("g8", [P, TT, 8])
        gi8 = sb("gi8", [P, TT, 8], U32)
        g_hot = sb("g_hot", [P, TT, 4 + EG * NG])
        g_f = sb("g_f", [P, TT, 2])
        esel = sb("esel", [P, TT, EG])
        e8 = sb("e8", [P, TT, 8])
        ei8 = sb("ei8", [P, TT, 8], U32)
        ei_f = sb("ei_f", [P, TT, 2])
        eid = sb("eid", [P, TT, 2])
        hot_bf = sb("hot_bf", [P, TT, NE], BF16)
        rank = sb("rank", [P, TT, 2])
        dest = sb("dest", [P, TT, 2], I32)
        soft = sb("soft", [P, 6, TT])
        pair_w = sb("pair_w", [P, 2, 2, TT])
        cnt_f = sb("cnt_f", [1, NE])
        cnt_i = sb("cnt_i", [1, 2, NE], I32)
        cnt_max = sb("cnt_max", [1, 2], I32)
        slot_pair = sb("slot_pair", [P, 2, NE], I32)
        slot_tok = sb("slot_tok", [P, 2, NE], I32)
        slot_f = sb("slot_f", [P, 2, NE])
        slot_half = sb("slot_half", [P, 2, NE], I32)
        half_of = sb("half_of", [P, 1])
        tok_now = sb("tok_now", [P, XB], I32)
        pair_now = sb("pair_now", [P, XB], I32)
        half_now = sb("half_now", [P, XB], I32)
        fence = sb("fence", [1, 2])

        def part(start, size, pattern=None, **kw):
            v = work[:, start:start + size]
            return v.rearrange(pattern, **kw) if pattern else v

        ang = part(0, 512, "p (n t e) -> p n t e", n=4, t=TT)
        lam_sb = part(512, 256, "p (n d) -> p n d", n=4)
        lam_t = part(768, 128, "p (n d) -> p n d", n=2)
        dqT = part(0, 2048, "p (h s) -> p h s", h=H)
        dkT = part(2048, 2048, "p (h s) -> p h s", h=H)
        dv = part(4096, 2048, "p (t c) -> p t c", t=TT)
        mv = part(6144, TT * H * (HD + 1), "p (t h e) -> p t h e", t=TT, h=H)
        qkT = part(8208, 4096, "p (c s) -> p c s", c=2 * H)
        rope_a = part(12304, 1024, "p (b c) -> p b c", b=2)
        rope_b = part(13328, 1024, "p (b c) -> p b c", b=2)
        roped = part(14352, 1024, "p (b c) -> p b c", b=2)
        conv_acc = part(15376, 1024, "p (b c) -> p b c", b=2)
        att_e = part(12304, 1024, "p (c k) -> p c k", c=2)
        att_a = part(13328, 512)
        att_aT = part(13840, 512)
        att_o = part(14352, 512)
        att_q = part(14864, 512)
        row_b = work[0:H, 8208:8720]
        row_u = work[0:H, 8720:9232]
        row_c = work[0:H, 9232:9744]
        row_m = work[0:H, 9744:10256]
        row_i = work[0:H, 11280:11792]
        row_f = work[0:H, 11792:12304]
        row_off = work[0:H, 10256:11280].rearrange("p (n j) -> p n j", n=8)
        ml_w = part(0, 2560, "p (b k) -> p b k", b=2)
        ml_s = part(2560, 2560, "p (b k) -> p b k", b=2)
        ml_h = part(5120, 1024, "p (b k) -> p b k", b=2)
        ml_q = part(14352, 512)
        gate_w = part(3072, KT * GC, "p (k c) -> p k c", k=KT)
        gate_h = work_r[:, 1024:1024 + KT * GC].rearrange("p (k c) -> p k c", k=KT)
        gate_l = work_r[:, 2048:2048 + KT * GC].rearrange("p (k c) -> p k c", k=KT)
        o_gate = ring[:, 2, 4096:6144].rearrange("p (t c) -> p t c", t=TT)
        mergedM = hT[:, 0:H, :]
        mergedD = ring[:, 3, 4096:6144].rearrange("p (h s) -> p h s", h=H)
        xn_mix = part(12304, 2048, "p (b c) -> p b c", b=2)
        xn_ffn = part(4096, 2048, "p (b c) -> p b c", b=2)

        def xn(n, t):
            return (xn_ffn if n % 2 else xn_mix)[:, t % 2, :]

        junk = part(15376, 1024)
        hot = part(8208, TT * 2 * NE, "p (t k e) -> p t k e", t=TT, k=2)
        at_slot = part(6144, 512).bitcast(BF16).rearrange("p (t k s) -> p t k s", t=TT, k=2)
        at_half = part(6656, 512).bitcast(BF16).rearrange("p (t k s) -> p t k s", t=TT, k=2)
        id_hot = part(7168, 256).bitcast(BF16).rearrange("p (t k i e) -> p t k i e", t=TT, k=2, i=2)
        iota_tmp = part(3584, 2 * P, "p (n s) -> p n s", n=2).bitcast(I32)
        rank_t = part(8464, TT * 2 * NE, "p (t k e) -> p t k e", t=TT, k=2)
        xg = part(0, XB * D, "p (b c) -> p b c", b=XB)
        xgT = part(4096, 2048, "p (b k s) -> p b k s", b=2, k=KT)
        hid = part(6144, 512, "p (b c) -> p b c", b=2)
        sil = part(6656, 512, "p (b c) -> p b c", b=2)
        y_sb = part(7168, 2048, "p (b c) -> p b c", b=2)
        last_w = part(9216, SLOT)
        ov_w = last_w
        ov_pair = part(15376, NE).bitcast(I32)
        ov_tok = part(15408, NE).bitcast(I32)
        ov_f = part(15440, NE)
        hidT = part(15472, 512, "p (b c) -> p b c", b=2)
        yp = part(0, 8192, "p (t k c) -> p t k c", t=TT, k=2)
        fin = part(8192, 4096, "p (t c) -> p t c", t=TT)
        g_final = part(12304, 1024)
        rest1 = work_r[:, 8208:8208 + 4096].rearrange("p (k s) -> p k s", k=KT)

        def hT_rest(n, t):
            if n == 0:
                return x_r[:, t, :].rearrange("p (k s) -> p k s", k=KT)
            return rest1[:, :, t * P:(t + 1) * P]

        yT = part(0, 4096, "p (c s) -> p c s", c=KT)
        c_sb = part(4096, 1024, "p (b s) -> p b s", b=2)
        cx = part(5120, 1024, "p (b s) -> p b s", b=2)
        c_acc = part(6144, 1024, "p (b s) -> p b s", b=2)

        xn_dram = [nc.dram_tensor(f"xn_rows_{n}", [S, D], F32).ap() for n in range(2)]
        pair_dram = [nc.dram_tensor(f"pair_rows_{n}", [2 * S, D], F32).ap() for n in range(2)]
        list_dram = [nc.dram_tensor(f"slot_list_{n}", [S * NE, 1], I32).ap() for n in range(2)]

        x_loaded = [sem(f"x_loaded_{t}") for t in range(TT)]
        first_loaded = sem("first_loaded")
        consts_loaded = sem("consts_loaded")
        slot_loaded = [sem(f"slot_loaded_{s}") for s in range(RING)]
        last_loaded = sem("last_loaded")
        mixer_used = sem("mixer_used")
        masks_ready = sem("masks_ready")
        pool_chain = sem("pool_chain")
        dve_chain = sem("dve_chain")
        act_chain = sem("act_chain")
        consts_ready = sem("consts_ready")
        lists_empty = sem("lists_empty")
        angles_ready = sem("angles_ready")
        rope_table = sem("rope_table")
        lam_sum = sem("lam_sum")
        lam_exp = sem("lam_exp")
        x_ready = sem("x_ready")
        sumsq = sem("sumsq")
        rstd_ready = sem("rstd_ready")
        xn_ready = sem("xn_ready")
        xT_done = sem("xT_done")
        high_ready = sem("high_ready")
        rest_ready = sem("rest_ready")
        gate_high = sem("gate_high")
        gate_split = sem("gate_split")
        w_high = sem("w_high")
        w_split = sem("w_split")
        hT_ready = sem("hT_ready")
        xn_stored = [sem(f"xn_stored_{b}") for b in range(2)]
        proj_done = sem("proj_done")
        gates_abs = sem("gates_abs")
        gates_ln = sem("gates_ln")
        rows_ready = sem("rows_ready")
        rowsT_done = sem("rowsT_done")
        ucol_ready = sem("ucol_ready")
        em_ready = sem("em_ready")
        rope_parts = sem("rope_parts")
        roped_ready = sem("roped_ready")
        ropeT_done = sem("ropeT_done")
        dqkT_ready = sem("dqkT_ready")
        kv_copied = sem("kv_copied")
        conv_ready = sem("conv_ready")
        qk_ready = sem("qk_ready")
        ogate_ready = sem("ogate_ready")
        att_scores = sem("att_scores")
        att_max = sem("att_max")
        att_exp = sem("att_exp")
        att_probs = sem("att_probs")
        att_T = sem("att_T")
        att_aT_ready = sem("att_aT_ready")
        att_pv = sem("att_pv")
        att_o_copied = sem("att_o_copied")
        head_ss = sem("head_ss")
        head_rstd = sem("head_rstd")
        att_normed = sem("att_normed")
        att_fT = sem("att_fT")
        diff_merged = sem("diff_merged")
        ml_maxima = sem("ml_maxima")
        ml_scores = sem("ml_scores")
        ml_exp = sem("ml_exp")
        ml_masked = sem("ml_masked")
        ml_sT = sem("ml_sT")
        ml_num = sem("ml_num")
        ml_normed = sem("ml_normed")
        ml_fT = sem("ml_fT")
        mlstm_merged = sem("mlstm_merged")
        wo_done = sem("wo_done")
        logits_done = sem("logits_done")
        hot_ready = sem("hot_ready")
        top_ready = sem("top_ready")
        soft_exp = sem("soft_exp")
        rank_done = sem("rank_done")
        count_done = sem("count_done")
        counts_ready = sem("counts_ready")
        dest_ready = sem("dest_ready")
        halves_ready = sem("halves_ready")
        slot_hot_ready = sem("slot_hot_ready")
        half_hot_ready = sem("half_hot_ready")
        slots_done = sem("slots_done")
        slots_ready = sem("slots_ready")
        xg_loaded = [sem(f"xg_loaded_{b}") for b in range(XB)]
        gT_done = sem("gT_done")
        xgT_ready = sem("xgT_ready")
        gu_done = sem("gu_done")
        silu_done = sem("silu_done")
        hid_ready = sem("hid_ready")
        hidT_done = sem("hidT_done")
        hidT_ready = sem("hidT_ready")
        down_done = sem("down_done")
        y_ready = sem("y_ready")
        y_stored = [sem(f"y_stored_{b}") for b in range(2)]
        tok_copied = sem("tok_copied")
        indirect_turn = sem("indirect_turn")
        pair_copied = sem("pair_copied")
        pairs_stored = sem("pairs_stored")
        yp_loaded = [sem(f"yp_loaded_{t}") for t in range(TT)]
        ov = [{n: sem(f"ov{layer}_{n}") for n in (
            "listed", "list", "idx", "w", "rows", "T", "xT", "gu", "silu", "hid", "hT", "hTc", "down", "y", "stored",
            "copied")}
            for layer in range(2)]
        c_done = sem("c_done")
        c_copied = sem("c_copied")
        c_evac = sem("c_evac")
        g_final_loaded = sem("g_final_loaded")
        out_ready = sem("out_ready")
        out_stored = sem("out_stored")

        dmas_of_use = [1] * N_MIX0 + [3] * (NE - 1) + [0] + [3] * KT + [1] * 2 + [3] * (NE - 1) + [0]

        def loaded_value(use):
            return 16 * sum(dmas_of_use[u] for u in range(use % RING, use + 1, RING))

        def expert_loaded_value(layer, i, b):
            return loaded_value(EXPERT_USE[layer] + b) + 48 * i

        def wait_slot_free(eng, use):
            u = use - RING
            if u < 0:
                return
            if u < N_MIX0:
                eng.wait_ge(mixer_used, u + 1)
            elif u < MIX_USE[1]:
                eng.wait_ge(down_done, u - N_MIX0 + 1)
            elif u < EXPERT_USE[1]:
                eng.wait_ge(mixer_used, MIX_DONE[1] + u - MIX_USE[1] + 1)
            else:
                eng.wait_ge(down_done, NE + u - EXPERT_USE[1] + 1)

        def expert_loop(eng, body):
            body(0, True, False)
            with eng.Fori(1, NE // RING - 1) as i:
                body(i, False, False)
            body(NE // RING - 1, False, True)

        def weights_of(layer, u):
            n = 2048 if layer == 0 else 3072
            s = (MIX_USE[layer] + u) % RING
            return ring[:, s, 0:n], ring_r[:, s, 0:n], ring_r[:, s, n:2 * n]

        consumed = {}
        for j in range(29):
            consumed[j] = ((gates_abs, 1) if j < 1 else (rope_parts, j) if j < 9 else
                           (kv_copied, j - 8) if j < 17 else (conv_ready, j - 16) if j < 25 else
                           (ogate_ready, j - 24))
        EARLY = 29

        def split_at(j):
            group = (j - 1) // 4
            if j < 1 or group + 1 >= len(L0_COLS):
                return []
            if j > ATT0:
                return [2 * group + 2, 2 * group + 3] if j % 4 == 3 else []
            return [2 * group + 2] if j % 4 == 3 else [2 * group + 3] if j % 4 == 0 else []

        ATT0 = 13
        N_CONST = 1 + 5 * 2 + 7

        block = ctx.enter_context(nc.Block())

        @block.sync
        def _(sp):
            for t in range(TT):
                sp.dma_start(x_sb[:, t, :], x_in[t * P:(t + 1) * P, :]).then_inc(x_loaded[t], 16)

            def load(use, dst, src):
                sp.dma_start(dst, src).then_inc(slot_loaded[use % RING], 16)

            def load_matrices(layer, e, slot, loaded, down_free=None):
                sl = bass.ds(e, 1)
                sp.dma_start(slot[:, 0:2048], w_gate[layer][sl].rearrange(
                    "o (p k) f -> p (o k f)", k=KT)).then_inc(loaded, 16)
                sp.dma_start(slot[:, 2048:4096], w_up[layer][sl].rearrange(
                    "o (p k) f -> p (o k f)", k=KT)).then_inc(loaded, 16)
                if down_free is not None:
                    sp.wait_ge(down_done, down_free)
                sp.dma_start(slot[:, 4096:6144].rearrange("p (k n) -> p k n", k=FT), w_down[layer][sl].rearrange(
                    "o (k p) n -> p (o k) n", p=P)).then_inc(loaded, 16)

            def load_expert(layer, i, b, down_free=None):
                s = (EXPERT_USE[layer] + b) % RING
                load_matrices(layer, i * RING + b, ring[:, s, :], slot_loaded[s], down_free)

            def load_last_expert(layer):
                if layer == 0:
                    sp.wait_ge(mlstm_merged, H)
                else:
                    sp.wait_ge(mixer_used, N_MIX0 + KT)
                load_matrices(layer, NE - 1, last_w, last_loaded)

            def load_w_out(use, w, c0):
                wait_slot_free(sp, use)
                load(use, ring[:, use % RING, 0:4096].rearrange("p (c n) -> p c n", c=4),
                     w[c0 * P:(c0 + 4) * P, :].rearrange("(c p) n -> p c n", p=P))

            def load_experts(layer):
                base = NE * layer

                def body(i, first, last):
                    for b in range(RING - 1 if last else RING):
                        if first:
                            if b == 2:
                                load_last_expert(layer)
                            wait_slot_free(sp, EXPERT_USE[layer] + b)
                            load_expert(layer, i, b)
                        else:
                            before = base + i * RING + b - RING + 1
                            sp.wait_ge(gu_done, before)
                            load_expert(layer, i, b, before)
                expert_loop(sp, body)

            def load_pairs(layer):
                sp.wait_ge(pairs_stored, layer + 1)
                src = pair_dram[layer].rearrange("(k t p) d -> t p k d", k=2, p=P)
                for t in range(TT):
                    sp.dma_start(yp[:, t, :, :], src[t]).then_inc(yp_loaded[t], 16)

            def const(dst, src):
                sp.dma_start(dst, src).then_inc(consts_loaded, 16)

            def load_consts():
                sp.dma_start(gate_b[:, :], gate_bias.rearrange("(n h) -> h n", h=H),
                             allow_slow_non_contiguous=True).then_inc(consts_loaded, 16)
                for n in range(2):
                    const(g_ffn[:, n, :], norm_ffn[n].rearrange("(p k) -> p k", k=KT))
                    const(router_w[:, n, :, 0:NG], w_rg[n].rearrange("(p k) c -> p k c", k=KT))
                    const(router_w[:, n, :, NG:], w_re[n].rearrange("(p k) c -> p k c", k=KT))
                    const(router_b[:, n, 0:NG], b_rg[n].partition_broadcast(P))
                    const(router_b[:, n, NG:], b_re[n].partition_broadcast(P))
                const(g_mlstm[:, :], mlstm_norm.rearrange("(p o) -> p o", o=1))
                const(g_diff[:, :], diff_norm.rearrange("(p o) -> p o", o=1))
                const(conv0_w[:, :, :], conv0)
                const(conv1_w[:, :, :], conv1)
                const(lam_sb[:, :, :], lam_vecs.partition_broadcast(P))
                sp.dma_start(pos_i[:, :], positions.rearrange("(t p) -> p t", p=P),
                             allow_slow_non_contiguous=True).then_inc(consts_loaded, 16)
                const(invf[:, :], inv_freq.partition_broadcast(P))

            for use in range(N_HALF):
                if use == 2:
                    load_consts()
                wait_slot_free(sp, use)
                c0 = L0_COLS[use // 2] + use % 2 * HC
                load(use, ring[:, use % RING, 0:2048].rearrange("p (k c) -> p k c", k=KT),
                     w_in0[:, c0:c0 + HC].rearrange("(p k) c -> p k c", k=KT))
            load_w_out(N_HALF, w_out0, 0)
            load_w_out(N_HALF + 1, w_out0, 4)
            sp.wait_ge(mixer_used, N_HALF)
            for t in range(TT):
                sp.dma_start(x_sb[:, t, :], x_in[t * P:(t + 1) * P, :]).then_inc(x_loaded[t], 16)
            load_experts(0)
            for ct in range(KT):
                use = MIX_USE[1] + ct
                wait_slot_free(sp, use)
                slot = ring[:, use % RING, 0:3072].rearrange("p (j k c) -> p j k c", j=3, k=KT)
                for j in range(3):
                    load(use, slot[:, j],
                         w_in1[:, j * D + ct * P:j * D + (ct + 1) * P].rearrange("(p k) c -> p k c", k=KT))
                if ct == 1:
                    load_pairs(0)
            load_w_out(MIX_USE[1] + KT, w_out1, 0)
            load_w_out(MIX_USE[1] + KT + 1, w_out1, 4)
            load_experts(1)
            load_pairs(1)
            for t in range(TT):
                sp.wait_ge(out_ready, t + 1)
                sp.dma_start(out[t * P:(t + 1) * P, :], fin[:, t, :]).then_inc(out_stored, 16)
            sp.wait_ge(out_stored, 16 * TT)

        @block.tensor
        def _(pe):
            def transpose_norm(n, t):
                k0 = 4 * n + t
                pe.wait_ge(xn_ready, k0 + 1)
                if k0:
                    pe.wait_ge(hT_ready, k0)
                src = xn(n, t).rearrange("s (p k) -> s k p", k=KT)
                for k in range(KT):
                    mm = pe.transpose(ps[:, k // 4, (k % 4) * P:(k % 4 + 1) * P], src[:, k, :], ident[:, :])
                mm.then_inc(xT_done, 1)

            def w_out_part(layer, t, chunks):
                use = MIX_USE[layer] + (N_HALF if layer == 0 else KT)
                for n in range(2):
                    if n and t >= 2:
                        router_tile(layer, t - 2)
                    for c in chunks:
                        w = ring[:, (use + c // 4) % RING, 0:4096].rearrange("p (c n) -> p c n", c=4)
                        lhs = ((mergedM if c < 4 else mergedD)[:, c % 4, t * P:(t + 1) * P] if layer == 0
                               else yT[:, c, t * P:(t + 1) * P])
                        mm = pe.matmul(ps[:, WO_BANK[t] + n, :], lhs, w[:, c % 4, n * 512:(n + 1) * 512],
                                       start=(c == 4), stop=(c == 3))
                return mm

            def w_out_weights(layer):
                use = MIX_USE[layer] + (N_HALF if layer == 0 else KT)
                pe.wait_ge(slot_loaded[use % RING], loaded_value(use))
                pe.wait_ge(slot_loaded[(use + 1) % RING], loaded_value(use + 1))

            def w_out_tile(layer, t):
                if t >= 2:
                    pe.wait_ge(x_ready, 8 * layer + t - 1)
                chunks = [4, 5, 6, 7, 0, 1, 2, 3]
                mm = w_out_part(layer, t, chunks[4:] if layer == 0 and t == 0 else chunks)
                mm.then_inc(wo_done, 1)
                if t == TT - 1:
                    pe.wait_ge(wo_done, 4 * layer + TT)
                    pe.sem_inc(mixer_used, 2)

            def router_tile(layer, t):
                pe.wait_ge(hT_ready, 4 * (2 * layer + 1) + t + 1)
                for k in range(KT):
                    mm = pe.matmul(ps[:, LOGIT_BANK[t], t * 36:t * 36 + 36], hT[:, k, t * P:(t + 1) * P],
                                   router_w[:, layer, k, :], start=(k == 0), stop=(k == KT - 1))
                mm.then_inc(logits_done, 1)

            def rank_tile(layer, t):
                pe.wait_ge(hot_ready, 4 * layer + t + 1)
                if t:
                    pe.wait_ge(dest_ready, 4 * layer + t)
                for j in range(t + 1):
                    mm = pe.matmul(ps[:, 3, t * NE:(t + 1) * NE], (before_bf if j == t else ones_bf)[:, :],
                                   hot_bf[:, j, :], start=(j == 0), stop=(j == t))
                mm.then_inc(rank_done, 1)

            def count_experts():
                for j in range(TT):
                    mm = pe.matmul(ps[0:1, 2, 256:256 + NE], ones_bf[:, 0:1], hot_bf[:, j, :],
                                   start=(j == 0), stop=(j == TT - 1))
                mm.then_inc(count_done, 1)

            def place_ids(hot_at, bank, ready):
                pe.wait_ge(ready[0], ready[1])
                for t in range(TT):
                    for k in range(2):
                        mm = pe.matmul(ps[:, bank, 0:2 * NE], hot_at[:, t, k, :],
                                       id_hot[:, t, k, :, :].rearrange("p i e -> p (i e)"),
                                       start=(t == 0 and k == 0), stop=(t == TT - 1 and k == 1))
                mm.then_inc(slots_done, 1)

            def w_out_norm_route(layer):
                n = 2 * layer + 1
                for t in range(TT):
                    w_out_tile(layer, t)
                    if t >= 2:
                        rank_tile(layer, t - 2)
                    if t >= 1:
                        transpose_norm(n, t - 1)
                router_tile(layer, TT - 2)
                transpose_norm(n, TT - 1)
                router_tile(layer, TT - 1)
                rank_tile(layer, TT - 2)
                rank_tile(layer, TT - 1)
                pe.wait_ge(x_ready, 8 * layer + TT)
                place_ids(at_slot, 4, (slot_hot_ready, 4 * (layer + 1)))
                count_experts()
                place_ids(at_half, 5, (half_hot_ready, 4 * (layer + 1)))

            def transpose_rows(src, out_sem):
                v = src.rearrange("s (p k) -> s k p", k=KT)
                for k in range(KT):
                    mm = pe.transpose(ps[:, k // 4, (k % 4) * P:(k % 4 + 1) * P], v[:, k, :], ident[:, :])
                mm.then_inc(out_sem, 1)

            def gate_up(w, xt, bank, small, out_sem):
                m = w[:, 0:4096].rearrange("p (g k f) -> p g k f", g=2, k=KT)
                order = ([(f, k) for k in range(KT) for f in range(FT)] if small else
                         [(f, k) for f in range(FT) for k in range(KT)])
                for f, k in order:
                    rhs = m[:, :, k, f * P:(f + 1) * P]
                    o = (ps[f * SMALL:(f + 1) * SMALL, bank, 0:2 * P] if small
                         else ps[:, bank, f * 2 * P:(f + 1) * 2 * P])
                    mm = pe.matmul(o.rearrange("s (g f) -> s g f", g=2), xt[:, k, 0:SMALL if small else CAP],
                                   rhs, start=(k == 0), stop=(k == KT - 1))
                mm.then_inc(out_sem, 1)

            def turn_hidden(hd, bank, small, out_sem):
                for f in range(1 if small else FT):
                    mm = pe.transpose(ps[:, bank, f * P:(f + 1) * P], hd[:, f * P:(f + 1) * P], ident[:, :])
                mm.then_inc(out_sem, 1)

            def down(w, ht, bank, small, out_sem):
                m = w[:, 4096:6144].rearrange("p (k n) -> p k n", k=FT)
                slots = SMALL if small else CAP
                for f in range(FT):
                    for n in range(2):
                        o = ps[n * SMALL:(n + 1) * SMALL, bank, :] if small else ps[:, bank + n, :]
                        mm = pe.matmul(o, ht[:, f * slots:(f + 1) * slots], m[:, f, n * 512:(n + 1) * 512],
                                       start=(f == 0), stop=(f == FT - 1))
                mm.then_inc(out_sem, 1)

            def experts(layer):
                base = NE * layer
                rows_before = 16 * (NE // XB) * layer

                def turn(i, b):
                    g = base + i * RING + b
                    pe.wait_ge(xg_loaded[b], rows_before + 16 * i + 16)
                    if not (isinstance(g, int) and g == 0):
                        pe.wait_ge(xgT_ready, g)
                    transpose_rows(xg[:, b, :], gT_done)

                def tokens_of(i, b):
                    return pe.value_load(cnt_i[0:1, layer, bass.ds(i * RING + b, 1)], min_val=0, max_val=S)

                def sized(count, step):
                    with pe.If(count > SMALL):
                        step(False)
                    with pe.Else():
                        step(True)

                def is_last(i, b):
                    return isinstance(i, int) and i * RING + b == NE - 1

                def weights(i, b):
                    return last_w if is_last(i, b) else ring[:, (EXPERT_USE[layer] + b) % RING, :]

                def gate_up_step(i, b, first):
                    g = base + i * RING + b
                    use = EXPERT_USE[layer] + b
                    count = tokens_of(i, b)
                    if is_last(i, b):
                        pe.wait_ge(last_loaded, 48 * (layer + 1))
                    else:
                        pe.wait_ge(slot_loaded[use % RING], expert_loaded_value(layer, i, b))
                    pe.wait_ge(xgT_ready, g + 1)
                    if not (first and b < 2 and layer == 0):
                        pe.wait_ge(hidT_ready, g - 1)
                    sized(count, lambda small: gate_up(weights(i, b), xgT[:, b % 2], 2 + b % 2, small, gu_done))

                def down_and_turn(i, b, before, first):
                    g = base + i * RING + b
                    if before:
                        down_step(*before, first)
                    count = tokens_of(i, b)
                    pe.wait_ge(hid_ready, g + 1)
                    sized(count, lambda small: turn_hidden(hid[:, b % 2, :], 2 + b % 2, small, hidT_done))

                def down_step(i, b, first):
                    g = base + i * RING + b
                    count = tokens_of(i, b)
                    pe.wait_ge(hidT_ready, g + 1)
                    if not (first and b < 2 and layer == 0):
                        pe.wait_ge(y_ready, g - 1)
                    sized(count, lambda small: down(weights(i, b), hidT[:, b % 2, :], 4 + 2 * (b % 2), small, down_done))

                pe.wait_ge(counts_ready, layer + 1)
                turn(0, 0)

                def body(i, first, last):
                    for b in range(RING):
                        gate_up_step(i, b, first)
                        if b < RING - 1:
                            turn(i, b + 1)
                        elif not last:
                            turn(i + 1, 0)
                        if b > 0:
                            down_and_turn(i, b, (i, b - 1), first)
                        else:
                            down_and_turn(i, b, None if first else (i - 1, RING - 1), False)
                expert_loop(pe, body)
                down_step(NE // RING - 1, RING - 1, False)

            def overflow(layer):
                o = ov[layer]
                most = pe.value_load(cnt_max[0:1, layer:layer + 1], min_val=0, max_val=S)
                for r in range(OV_ROUNDS):
                    with pe.If(most > CAP * (r + 1)):
                        with pe.Fori(0, NE) as e:
                            q = e + r * NE + 1
                            pe.wait_ge(o["rows"], 16 * q)
                            transpose_rows(xg[:, 0, :], o["T"])
                            pe.wait_ge(o["xT"], q)
                            pe.wait_ge(o["w"], 48 * q)
                            gate_up(ov_w, xgT[:, 0], 2, False, o["gu"])
                            pe.wait_ge(o["hid"], q)
                            turn_hidden(hid[:, 0, :], 2, False, o["hT"])
                            pe.wait_ge(o["hTc"], q)
                            down(ov_w, hidT[:, 0, :], 4, False, o["down"])

            pe.wait_ge(masks_ready, 3)
            for t in range(TT):
                transpose_norm(0, t)

            pe.wait_ge(gate_split, 1)
            pe.wait_ge(rest_ready, TT)

            def products(out, high, rest, k):
                (lh, rh), (ll, rl) = high, rest
                for n, (a, b) in enumerate(((lh, rh), (lh, rl), (ll, rh))):
                    mm = pe.matmul(out, a, b, start=(k == 0 and n == 0), stop=(k == KT - 1 and n == 2))
                return mm

            def project(j):
                if j >= 2:
                    pe.wait_ge(*consumed[j - 2])
                bank = ps[:, j % 2, :]
                rests = x_r[:, :, :].rearrange("p t (k s) -> p k t s", k=KT)
                if j == 0:
                    for k in range(KT):
                        mm = products(ps[0:GC, 0, :], (gate_h[:, k, :], hT_h[:, k, :]), (gate_l[:, k, :], rests[:, k]), k)
                    mm.then_inc(proj_done, 1)
                    return
                group, t = (j - 1) // 4, (j - 1) % 4
                pe.wait_ge(w_split, 2 * group + 2)

                def w(half):
                    _, low, high = weights_of(0, 2 * group + half)
                    return (high.rearrange("p (k c) -> p k c", k=KT), low.rearrange("p (k c) -> p k c", k=KT))

                if group in (4, 5):
                    high, low = w(t // 2)
                    c = slice((t % 2) * P, (t % 2 + 1) * P)
                    for k in range(KT):
                        mm = products(bank, (high[:, k, c], hT_h[:, k, :]), (low[:, k, c], rests[:, k]), k)
                else:
                    for half in range(2):
                        high, low = w(half)
                        for k in range(KT):
                            mm = products(bank[:, half * HC:(half + 1) * HC],
                                          (hT_h[:, k, t * P:(t + 1) * P], high[:, k, :]),
                                          (hT_rest(0, t)[:, k, :], low[:, k, :]), k)
                mm.then_inc(proj_done, 1)
                if t == 3:
                    pe.wait_ge(proj_done, j + 1)
                    pe.sem_inc(mixer_used, 2)

            def rope_T(r):
                pe.wait_ge(roped_ready, r + 1)
                if r >= 2:
                    pe.wait_ge(dqkT_ready, r - 1)
                for h in range(H):
                    mm = pe.transpose(ps[:, 2 + r % 2, h * P:(h + 1) * P], roped[:, r % 2, h * P:(h + 1) * P],
                                      ident[:, :])
                mm.then_inc(ropeT_done, 1)

            def gate_cols_T():
                pe.wait_ge(rows_ready, 1)
                for n, (j, i) in enumerate(PAIRS):
                    src = row_u[:, j * P:(j + 1) * P] if i == j else row_off[:, OFF[(j, i)], :]
                    mm = pe.transpose(ps[:, 5, n * H:(n + 1) * H], src, ident[0:H, 0:H])
                for i in range(TT):
                    n = len(PAIRS) + i
                    mm = pe.transpose(ps[:, 5, n * H:(n + 1) * H], row_m[:, i * P:(i + 1) * P], ident[0:H, 0:H])
                mm.then_inc(rowsT_done, 1)

            def att_score(a):
                h, i = a // TT, a % TT
                n = (i + 1) * P
                if a == 0:
                    pe.wait_ge(dqkT_ready, 8)
                    pe.wait_ge(ucol_ready, 1)
                else:
                    pe.wait_ge(att_exp, a)
                for c in range(2):
                    q = slice(c * DD, (c + 1) * DD)
                    if i:
                        pe.matmul(ps[:, 4 + c, 0:i * P], dqT[q, h, i * P:n], dkT[q, h, 0:i * P],
                                  start=True, stop=True)
                    pe.matmul(ps[:, 4 + c, i * P:n], dqT[q, h, i * P:n], dkT[q, h, i * P:n],
                              start=True, stop=False)
                    mm = pe.matmul(ps[:, 4 + c, i * P:n], ident_bf[:, :], causal_bf[:, :], start=False, stop=True)
                mm.then_inc(att_scores, 1)

            def att_turn(a):
                i = a % TT
                pe.wait_ge(att_probs, a + 1)
                if a >= 1:
                    pe.wait_ge(att_aT_ready, a)
                for j in range(i + 1):
                    mm = pe.transpose(ps[:, 6, j * P:(j + 1) * P], att_a[:, j * P:(j + 1) * P], ident[:, :])
                mm.then_inc(att_T, 1)

            def att_values(a):
                h, i = a // TT, a % TT
                pe.wait_ge(att_aT_ready, a + 1)
                if i == 0:
                    if h:
                        pe.wait_ge(att_o_copied, h)
                    else:
                        pe.wait_ge(kv_copied, 4)
                for j in range(i + 1):
                    mm = pe.matmul(ps[:, 7, i * P:(i + 1) * P], att_aT[:, j * P:(j + 1) * P],
                                   dv[:, j, h * HD:(h + 1) * HD], start=(j == 0), stop=(j == i))
                mm.then_inc(att_pv, 1)

            def att_finish_T(h):
                pe.wait_ge(att_normed, h + 1)
                if h:
                    pe.wait_ge(diff_merged, h)
                for i in range(TT):
                    mm = pe.transpose(ps[:, FT_BANK[h], i * P:(i + 1) * P], att_o[:, i * P:(i + 1) * P], ident[:, :])
                mm.then_inc(att_fT, 1)

            def ml_max(h):
                if h == 0:
                    pe.wait_ge(ogate_ready, TT)
                elif h >= 2:
                    pe.wait_ge(ml_exp, h - 1)
                pe.matmul(ps[:, h % 2, :], ident[0:H, h:h + 1].to_broadcast([H, P]), negc[:, :], start=True,
                          stop=True).then_inc(ml_maxima, 1)

            def ml_score(h):
                if h == 0:
                    pe.wait_ge(diff_merged, H - 1)
                    pe.wait_ge(att_exp, 16)
                    pe.wait_ge(qk_ready, 2 * H)
                else:
                    pe.wait_ge(ml_sT, h)
                for j in range(TT):
                    bank, c0 = ML_BANK[j]
                    mm = pe.matmul(ps[:, bank, c0:c0 + S - j * P], qkT[:, H + h, j * P:(j + 1) * P],
                                   qkT[:, h, j * P:S], start=True, stop=True)
                mm.then_inc(ml_scores, 1)

            def ml_values(h):
                pe.wait_ge(ml_sT, h + 1)
                if h == 0:
                    pe.wait_ge(kv_copied, 8)
                    pe.wait_ge(diff_merged, H)
                else:
                    pe.wait_ge(ml_normed, h)
                for i in range(TT):
                    c0 = (i % 2) * (HD + 1)
                    for j in range(i + 1):
                        s0 = ML_COL[j] + (i - j) * P
                        mm = pe.matmul(ps[:, 5 + i // 2, c0:c0 + HD + 1], ml_s[:, h % 2, s0:s0 + P],
                                       mv[:, j, h, :], start=(j == 0), stop=(j == i))
                mm.then_inc(ml_num, 1)

            def ml_finish_T(h):
                pe.wait_ge(ml_normed, h + 1)
                if h:
                    pe.wait_ge(mlstm_merged, h)
                for i in range(TT):
                    mm = pe.transpose(ps[:, 7, i * P:(i + 1) * P], ml_h[:, h % 2, i * P:(i + 1) * P], ident[:, :])
                mm.then_inc(ml_fT, 1)

            for j in range(ATT0 + 19):
                if j < 29:
                    project(j)
                if j == 6:
                    gate_cols_T()
                if 4 <= j < 12:
                    rope_T(j - 4)
                a = j - ATT0
                if 0 <= a - 2 < 16:
                    att_values(a - 2)
                if 0 <= a - 1 < 16:
                    att_turn(a - 1)
                if 0 <= a < 16:
                    att_score(a)
                if a >= 6 and (a - 6) % 4 == 0:
                    att_finish_T((a - 6) // 4)
                if j == EARLY:
                    ml_max(0)
                    ml_score(0)
                    ml_max(1)

            for h in range(H):
                if h + 1 < H:
                    ml_score(h + 1)
                ml_values(h)
                if h + 2 < H:
                    ml_max(h + 2)
                if h:
                    ml_finish_T(h - 1)
            w_out_weights(0)
            w_out_part(0, 0, [4, 5, 6, 7])
            ml_finish_T(H - 1)

            pe.wait_ge(mlstm_merged, H)
            w_out_norm_route(0)
            experts(0)
            overflow(0)

            for t in range(TT):
                transpose_norm(2, t)
            pe.wait_ge(rest_ready, 2 * TT)
            for ct in range(KT):
                pe.wait_ge(w_split, N_HALF + ct + 1)
                if ct >= 2:
                    pe.wait_ge(c_evac, ct - 1)
                _, low, high = (v.rearrange("p (j k c) -> p j k c", j=3, k=KT) for v in weights_of(1, ct))
                for n, j in enumerate((1, 2, 0)):
                    for k in range(KT):
                        mm = products(ps[:, 2 + 3 * (ct % 2) + n, :], (high[:, j, k, :], hT_h[:, k, :]),
                                      (low[:, j, k, :], rest1[:, k, :]), k)
                    mm.then_inc(c_done, 1)
                pe.wait_ge(c_done, 3 * (ct + 1))
                pe.sem_inc(mixer_used, 1)
            pe.wait_ge(c_evac, KT)
            w_out_weights(1)
            w_out_norm_route(1)
            experts(1)
            overflow(1)

        @block.scalar
        def _(act):
            n_chain = [0]

            def link(ins):
                n_chain[0] += 1
                ins.then_inc(act_chain, 1)
                act.wait_ge(act_chain, n_chain[0])

            for n in range(2):
                act.dma_start(g_mix[:, n, :], norm_mix[n].rearrange("(p k) -> p k", k=KT)).then_inc(first_loaded, 16)
            for n in range(2):
                act.dma_start(gate_w[:, :, n * GF:n * GF + H], w_in0[:, C_GATE + n * H:C_GATE + (n + 1) * H].rearrange(
                    "(p k) c -> p k c", k=KT)).then_inc(first_loaded, 16)

            def square(n, t):
                k0 = 4 * n + t
                if n == 0:
                    act.wait_ge(x_loaded[t], 16)
                else:
                    act.wait_ge(x_ready, 4 * (n - 1) + t + 1)
                if k0:
                    act.wait_ge(sumsq, k0)
                act.activation(junk, x_sb[:, t, :], ACT.Square, accum_out=ss[:, n, t:t + 1]).then_inc(sumsq, 1)

            def store_rows(layer, t):
                act.wait_ge(xn_ready, 4 * (2 * layer + 1) + t + 1)
                act.dma_start(xn_dram[layer][t * P:(t + 1) * P, :], xn(2 * layer + 1, t)).then_inc(xn_stored[t % 2], 16)

            def norm_route(layer):
                for t in range(TT):
                    square(2 * layer + 1, t)
                    store_rows(layer, t)
                act.wait_ge(top_ready, layer + 1)
                for t in range(TT):
                    act.activation(g_hot[:, t, 0:NG], lg[:, t, 0:NG], ACT.Exp, bias=soft[:, 0, t:t + 1],
                                   accum_out=soft[:, 1, t:t + 1])
                act.activation(soft[:, 3, :], soft[:, 2, :], ACT.Exp).then_inc(soft_exp, 1)

            def silu_step(bank, sil_v, gate_sem, gate_value, out_sem):
                act.wait_ge(gate_sem, gate_value)
                act.activation(sil_v.rearrange("p (f c) -> p f c", f=FT),
                               ps[:, bank, :].rearrange("p (f g c) -> p f g c", f=FT, g=2)[:, :, 0, :],
                               ACT.Silu).then_inc(out_sem, 1)

            def y_copy(bank, y_v, out_sem):
                act.activation(y_v.rearrange("p (n c) -> p n c", n=2), ps[:, bank:bank + 2, :],
                               ACT.Copy).then_inc(out_sem, 1)

            def experts(layer):
                base = NE * layer
                stored_before = 16 * (NE // 2) * layer

                def silu_of(i, b, first):
                    g = base + i * RING + b
                    if not (first and b < 2 and layer == 0):
                        act.wait_ge(hid_ready, g - 1)
                    silu_step(2 + b % 2, sil[:, b % 2, :], gu_done, g + 1, silu_done)

                def y_of(i, b, first):
                    g = base + i * RING + b
                    act.wait_ge(down_done, g + 1)
                    if not (first and b < 2 and layer == 0):
                        act.wait_ge(y_stored[b % 2], stored_before + 32 * i + 16 * ((b - 2) // 2 + 1))
                    y_copy(4 + 2 * (b % 2), y_sb[:, b % 2, :], y_ready)

                def body(i, first, last):
                    for b in range(RING):
                        silu_of(i, b, first)
                        if b > 0:
                            y_of(i, b - 1, first)
                        elif not first:
                            y_of(i - 1, RING - 1, False)
                expert_loop(act, body)
                y_of(NE // RING - 1, RING - 1, False)

            def overflow(layer):
                o = ov[layer]
                act.wait_ge(counts_ready, layer + 1)
                most = act.value_load(cnt_max[0:1, layer:layer + 1], min_val=0, max_val=S)
                for r in range(OV_ROUNDS):
                    with act.If(most > CAP * (r + 1)):
                        with act.Fori(0, NE) as e:
                            q = e + r * NE + 1
                            sl = bass.ds(e, 1)
                            act.dma_start(ov_w[:, 0:2048], w_gate[layer][sl].rearrange(
                                "o (p k) f -> p (o k f)", k=KT)).then_inc(o["w"], 16)
                            act.dma_start(ov_w[:, 2048:4096], w_up[layer][sl].rearrange(
                                "o (p k) f -> p (o k f)", k=KT)).then_inc(o["w"], 16)
                            act.dma_start(ov_w[:, 4096:6144].rearrange("p (k n) -> p k n", k=FT), w_down[layer][
                                sl].rearrange("o (k p) n -> p (o k) n", p=P)).then_inc(o["w"], 16)
                            silu_step(2, sil[:, 0, :], o["gu"], q, o["silu"])
                            act.wait_ge(o["down"], q)
                            y_copy(4, y_sb[:, 0, :], o["y"])

            def high_part(n, t):
                act.wait_ge(hT_ready, 4 * n + t + 1)
                act.activation(hT_h[:, :, t * P:(t + 1) * P], xn(n, t).rearrange("p (k s) -> p k s", k=KT),
                               ACT.Copy).then_inc(high_ready, 1)

            def high_weights(layer, u):
                use = MIX_USE[layer] + u
                act.wait_ge(slot_loaded[use % RING], loaded_value(use))
                w, _, high = weights_of(layer, u)
                act.activation(high, w, ACT.Copy).then_inc(w_high, 1)

            for t in range(TT):
                square(0, t)
            act.wait_ge(first_loaded, 16 * 4)
            act.wait_ge(consts_ready, 1)
            act.activation(gate_h, gate_w[:, :, :], ACT.Copy).then_inc(gate_high, 1)
            for t in range(TT):
                high_part(0, t)
                if t >= 2:
                    high_weights(0, t - 2)
            act.wait_ge(lam_sum, 1)
            act.activation(lam_c[:, 2:4], lam_c[:, 0:2], ACT.Exp).then_inc(lam_exp, 1)
            act.wait_ge(angles_ready, 1)
            act.activation(sin_t[:, :, :], ang[:, 2, :, :], ACT.Sin)
            act.activation(cos_t[:, :, :], ang[:, 3, :, :], ACT.Sin).then_inc(rope_table, 1)
            act.wait_ge(gates_abs, 1)
            link(act.activation(row_m[:, :], row_c[:, :], ACT.Exp, scale=-1.0))
            act.activation(row_c[:, :], row_m[:, :], ACT.Ln, bias=1.0).then_inc(gates_ln, 1)

            def rope_copy(r):
                act.wait_ge(ropeT_done, r + 1)
                dst = (dqT if r < 4 else dkT)[:, :, (r % 4) * P:(r % 4 + 1) * P]
                act.activation(dst, ps[:, 2 + r % 2, :].rearrange("p (h s) -> p h s", h=H),
                               ACT.Copy).then_inc(dqkT_ready, 1)

            def job(j):
                if 9 <= j < 17:
                    act.wait_ge(proj_done, j + 1)
                    t = (j - 1) % 4
                    if j < 13:
                        act.activation(dv[:, t, :], ps[:, j % 2, :], ACT.Copy).then_inc(kv_copied, 1)
                    else:
                        act.activation(mv[:, t, :, 0:HD], ps[:, j % 2, :].rearrange("p (h e) -> p h e", h=H),
                                       ACT.Copy).then_inc(kv_copied, 1)
                elif 17 <= j < 25:
                    act.wait_ge(conv_ready, j - 16)
                    act.activation(qkT[:, j - 17, :], conv_acc[:, j % 2, :], ACT.Silu).then_inc(qk_ready, 1)
                elif 25 <= j < 29:
                    act.wait_ge(proj_done, j + 1)
                    act.activation(o_gate[:, j - 25, :], ps[:, j % 2, :], ACT.Sigmoid).then_inc(ogate_ready, 1)

            def att_copy_T(a):
                n = (a % TT + 1) * P
                act.wait_ge(att_T, a + 1)
                if a >= 1:
                    act.wait_ge(att_pv, a)
                act.activation(att_aT[:, 0:n], ps[:, 6, 0:n], ACT.Copy).then_inc(att_aT_ready, 1)

            def att_exps(a):
                n = (a % TT + 1) * P
                act.wait_ge(att_max, a + 1)
                if a >= 1:
                    act.wait_ge(att_probs, a)
                for c in range(2):
                    ins = act.activation(att_e[:, c, 0:n], ps[:, 4 + c, 0:n], ACT.Exp, bias=att_s[:, 2 + c:3 + c],
                                         scale=DD ** -0.5, accum_out=att_s[:, 4 + c:5 + c])
                ins.then_inc(att_exp, 1)

            def ml_weights(h):
                act.wait_ge(ml_maxima, h + 1)
                if h == 0:
                    act.wait_ge(att_scores, 16)
                if h == 0:
                    act.wait_ge(ucol_ready, 1)
                if h >= 2:
                    act.wait_ge(ml_sT, h - 1)
                for n, (j, i) in enumerate(PAIRS):
                    c0 = ML_COL[j] + (i - j) * P
                    ins = act.activation(ml_w[:, h % 2, c0:c0 + P], ps[:, h % 2, i * P:(i + 1) * P], ACT.Exp,
                                         bias=ucol[:, n, h:h + 1])
                ins.then_inc(ml_exp, 1)

            for j in range(ATT0 + 19):
                for u in split_at(j):
                    high_weights(0, u)
                job(j)
                if 4 <= j < 12:
                    rope_copy(j - 4)
                if j == 8:
                    act.wait_ge(ucol_ready, 1)
                    act.activation(em[:, :, :], ucol[:, len(PAIRS):, :], ACT.Exp).then_inc(em_ready, 1)
                a = j - ATT0
                if a - 2 >= 0 and (a - 2) % 4 == 3 and a - 2 < 16:
                    h = (a - 2) // 4
                    act.wait_ge(att_pv, 4 * h + 4)
                    if h:
                        act.wait_ge(att_fT, h)
                    act.activation(att_o[:, :], ps[:, 7, :], ACT.Copy).then_inc(att_o_copied, 1)
                if 0 <= a - 1 < 16:
                    att_copy_T(a - 1)
                if 0 <= a < 16:
                    att_exps(a)
                if a >= 6 and (a - 6) % 4 == 0:
                    h = (a - 6) // 4
                    act.wait_ge(att_fT, h + 1)
                    act.activation(mergedD[:, h, :], ps[:, FT_BANK[h], :], ACT.Copy, scale=g_diff_s[:, 0:1]).then_inc(
                        diff_merged, 1)
                if j == EARLY:
                    ml_weights(0)

            def ml_merge(h):
                act.wait_ge(ml_fT, h + 1)
                if h == 0:
                    act.wait_ge(mixer_used, N_HALF)
                act.activation(mergedM[:, h, :], ps[:, 7, :], ACT.Copy, scale=g_mlstm[:, 0:1]).then_inc(
                    mlstm_merged, 1)

            for h in range(H):
                if h + 1 < H:
                    ml_weights(h + 1)
                if h:
                    ml_merge(h - 1)
            ml_merge(H - 1)
            norm_route(0)
            experts(0)
            overflow(0)

            for u in range(2):
                high_weights(1, u)
            for t in range(TT):
                square(2, t)
                if t:
                    high_part(2, t - 1)
            high_part(2, TT - 1)
            for ct in range(KT):
                act.wait_ge(c_done, 3 * ct + 1)
                if ct >= 2:
                    act.wait_ge(c_evac, ct - 1)
                act.activation(c_sb[:, ct % 2, :], ps[:, 2 + 3 * (ct % 2), :], ACT.Copy).then_inc(c_copied, 1)
                if ct + 2 < KT:
                    high_weights(1, ct + 2)
            norm_route(1)
            experts(1)
            overflow(1)
            act.dma_start(g_final, final_norm.partition_broadcast(P)).then_inc(g_final_loaded, 16)
            for t in range(TT):
                square(4, t)

        @block.vector
        def _(dve):
            n_chain = [0]

            def link(ins):
                n_chain[0] += 1
                ins.then_inc(dve_chain, 1)
                dve.wait_ge(dve_chain, n_chain[0])

            def normalise(n, t):
                k0 = 4 * n + t
                dve.wait_ge(rstd_ready, k0 + 1)
                if k0 >= 2:
                    dve.wait_ge(xT_done, k0 - 1)
                if n in (0, 2) and t >= 2:
                    dve.wait_ge(rest_ready, 4 * (n // 2) + t - 1)
                if n in (1, 3) and t >= 2:
                    dve.wait_ge(xn_stored[t % 2], 16 * (n // 2 * 2 + 1))
                dve.tensor_scalar(xn(n, t), x_sb[:, t, :], rstd[:, n, t:t + 1], None,
                                  ALU.mult).then_inc(xn_ready, 1)

            def gain_T(n, t):
                k0 = 4 * n + t
                dve.wait_ge(xT_done, k0 + 1)
                g = g_ffn[:, n // 2, :].unsqueeze(2).to_broadcast([P, KT, P])
                dve.tensor_tensor(hT[:, :, t * P:(t + 1) * P],
                                  ps[:, 0:2, :].rearrange("p b (k s) -> p (b k) s", s=P), g,
                                  ALU.mult).then_inc(hT_ready, 1)

            def turned(n, t):
                dve.wait_ge(xT_done, 4 * n + t + 1)
                g = g_mix[:, n // 2, :].unsqueeze(2).to_broadcast([P, KT, P])
                dve.tensor_tensor(xn(n, t).rearrange("p (k s) -> p k s", k=KT),
                                  ps[:, 0:2, :].rearrange("p b (k s) -> p (b k) s", s=P), g,
                                  ALU.mult).then_inc(hT_ready, 1)

            def rest_part(n, t):
                dve.wait_ge(high_ready, 4 * (n // 2) + t + 1)
                dve.tensor_tensor(hT_rest(n, t), xn(n, t).rearrange("p (k s) -> p k s", k=KT),
                                  hT_h[:, :, t * P:(t + 1) * P], ALU.subtract).then_inc(rest_ready, 1)

            def rest_weights(layer, u):
                dve.wait_ge(w_high, (0 if layer == 0 else N_HALF) + u + 1)
                w, low, high = weights_of(layer, u)
                dve.tensor_tensor(low, w, high, ALU.subtract).then_inc(w_split, 1)

            def norm_split(n, before):
                before(0)
                for t in range(TT):
                    if t + 1 < TT:
                        before(t + 1)
                    if t >= 2:
                        rest_part(n, t - 2)
                    normalise(n, t)
                    if t:
                        turned(n, t - 1)
                turned(n, TT - 1)
                rest_part(n, TT - 2)
                rest_part(n, TT - 1)

            def residual(layer, t):
                dve.wait_ge(wo_done, 4 * layer + t + 1)
                if layer == 0:
                    dve.wait_ge(x_loaded[t], 32)
                b = WO_BANK[t]
                dve.tensor_tensor(x_sb[:, t, :].rearrange("p (n c) -> p n c", n=2), ps[:, b:b + 2, :],
                                  x_sb[:, t, :].rearrange("p (n c) -> p n c", n=2), ALU.add).then_inc(x_ready, 1)

            def route(layer, t):
                dve.wait_ge(logits_done, 4 * layer + t + 1)
                dve.tensor_tensor(lg[:, t, 0:NG], ps[:, LOGIT_BANK[t], t * 36:t * 36 + NG], router_b[:, layer, 0:NG], ALU.add)
                link(dve.tensor_tensor(lg[:, t, 8:8 + NE], ps[:, LOGIT_BANK[t], t * 36 + NG:t * 36 + 36],
                                       router_b[:, layer, NG:], ALU.add))
                link(dve.max(g8[:, t, :], lg[:, t, 0:8]))
                link(dve.max_index(gi8[:, t, :], g8[:, t, :], lg[:, t, 0:8]))
                link(dve.tensor_copy(g_f[:, t, 0:1], gi8[:, t, 0:1]))
                dve.tensor_scalar(g_f[:, t, 1:2], g_f[:, t, 0:1], float(EG), None, ALU.mult)
                link(dve.tensor_scalar(g_hot[:, t, 0:NG], iota32[:, 0:NG], g_f[:, t, 0:1], None, ALU.is_equal))
                masked = g_hot[:, t, NG:].rearrange("p (e g) -> p e g", g=NG)
                link(dve.tensor_tensor(masked, lg[:, t, 8:].rearrange("p (g e) -> p e g", g=NG),
                                       g_hot[:, t, 0:NG].unsqueeze(1).to_broadcast([P, EG, NG]), ALU.mult))
                link(dve.tensor_reduce(esel[:, t, :], masked, AX_X, ALU.add))
                link(dve.max(e8[:, t, :], esel[:, t, :]))
                link(dve.max_index(ei8[:, t, :], e8[:, t, :], esel[:, t, :]))
                link(dve.tensor_copy(ei_f[:, t, :], ei8[:, t, 0:2]))
                link(dve.tensor_scalar(eid[:, t, :], ei_f[:, t, :], g_f[:, t, 1:2], None, ALU.add))
                dve.tensor_scalar(hot[:, t, 0, :], iota32[:, :], eid[:, t, 0:1], None, ALU.is_equal)
                link(dve.tensor_scalar(hot[:, t, 1, :], iota32[:, :], eid[:, t, 1:2], None, ALU.is_equal))
                dve.tensor_tensor(hot_bf[:, t, :], hot[:, t, 0, :], hot[:, t, 1, :], ALU.add).then_inc(hot_ready, 1)
                for k in range(2):
                    dve.tensor_scalar(id_hot[:, t, k, 0, :], hot[:, t, k, :], tok_f[:, 0:1], None, ALU.mult)
                    dve.tensor_scalar(id_hot[:, t, k, 1, :], hot[:, t, k, :], float(t * P + k * S - EMPTY), None,
                                      ALU.mult)

            def place(layer, t):
                dve.wait_ge(rank_done, 4 * layer + t + 1)
                link(dve.tensor_tensor(rank_t[:, t], hot[:, t],
                                       ps[:, 3, t * NE:(t + 1) * NE].unsqueeze(1).to_broadcast([P, 2, NE]), ALU.mult))
                link(dve.tensor_reduce(rank[:, t, :], rank_t[:, t], AX_X, ALU.add))
                for k in range(2):
                    ins = dve.tensor_scalar(at_slot[:, t, k, :], iota_slot[:, :], rank[:, t, k:k + 1], None,
                                            ALU.is_equal)
                ins.then_inc(slot_hot_ready, 1)
                for k in range(2):
                    ins = dve.tensor_scalar(at_half[:, t, k, :], iota_half[:, :], rank[:, t, k:k + 1], None,
                                            ALU.is_equal)
                ins.then_inc(half_hot_ready, 1)
                dve.scalar_tensor_tensor(out=dest[:, t, :], in0=rank[:, t, :], scalar=float(NE), in1=eid[:, t, :],
                                         op0=ALU.mult, op1=ALU.add).then_inc(dest_ready, 1)

            def w_out_norm_route(layer):
                n = 2 * layer + 1
                for t in range(TT):
                    residual(layer, t)
                    if t >= 1:
                        gain_T(n, t - 1)
                    normalise(n, t)
                    if t == TT - 1:
                        gain_T(n, t)
                    if t >= 1:
                        route(layer, t - 1)
                    if t >= 2:
                        place(layer, t - 2)
                place(layer, TT - 2)
                route(layer, TT - 1)
                place(layer, TT - 1)
                dve.wait_ge(slots_done, 2 * layer + 1)
                link(dve.tensor_scalar(slot_f[:, 1, :], ps[:, 4, NE:2 * NE], float(EMPTY), None, ALU.add))
                link(dve.tensor_tensor(slot_f[:, 0, :], slot_f[:, 1, :], ps[:, 4, 0:NE], ALU.add))
                dve.tensor_copy(slot_pair[:, layer, :], slot_f[:, 0, :])
                slot_tokens(slot_f[:, 1, :], slot_f[:, 0, :], slot_tok[:, layer, :])
                dve.wait_ge(count_done, layer + 1)
                link(dve.tensor_copy(cnt_f[:, :], ps[0:1, 2, 256:256 + NE]))
                dve.tensor_copy(cnt_i[:, layer, :], cnt_f[:, :])
                link(dve.tensor_reduce(cnt_max[:, layer:layer + 1], cnt_f[:, :], AX_X, ALU.max))
                dve.engine_nop().then_inc(counts_ready, 1)
                dve.engine_nop().then_inc(slots_ready, 1)
                dve.wait_ge(slots_done, 2 * layer + 2)
                link(dve.tensor_scalar(slot_f[:, 1, :], ps[:, 5, NE:2 * NE], float(EMPTY), None, ALU.add))
                link(dve.tensor_tensor(slot_f[:, 0, :], slot_f[:, 1, :], ps[:, 5, 0:NE], ALU.add))
                dve.tensor_scalar(slot_half[:, layer, :], slot_f[:, 0, :], 2.0, half_of[:, 0:1], ALU.mult,
                                  ALU.add).then_inc(halves_ready, 1)
                dve.tensor_scalar(soft[:, 0, :], g8[:, :, 0], -1.0, None, ALU.mult)
                dve.tensor_tensor(soft[:, 2, :], e8[:, :, 1], e8[:, :, 0], ALU.subtract).then_inc(top_ready, 1)
                dve.wait_ge(soft_exp, layer + 1)
                link(dve.tensor_scalar(soft[:, 4, :], soft[:, 3, :], 1.0, None, ALU.add))
                link(dve.tensor_tensor(soft[:, 5, :], soft[:, 4, :], soft[:, 1, :], ALU.mult))
                link(dve.reciprocal(pair_w[:, layer, 0, :], soft[:, 5, :]))
                link(dve.tensor_tensor(pair_w[:, layer, 1, :], pair_w[:, layer, 0, :], soft[:, 3, :], ALU.mult))

            def slot_tokens(tmp, pairs, toks):
                link(dve.tensor_scalar(tmp, pairs, float(S), -float(S), ALU.is_ge, ALU.mult))
                link(dve.tensor_tensor(toks, tmp, pairs, ALU.add))

            def gathered_gain(layer, dst, out_sem):
                g = g_ffn[:, layer, :].unsqueeze(2).to_broadcast([P, KT, P])
                dve.tensor_tensor(dst, ps[:, 0:2, :].rearrange("p b (k s) -> p (b k) s", s=P), g,
                                  ALU.mult).then_inc(out_sem, 1)

            def hidden(bank, sil_v, hid_v, out_sem):
                dve.tensor_tensor(hid_v.rearrange("p (f c) -> p f c", f=FT), sil_v.rearrange("p (f c) -> p f c", f=FT),
                                  ps[:, bank, :].rearrange("p (f g c) -> p f g c", f=FT, g=2)[:, :, 1, :],
                                  ALU.mult).then_inc(out_sem, 1)

            def hidden_T(bank, ht_v, out_sem):
                dve.tensor_copy(ht_v, ps[:, bank, 0:2 * P]).then_inc(out_sem, 1)

            def experts(layer):
                base = NE * layer

                def gain_of(i, b, early):
                    g = base + i * RING + b
                    dve.wait_ge(gT_done, g + 1)
                    if not (early and layer == 0):
                        dve.wait_ge(gu_done, g - 1)
                    gathered_gain(layer, xgT[:, b % 2], xgT_ready)

                def hidden_of(i, b, first):
                    g = base + i * RING + b
                    dve.wait_ge(silu_done, g + 1)
                    if not (first and b < 2 and layer == 0):
                        dve.wait_ge(hidT_done, g - 1)
                    hidden(2 + b % 2, sil[:, b % 2, :], hid[:, b % 2, :], hid_ready)

                def hidden_T_of(i, b, first):
                    g = base + i * RING + b
                    dve.wait_ge(hidT_done, g + 1)
                    if not (first and b < 2 and layer == 0):
                        dve.wait_ge(down_done, g - 1)
                    hidden_T(2 + b % 2, hidT[:, b % 2, :], hidT_ready)

                gain_of(0, 0, True)

                def body(i, first, last):
                    for b in range(RING):
                        hidden_of(i, b, first)
                        if b < RING - 1:
                            gain_of(i, b + 1, first and b == 0)
                        elif not last:
                            gain_of(i + 1, 0, False)
                        hidden_T_of(i, b, first)
                expert_loop(dve, body)

            def overflow(layer):
                o = ov[layer]
                most = dve.value_load(cnt_max[0:1, layer:layer + 1], min_val=0, max_val=S)
                for r in range(OV_ROUNDS):
                    with dve.If(most > CAP * (r + 1)):
                        dve.wait_ge(o["list"], 16 * (r + 1))
                        dve.tensor_scalar(ov_f[:, :], ov_pair[:, :], float(S), -float(S), ALU.is_ge,
                                          ALU.mult).then_inc(o["idx"], 1)
                        dve.wait_ge(o["idx"], 2 * r + 1)
                        dve.tensor_tensor(ov_tok[:, :], ov_f[:, :], ov_pair[:, :], ALU.add).then_inc(o["idx"], 1)
                        with dve.Fori(0, NE) as e:
                            q = e + r * NE + 1
                            dve.wait_ge(o["T"], q)
                            gathered_gain(layer, xgT[:, 0], o["xT"])
                            dve.wait_ge(o["silu"], q)
                            hidden(2, sil[:, 0, :], hid[:, 0, :], o["hid"])
                            dve.wait_ge(o["hT"], q)
                            hidden_T(2, hidT[:, 0, :], o["hTc"])

            def combine(layer, t):
                dve.wait_ge(yp_loaded[t], 16 * (layer + 1))
                for k in range(2):
                    ins = dve.scalar_tensor_tensor(out=x_sb[:, t, :], in0=yp[:, t, k, :],
                                                   scalar=pair_w[:, layer, k, t:t + 1], in1=x_sb[:, t, :],
                                                   op0=ALU.mult, op1=ALU.add)
                    if k == 0:
                        link(ins)
                ins.then_inc(x_ready, 1)

            dve.memset(neg_half[:, :], -0.5)
            dve.memset(zeros4[:, :], 0.0)
            dve.memset(gate_w[:, :, H:GF], 0.0)
            dve.memset(half_of[0:SMALL, :], 0.0)
            dve.memset(half_of[SMALL:P, :], 1.0)
            dve.memset(lg[:, :, 4:8], NEG)
            dve.memset(m_state[:, 0:1], 0.0)
            dve.memset(mv[:, :, :, HD:HD + 1], 1.0)
            dve.wait_ge(masks_ready, 3)
            dve.tensor_copy(iota_slot[:, :], iota_tmp[:, 0, :])
            dve.tensor_copy(iota_half[:, :], iota_tmp[:, 1, :])
            dve.tensor_copy(tok_f[:, :], pair_id[:, 0, 0:1])
            link(dve.tensor_copy(iota32[:, :], iota32_i[:, :]))
            link(dve.tensor_copy(ident_bf[:, :], ident[:, :]))
            dve.engine_nop().then_inc(consts_ready, 1)

            def before_tile(t):
                if t == 1:
                    dve.wait_ge(gate_high, 1)
                    dve.tensor_tensor(gate_l, gate_w[:, :, :], gate_h, ALU.subtract).then_inc(gate_split, 1)

            norm_split(0, before_tile)
            for u in range(2):
                rest_weights(0, u)
            dve.wait_ge(consts_loaded, 16 * N_CONST)

            link(dve.tensor_tensor(lam_t[:, :, :], lam_sb[:, 0::2, :], lam_sb[:, 1::2, :], ALU.mult))
            dve.tensor_reduce(lam_c[:, 0:2], lam_t[:, :, :], AX_X, ALU.add).then_inc(lam_sum, 1)
            dve.tensor_scalar(g_diff_s[:, :], g_diff[:, :], 1.0 - LAM_INIT, None, ALU.mult)

            link(dve.tensor_copy(pos_f[:, :], pos_i[:, :]))
            for t in range(TT):
                ins = dve.tensor_scalar(ang[:, 0, t, :], invf[:, :], pos_f[:, t:t + 1], None, ALU.mult)
            link(ins)
            link(dve.tensor_scalar(ang[:, 1], ang[:, 0], 0.15915494309189535, MAGIC, ALU.mult, ALU.add))
            link(dve.tensor_scalar(ang[:, 1], ang[:, 1], MAGIC, None, ALU.subtract))
            for c in TWO_PI:
                link(dve.scalar_tensor_tensor(out=ang[:, 0], in0=ang[:, 1], scalar=-c, in1=ang[:, 0],
                                              op0=ALU.mult, op1=ALU.add))
            link(dve.tensor_scalar(ang[:, 2], ang[:, 0], PI_IN, -PI_IN, ALU.min, ALU.max))
            link(dve.tensor_scalar(ang[:, 0], ang[:, 0], 1.5707963267948966, None, ALU.add))
            link(dve.tensor_scalar(ang[:, 1], ang[:, 0], PI_IN, -6.283185307179586, ALU.is_gt, ALU.mult))
            link(dve.tensor_tensor(ang[:, 3], ang[:, 0], ang[:, 1], ALU.add))
            dve.tensor_scalar(ang[:, 3], ang[:, 3], PI_IN, -PI_IN, ALU.min, ALU.max).then_inc(angles_ready, 1)
            dve.wait_ge(lam_exp, 1)
            link(dve.scalar_tensor_tensor(out=lam_c[:, 4:5], in0=lam_c[:, 3:4], scalar=-LAM_INIT, in1=lam_c[:, 2:3],
                                          op0=ALU.add, op1=ALU.subtract))

            def gates_a():
                dve.wait_ge(proj_done, 1)
                link(dve.tensor_copy(row_f[:, :], ps[GF:GC, 0, :]))
                dve.tensor_scalar(row_i[:, :], ps[0:H, 0, :], gate_b[:, 0:1], None, ALU.add)
                link(dve.tensor_scalar(row_f[:, :], row_f[:, :], gate_b[:, 1:2], None, ALU.add))
                link(dve.tensor_scalar(row_m[:, :], row_f[:, :], -1.0, None, ALU.mult))
                dve.tensor_tensor(row_c[:, :], row_f[:, :], row_m[:, :], ALU.max).then_inc(gates_abs, 1)

            def gates_b():
                dve.wait_ge(gates_ln, 1)
                link(dve.scalar_tensor_tensor(out=row_f[:, :], in0=row_f[:, :], scalar=0.0, in1=row_c[:, :],
                                              op0=ALU.min, op1=ALU.subtract))

            def gate_rows():
                for i in range(TT):
                    q = slice(i * P, (i + 1) * P)
                    ins = dve.tensor_tensor_scan(row_b[:, q], row_f[:, q], zeros4[:, :], 0.0, ALU.add, ALU.add)
                link(ins)
                link(dve.tensor_tensor(row_u[:, :], row_i[:, :], row_b[:, :], ALU.subtract))
                for i in range(TT):
                    q = slice(i * P, (i + 1) * P)
                    end = (i + 1) * P - 1
                    link(dve.tensor_tensor_scan(row_c[:, q], row_u[:, q], row_u[:, q], m_state[:, i:i + 1],
                                                ALU.max, ALU.max))
                    link(dve.tensor_tensor(m_state[:, i + 1:i + 2], row_c[:, end:end + 1], row_b[:, end:end + 1],
                                           ALU.add))
                dve.tensor_scalar(negc[:, :], row_c[:, :], -1.0, None, ALU.mult)
                link(dve.scalar_tensor_tensor(out=row_m[:, :], in0=row_b[:, :], scalar=-1.0, in1=row_c[:, :],
                                              op0=ALU.mult, op1=ALU.subtract))
                for (j, i), n in OFF.items():
                    prev = row_u[:, j * P:(j + 1) * P] if i == j + 1 else row_off[:, OFF[(j, i - 1)], :]
                    link(dve.tensor_scalar(row_off[:, n, :], prev, row_b[:, i * P - 1:i * P], None, ALU.add))
                dve.engine_nop().then_inc(rows_ready, 1)

            def rope(r):
                j = r + 1
                t = r % 4
                if r == 0:
                    dve.wait_ge(rope_table, 1)
                dve.wait_ge(proj_done, j + 1)
                if r >= 2:
                    dve.wait_ge(roped_ready, r - 1)
                src = ps[:, j % 2, :].rearrange("p (g e) -> p g e", e=HALF)
                for tab, dst in ((cos_t, rope_a), (sin_t, rope_b)):
                    ins = dve.tensor_tensor(dst[:, r % 2, :].rearrange("p (g e) -> p g e", e=HALF), src,
                                            tab[:, t, :].unsqueeze(1).to_broadcast([P, 2 * 2 * H, HALF]), ALU.mult)
                ins.then_inc(rope_parts, 1)

            def conv(j):
                ch = j - 17
                dve.wait_ge(proj_done, j + 1)
                if ch >= 2:
                    dve.wait_ge(qk_ready, ch - 1)
                acc = conv_acc[:, j % 2, :]
                src = ps[:, j % 2, :]
                link(dve.tensor_scalar(acc, src, conv0_w[:, ch, 3:4], None, ALU.mult))
                for s in range(1, 4):
                    ins = dve.scalar_tensor_tensor(out=acc[:, s:S], in0=src[:, 0:S - s],
                                                   scalar=conv0_w[:, ch, 3 - s:4 - s], in1=acc[:, s:S],
                                                   op0=ALU.mult, op1=ALU.add)
                    if s < 3:
                        link(ins)
                ins.then_inc(conv_ready, 1)

            def att_maxima(a):
                n = (a % TT + 1) * P
                dve.wait_ge(att_scores, a + 1)
                link(dve.tensor_reduce(att_s[:, 0:2], ps[:, 4:6, 0:n], AX_X, ALU.max))
                dve.tensor_scalar(att_s[:, 2:4], att_s[:, 0:2], -(DD ** -0.5), None, ALU.mult).then_inc(att_max, 1)

            def att_combine(a):
                n = (a % TT + 1) * P
                dve.wait_ge(att_exp, a + 1)
                if a >= 1:
                    dve.wait_ge(att_T, a)
                link(dve.reciprocal(att_s[:, 6:8], att_s[:, 4:6]))
                link(dve.tensor_tensor(att_s[:, 8:9], att_s[:, 7:8], lam_c[:, 4:5], ALU.mult))
                link(dve.tensor_scalar(att_e[:, 1, 0:n], att_e[:, 1, 0:n], att_s[:, 8:9], None, ALU.mult))
                dve.scalar_tensor_tensor(out=att_a[:, 0:n], in0=att_e[:, 0, 0:n], scalar=att_s[:, 6:7],
                                         in1=att_e[:, 1, 0:n], op0=ALU.mult, op1=ALU.add).then_inc(att_probs, 1)

            def att_norm(h):
                dve.wait_ge(att_o_copied, h + 1)
                link(dve.tensor_tensor(att_q[:, :], att_o[:, :], att_o[:, :], ALU.mult))
                dve.tensor_reduce(hn[:, h, :], att_q[:, :].rearrange("p (i e) -> p i e", e=HD), AX_X,
                                  ALU.add).then_inc(head_ss, 1)
                dve.wait_ge(head_rstd, h + 1)
                v = att_o[:, :].rearrange("p (i e) -> p i e", e=HD)
                dve.tensor_tensor(v, v, hn_r[:, h, :].unsqueeze(2).to_broadcast([P, TT, HD]),
                                  ALU.mult).then_inc(att_normed, 1)

            for j in range(ATT0 + 19):
                for u in split_at(j) if j < ATT0 else ():
                    rest_weights(0, u)
                if j == 0:
                    gates_a()
                elif j < 9:
                    rope(j - 1)
                elif 17 <= j < 25:
                    conv(j)
                if j == 1:
                    gates_b()
                if j == 2:
                    gate_rows()
                if j == 7:
                    dve.wait_ge(rowsT_done, 1)
                    dve.tensor_copy(ucol[:, :, :], ps[:, 5, 0:(len(PAIRS) + TT) * H].rearrange(
                        "p (n h) -> p n h", h=H)).then_inc(ucol_ready, 1)
                a = j - ATT0
                if 0 <= a < 16:
                    att_maxima(a)
                    att_combine(a)
                if a >= 5 and (a - 5) % 4 == 0 and (a - 5) // 4 < H:
                    att_norm((a - 5) // 4)

            def ml_weighted(h):
                dve.wait_ge(ml_masked, 4 * h + 4)
                dve.wait_ge(ml_scores, h + 1)
                if h == 0:
                    dve.wait_ge(att_pv, 16)
                if h >= 2:
                    dve.wait_ge(ml_num, h - 1)
                for j in range(TT):
                    bank, c0 = ML_BANK[j]
                    w = S - j * P
                    ins = dve.scalar_tensor_tensor(out=ml_s[:, h % 2, ML_COL[j]:ML_COL[j] + w],
                                                   in0=ps[:, bank, c0:c0 + w], scalar=HD ** -0.5,
                                                   in1=ml_w[:, h % 2, ML_COL[j]:ML_COL[j] + w],
                                                   op0=ALU.mult, op1=ALU.mult)
                ins.then_inc(ml_sT, 1)

            def ml_normalise(h):
                dve.wait_ge(ml_num, h + 1)
                if h == 0:
                    dve.wait_ge(em_ready, 1)
                if h >= 2:
                    dve.wait_ge(ml_fT, h - 1)
                nd = ps[:, 5:7, 0:2 * (HD + 1)].rearrange("p b (i e) -> p b i e", e=HD + 1)
                two = "p (b i) -> p b i"
                link(dve.tensor_copy(den_t[:, 0, :].rearrange(two, b=2), nd[:, :, :, HD]))
                link(dve.tensor_scalar(den_t[:, 1, :], den_t[:, 0, :], -1.0, None, ALU.mult))
                link(dve.tensor_tensor(den_t[:, 2, :], den_t[:, 0, :], den_t[:, 1, :], ALU.max))
                link(dve.tensor_tensor(den_t[:, 1, :], den_t[:, 2, :], em[:, :, h], ALU.max))
                link(dve.reciprocal(den_t[:, 3, :], den_t[:, 1, :]))
                hm = ml_h[:, h % 2, :]
                for b in range(2):
                    ins = dve.tensor_tensor(hm[:, b * 256:(b + 1) * 256].rearrange("p (i e) -> p i e", e=HD),
                                            nd[:, b, :, 0:HD],
                                            den_t[:, 3, 2 * b:2 * b + 2].unsqueeze(2).to_broadcast([P, 2, HD]),
                                            ALU.mult)
                link(ins)
                link(dve.tensor_tensor(ml_q[:, :], hm, hm, ALU.mult))
                dve.tensor_reduce(hn[:, H + h, :], ml_q[:, :].rearrange("p (i e) -> p i e", e=HD), AX_X,
                                  ALU.add).then_inc(head_ss, 1)
                dve.wait_ge(head_rstd, H + h + 1)
                for i in range(TT):
                    q = slice(i * P, (i + 1) * P)
                    ins = dve.scalar_tensor_tensor(out=hm[:, q], in0=hm[:, q], scalar=hn_r[:, H + h, i:i + 1],
                                                   in1=o_gate[:, i, h * HD:(h + 1) * HD],
                                                   op0=ALU.mult, op1=ALU.mult)
                ins.then_inc(ml_normed, 1)

            ml_weighted(0)
            for h in range(H):
                if h + 1 < H:
                    ml_weighted(h + 1)
                if h == 0:
                    dve.wait_ge(ogate_ready, TT)
                ml_normalise(h)

            w_out_norm_route(0)
            experts(0)
            overflow(0)

            for u in range(2):
                rest_weights(1, u)
            norm_split(2, lambda t: combine(0, t))
            for ct in range(KT):
                b = 2 + 3 * (ct % 2)
                dve.wait_ge(c_copied, ct + 1)
                dve.wait_ge(c_done, 3 * ct + 2)
                v, acc = cx[:, ct % 2, :], c_acc[:, ct % 2, :]
                link(dve.tensor_tensor(v, c_sb[:, ct % 2, :], ps[:, b + 1, :], ALU.mult))
                link(dve.tensor_scalar(acc, v, conv1_w[:, ct, 2:3], None, ALU.mult))
                for s in range(1, 3):
                    link(dve.scalar_tensor_tensor(out=acc[:, s:S], in0=v[:, 0:S - s],
                                                  scalar=conv1_w[:, ct, 2 - s:3 - s], in1=acc[:, s:S],
                                                  op0=ALU.mult, op1=ALU.add))
                dve.wait_ge(c_done, 3 * ct + 3)
                dve.tensor_tensor(yT[:, ct, :], acc, ps[:, b + 2, :], ALU.mult).then_inc(c_evac, 1)
                if ct + 2 < KT:
                    rest_weights(1, ct + 2)
            w_out_norm_route(1)
            experts(1)
            overflow(1)

            dve.wait_ge(g_final_loaded, 16)
            combine(1, 0)
            for t in range(TT):
                if t + 1 < TT:
                    combine(1, t + 1)
                dve.wait_ge(rstd_ready, 16 + t + 1)
                dve.scalar_tensor_tensor(out=fin[:, t, :], in0=x_sb[:, t, :], scalar=rstd[:, 4, t:t + 1],
                                         in1=g_final, op0=ALU.mult, op1=ALU.mult).then_inc(out_ready, 1)

        @block.gpsimd
        def _(pool):
            n_chain = [0]

            def link(ins):
                n_chain[0] += 1
                ins.then_inc(pool_chain, 1)
                pool.wait_ge(pool_chain, n_chain[0])

            def root(n, t):
                pool.wait_ge(sumsq, 4 * n + t + 1)
                link(pool.tensor_scalar(ms[:, n, t:t + 1], ss[:, n, t:t + 1], 1.0 / D, EPS, ALU.mult, ALU.add))
                pool.tensor_tensor(rstd[:, n, t:t + 1], ms[:, n, t:t + 1], neg_half[:, 0:1],
                                   ALU.pow).then_inc(rstd_ready, 1)

            def head_root(m):
                pool.wait_ge(head_ss, m + 1)
                link(pool.tensor_scalar(hn_ms[:, m, :], hn[:, m, :], 1.0 / HD, EPS, ALU.mult, ALU.add))
                pool.tensor_tensor(hn_r[:, m, :], hn_ms[:, m, :], neg_half[:, :], ALU.pow).then_inc(head_rstd, 1)

            pool.memset(ident[:, :], 0.0)
            pool.memset(causal_bf[:, :], 0.0)
            pool.memset(before_bf[:, :], 0.0)
            pool.memset(ones_bf[:, :], 1.0)
            pool.memset(empty_i[:, :], EMPTY)
            pool_zero = pool.engine_nop()
            link(pool_zero)
            pool.affine_select(out=ident[:, :], in_=ident[:, :], compare_op=ALU.not_equal, fill=1.0, base=0,
                               pattern=[[-1, P]], channel_multiplier=1)
            pool.affine_select(out=causal_bf[:, :], in_=causal_bf[:, :], compare_op=ALU.is_ge, fill=MASK, base=0,
                               pattern=[[-1, P]], channel_multiplier=1)
            pool.affine_select(out=before_bf[:, :], in_=before_bf[:, :], compare_op=ALU.is_ge, fill=1.0, base=0,
                               pattern=[[-1, P]], channel_multiplier=1)
            pool.iota(iota32_i[:, :], [[1, NE]], base=0, channel_multiplier=0)
            pool.iota(iota_tmp[:, 0, :], [[1, P]], base=0, channel_multiplier=0)
            pool.iota(iota_tmp[:, 1, :], [[0, 2], [1, SMALL]], base=0, channel_multiplier=0)
            link(pool.iota(pair_id[:, :, :], [[P, TT], [S, 2]], base=0, channel_multiplier=1))
            pool.engine_nop().then_inc(masks_ready, 3)
            for n in range(2):
                pool.dma_start(list_dram[n].rearrange("(p c) o -> p (c o)", c=P), empty_i[:, :]).then_inc(
                    lists_empty, 16)

            pool.wait_ge(consts_ready, 1)
            for t in range(TT):
                root(0, t)

            def rope_sum(r):
                pool.wait_ge(rope_parts, r + 1)
                if r >= 2:
                    pool.wait_ge(ropeT_done, r - 1)
                a, b, o = (v[:, r % 2, :].rearrange("p (g x e) -> p g x e", x=2, e=HALF)
                           for v in (rope_a, rope_b, roped))
                pool.tensor_tensor(o[:, :, 0, :], a[:, :, 0, :], b[:, :, 1, :], ALU.subtract)
                pool.tensor_tensor(o[:, :, 1, :], a[:, :, 1, :], b[:, :, 0, :], ALU.add).then_inc(roped_ready, 1)

            for j in range(1, 27):
                for u in split_at(j) if j >= ATT0 else ():
                    pool.wait_ge(w_high, u + 1)
                    w, low, high = weights_of(0, u)
                    pool.tensor_tensor(low, w, high, ALU.subtract).then_inc(w_split, 1)
                if j < 9:
                    rope_sum(j - 1)
                if j >= 18 and (j - 18) % 4 == 0:
                    head_root((j - 18) // 4)

            def ml_mask(h):
                pool.wait_ge(ml_exp, h + 1)
                for j in range(TT):
                    v = ml_w[:, h % 2, ML_COL[j]:ML_COL[j] + P]
                    pool.affine_select(out=v, in_=v, compare_op=ALU.is_ge, fill=0.0, base=0, pattern=[[1, P]],
                                       channel_multiplier=-1).then_inc(ml_masked, 1)

            ml_mask(0)
            head_root(H - 1)
            for h in range(H):
                if h + 1 < H:
                    ml_mask(h + 1)
                head_root(H + h)

            def roots(n):
                for t in range(TT):
                    root(n, t)

            def scatter_ids(layer):
                for t in range(TT):
                    for k in range(2):
                        pool.indirect_dma_start(
                            out=list_dram[layer][:, :],
                            out_offset=bass.IndirectOffsetOnAxis(ap=dest[:, t, k:k + 1], axis=0),
                            in_=pair_id[:, t, k:k + 1], in_offset=None, bounds_check=S * NE - 1,
                            oob_is_err=False).then_inc(ov[layer]["listed"], 16)
                pool.wait_ge(ov[layer]["listed"], 16 * 2 * TT)

            def gather(layer, tokens, dst, out_sem):
                pool.indirect_dma_start(
                    out=dst, out_offset=None, in_=xn_dram[layer][:, :],
                    in_offset=bass.IndirectOffsetOnAxis(ap=tokens, axis=0),
                    bounds_check=last_token, oob_is_err=False).then_inc(out_sem, 16)

            def scatter(layer, pairs, src, out_sem):
                pool.indirect_dma_start(
                    out=pair_dram[layer][:, :], out_offset=bass.IndirectOffsetOnAxis(ap=pairs, axis=0),
                    in_=src, in_offset=None, bounds_check=last_pair, oob_is_err=False).then_inc(out_sem, 16)

            def scatter_halves(layer, halves, src, out_sem):
                pool.indirect_dma_start(
                    out=pair_dram[layer].rearrange("r (n c) -> (r n) c", n=2),
                    out_offset=bass.IndirectOffsetOnAxis(ap=halves, axis=0),
                    in_=src, in_offset=None, bounds_check=last_half, oob_is_err=False).then_inc(out_sem, 16)

            def tokens_of(layer, e):
                return pool.value_load(cnt_i[0:1, layer, bass.ds(e, 1)], min_val=0, max_val=S)

            def experts(layer):
                base = NE * layer
                pool.wait_ge(x_ready, 8 * layer + TT)
                pool.wait_ge(slots_ready, layer + 1)
                for b in range(2):
                    pool.wait_ge(xn_stored[b], 32 * (layer + 1))

                def gather_step(e, b):
                    pool.tensor_copy(tok_now[:, b:b + 1], slot_tok[:, layer, bass.ds(e, 1)]).then_inc(tok_copied, 1)
                    pool.wait_ge(tok_copied, base + e + 1)
                    pool.sem_inc(indirect_turn, 1)
                    count = tokens_of(layer, e)
                    with pool.If(count > SMALL):
                        gather(layer, tok_now[:, b:b + 1], xg[:, b, :], xg_loaded[b])
                    with pool.Else():
                        with pool.If(count > TINY):
                            gather(layer, tok_now[0:SMALL, b:b + 1], xg[0:SMALL, b, :], xg_loaded[b])
                        with pool.Else():
                            gather(layer, tok_now[0:TINY, b:b + 1], xg[0:TINY, b, :], xg_loaded[b])

                for b in range(XB):
                    gather_step(b, b)
                pool.wait_ge(halves_ready, layer + 1)

                def body(i, first, last):
                    for b in range(RING):
                        e = i * RING + b
                        pool.tensor_copy(half_now[:, b:b + 1], slot_half[:, layer, bass.ds(e, 1)])
                        pool.tensor_copy(pair_now[:, b:b + 1], slot_pair[:, layer, bass.ds(e, 1)]).then_inc(
                            pair_copied, 1)
                        pool.wait_ge(y_ready, base + e + 1)
                        pool.wait_ge(pair_copied, base + e + 1)
                        pool.sem_inc(indirect_turn, 1)
                        with pool.If(tokens_of(layer, e) > SMALL):
                            scatter(layer, pair_now[:, b:b + 1], y_sb[:, b % 2, :], y_stored[b % 2])
                        with pool.Else():
                            scatter_halves(layer, half_now[:, b:b + 1], y_sb[:, b % 2, 0:512], y_stored[b % 2])
                        if not last:
                            pool.wait_ge(gT_done, base + e + 1)
                            gather_step(e + XB, b)
                expert_loop(pool, body)
                for b in range(2):
                    pool.wait_ge(y_stored[b], 16 * (NE // 2) * (layer + 1))

            def overflow(layer):
                o = ov[layer]
                pool.wait_ge(counts_ready, layer + 1)
                most = pool.value_load(cnt_max[0:1, layer:layer + 1], min_val=0, max_val=S)
                for r in range(OV_ROUNDS):
                    with pool.If(most > CAP * (r + 1)):
                        if r == 0:
                            scatter_ids(layer)
                        s0 = CAP * (r + 1) * NE
                        pool.dma_start(ov_pair[:, :], list_dram[layer][s0:s0 + CAP * NE, :].rearrange(
                            "(s e) o -> s (e o)", e=NE)).then_inc(o["list"], 16)
                        pool.wait_ge(o["idx"], 2 * r + 2)
                        with pool.Fori(0, NE) as e:
                            q = e + r * NE + 1
                            pool.tensor_copy(tok_now[:, 0:1], ov_tok[:, bass.ds(e, 1)])
                            pool.tensor_copy(pair_now[:, 0:1], ov_pair[:, bass.ds(e, 1)]).then_inc(o["copied"], 1)
                            pool.wait_ge(o["copied"], q)
                            pool.sem_inc(indirect_turn, 1)
                            gather(layer, tok_now[:, 0:1], xg[:, 0, :], o["rows"])
                            pool.wait_ge(o["y"], q)
                            pool.sem_inc(indirect_turn, 1)
                            scatter(layer, pair_now[:, 0:1], y_sb[:, 0, :], o["stored"])
                            pool.wait_ge(o["stored"], 16 * q)
                pool.memset(fence[:, layer:layer + 1], 0.0).then_inc(pairs_stored, 1)

            last_token = pool.to_reg(S - 1)
            last_pair = pool.to_reg(2 * S - 1)
            last_half = pool.to_reg(4 * S - 1)
            pool.wait_ge(lists_empty, 32)
            roots(1)
            experts(0)
            overflow(0)
            for t in range(TT):
                root(2, t)
            roots(3)
            experts(1)
            overflow(1)
            for t in range(TT):
                root(4, t)


OFF = {p: n for n, p in enumerate([(j, i) for j in range(TT) for i in range(j + 1, TT)])}
WO_BANK = [3, 6, 4, 6]
FT_BANK = [2, 2, 2, 5]
LOGIT_BANK = [2, 2, 2, 5]
ML_BANK = [(2, 0), (3, 0), (4, 0), (3, 384)]
ML_COL = [0, 512, 896, 1152]


_INS = ['x', 'positions', 'norm_mix', 'norm_ffn', 'ab_w_in', 'ab_gate_bias', 'ab_conv_w', 'ab_mlstm_norm',
        'ab_lambda', 'ab_diff_norm', 'ab_w_out', 'c_w_in', 'c_conv_w', 'c_w_out', 'moe_w_rg', 'moe_b_rg',
        'moe_w_re', 'moe_b_re', 'moe_w_gate', 'moe_w_up', 'moe_w_down', 'final_norm']


def kernel(**inputs):
    import numpy as _np
    import concourse.bacc as _bacc
    from concourse.bass_utils import run_bass_kernel_spmd as _run

    nc = _bacc.Bacc("TRN2", target_bir_lowering=False, num_devices=1)
    arrays, aps = {}, {}

    def give(name, a):
        a = _np.ascontiguousarray(a)
        arrays[f"in_{name}"] = a
        aps[name] = nc.dram_tensor(f"in_{name}", a.shape, mybir.dt.from_np(a.dtype), kind="ExternalInput").ap()

    for name in _INS:
        a = _np.asarray(inputs[name])
        if name in ('x', 'positions') or name.startswith('ab_') or name.startswith('c_'):
            a = a[0]
        if name in ('ab_conv_w', 'c_conv_w'):
            a = a.reshape(a.shape[0], -1, P).transpose(2, 1, 0)
        if name.startswith('moe_w_') and a.ndim == 5:
            a = a.reshape(a.shape[0], NE, *a.shape[3:])
        give(name, a)
    half = _np.arange(HALF, dtype=_np.float32) / _np.float32(HALF)
    give('inv_freq', (_np.float32(1.0) / _np.power(_np.float32(10000.0), half)).astype(_np.float32))
    out = nc.dram_tensor("out_dram", (S, D), F32, kind="ExternalOutput").ap()
    build(nc, *[aps[n] for n in _INS], aps['inv_freq'], out)
    r = _run(nc, [arrays], core_ids=[0])
    return r.results[0]["out_dram"].reshape(1, S, D)
```
